# Optimizing a Trainium2 kernel written in Bass

```python
import math
import jax, jax.numpy as jnp
from jax import lax
import numpy as np

D_MODEL = 1024
BATCH = 1
SEQ = 512
DEPTH = 2
DEC_BATCH = 8
DEC_SEQ = 8
PAST_LEN = 256
PAGE_SIZE = 128

H_A = 4
DK_A = 64
DV_A = 2 * DK_A
H_B = 4
G_B = 2
R_B = H_B // G_B
DH_B = 128
CMP_LEN = 32
CMP_STRIDE = 16
SEL_BLOCK = 64
TOP_N = 16
WINDOW = 512
H_C = 4
DK_C = D_MODEL // 2 // H_C
DV_C = D_MODEL // H_C
GATE_RANK = 16
GATE_TAU = 16.0
GLA_CHUNK = 64
D_FF = 4 * D_MODEL
ROPE_THETA = 10000.0
Q_BLOCK = 128
EPS = 1e-6
N_EVEN = (DEPTH + 1) // 2
N_ODD = DEPTH // 2
EVEN_SIZES = [H_A * 2 * DK_A, H_A * 2 * DK_A, H_A * DV_A, H_B * DH_B] + [G_B * DH_B] * 6 + [H_B * 3]
EVEN_IN = sum(EVEN_SIZES)
EVEN_MIX = H_A * DV_A + H_B * DH_B
ODD_SIZES = [H_C * DK_C, H_C * DK_C, H_C * DV_C, H_C * DV_C, GATE_RANK]
ODD_IN = sum(ODD_SIZES)

kernel_name = "hybrid_diffattn_nsa_gla_adaln_step"

def rms_norm(x, w):
    xf = x.astype(jnp.float32)
    y = xf * lax.rsqrt(jnp.mean(xf * xf, axis=-1, keepdims=True) + EPS)
    return (y * w.astype(jnp.float32)).astype(x.dtype)

def masked_softmax(s, mask):
    s = jnp.where(mask, s.astype(jnp.float32), -jnp.inf)
    m = jnp.max(s, axis=-1, keepdims=True)
    m = jnp.where(jnp.isfinite(m), m, 0.0)
    p = jnp.exp(s - m)
    return p / jnp.maximum(jnp.sum(p, axis=-1, keepdims=True), 1e-30)

def rope(x, pos):
    d = x.shape[-1]
    inv = ROPE_THETA ** (-jnp.arange(0, d, 2, dtype=jnp.float32) / d)
    ang = pos.astype(jnp.float32)[:, None] * inv[None, :]
    ang = ang.reshape(ang.shape[:1] + (1,) * (x.ndim - 3) + ang.shape[1:])
    cos, sin = jnp.cos(ang), jnp.sin(ang)
    xf = x.astype(jnp.float32)
    x1, x2 = xf[..., : d // 2], xf[..., d // 2:]
    return jnp.concatenate([x1 * cos - x2 * sin, x2 * cos + x1 * sin], axis=-1).astype(x.dtype)

def adaln(c, w, b):
    mod = (jax.nn.silu(c) @ w + b).reshape(c.shape[0], 6, D_MODEL)
    return [mod[:, i, None, :] for i in range(6)]

def modulate(h, shift, scale):
    return h * (1.0 + scale) + shift

def sqrelu_mlp(h, w1, w2):
    return jnp.square(jax.nn.relu(h @ w1)) @ w2

def residual_layer(y, mod, n1, n2, mixer, w1, w2):
    h = modulate(rms_norm(y, n1), mod[0], mod[1])
    out, state = mixer(h)
    y = y + (mod[2] * out).astype(y.dtype)
    h = modulate(rms_norm(y, n2), mod[3], mod[4])
    y = y + (mod[5] * sqrelu_mlp(h, w1, w2)).astype(y.dtype)
    return y, state

def diff_lambda(lw, lam_init):
    lw = lw.astype(jnp.float32)
    return jnp.exp(jnp.sum(lw[0] * lw[1])) - jnp.exp(jnp.sum(lw[2] * lw[3])) + lam_init

def diff_attention(q, q_pos, k, v, k_pos, lam):
    N, Q = q.shape[0], q.shape[1]
    qb = math.gcd(Q, Q_BLOCK)
    nb = Q // qb
    qs = q.reshape((N, nb, qb) + q.shape[2:]).swapaxes(0, 1)
    ps = q_pos.reshape(nb, qb)

    def block(args):
        qi, pi = args
        s = jnp.einsum('nqhmd,nkhmd->nhmqk', qi, k) * DK_A ** -0.5
        p = masked_softmax(s, k_pos[None, :] <= pi[:, None])
        a = p[:, :, 0] - lam * p[:, :, 1]
        return jnp.einsum('nhqk,nkhe->nqhe', a.astype(v.dtype), v)

    o = lax.map(block, (qs, ps))
    return o.swapaxes(0, 1).reshape(N, Q, H_A, DV_A)

def compress(x, pe, w1, w2):
    N, L = x.shape[0], x.shape[1]
    n_cmp = (L - CMP_LEN) // CMP_STRIDE + 1
    idx = CMP_STRIDE * jnp.arange(n_cmp)[:, None] + jnp.arange(CMP_LEN)[None, :]
    blk = x[:, idx] + pe[:, None, :]
    blk = blk.transpose(0, 1, 3, 2, 4).reshape(N, n_cmp, G_B, CMP_LEN * DH_B)
    return jax.nn.silu(blk @ w1) @ w2

def block_cover(n_cmp, n_sel):
    cs = CMP_STRIDE * jnp.arange(n_cmp)[:, None]
    ss = SEL_BLOCK * jnp.arange(n_sel)[None, :]
    return ((cs < ss + SEL_BLOCK) & (cs + CMP_LEN > ss)).astype(jnp.float32)

def sel_attend(q, q_pos, idx, kb, vb):
    N, Qc = q.shape[0], q.shape[1]
    K = idx.shape[-1]
    n_i = jnp.arange(N)[:, None, None, None]
    g_i = jnp.arange(G_B)[None, :, None, None]
    ksel = kb[n_i, g_i, idx].reshape(N, G_B, Qc, K * SEL_BLOCK, DH_B)
    vsel = vb[n_i, g_i, idx].reshape(N, G_B, Qc, K * SEL_BLOCK, DH_B)
    s = jnp.einsum('nqgrd,ngqmd->ngrqm', q, ksel) * DH_B ** -0.5
    tok = (idx[..., None] * SEL_BLOCK + jnp.arange(SEL_BLOCK)).reshape(N, G_B, Qc, K * SEL_BLOCK)
    mask = (tok <= q_pos[None, None, :, None])[:, :, None]
    p = masked_softmax(s, mask)
    return jnp.einsum('ngrqm,ngqmd->nqgrd', p.astype(vsel.dtype), vsel)

def nsa_cmp_sel(q, q_pos, kc, vc, ks, vs, pe, w1, w2, sel_chunk):
    N, L = kc.shape[0], kc.shape[1]
    Q = q.shape[1]
    kcc = compress(kc, pe[0], w1[0], w2[0])
    vcc = compress(vc, pe[1], w1[1], w2[1])
    n_cmp = kcc.shape[1]
    s = jnp.einsum('nqgrd,nkgd->ngrqk', q, kcc) * DH_B ** -0.5
    cmp_end = CMP_STRIDE * jnp.arange(n_cmp) + (CMP_LEN - 1)
    p_cmp = masked_softmax(s, cmp_end[None, :] <= q_pos[:, None])
    o_cmp = jnp.einsum('ngrqk,nkgd->nqgrd', p_cmp.astype(vcc.dtype), vcc)
    n_sel = -(-L // SEL_BLOCK)
    imp = jnp.einsum('ngrqk,ks->ngqs', p_cmp, block_cover(n_cmp, n_sel))
    blk = jnp.arange(n_sel)[None, :]
    valid = blk * SEL_BLOCK <= q_pos[:, None]
    forced = (blk == 0) | (blk == (q_pos // SEL_BLOCK)[:, None])
    imp = jnp.where(forced, jnp.inf, jnp.where(valid, imp, -jnp.inf))
    K = min(TOP_N, n_sel)
    _, idx = lax.top_k(imp, K)
    pad = n_sel * SEL_BLOCK - L

    def to_blocks(x):
        x = jnp.pad(x, ((0, 0), (0, pad), (0, 0), (0, 0)))
        return x.reshape(N, n_sel, SEL_BLOCK, G_B, DH_B).transpose(0, 3, 1, 2, 4)

    kb, vb = to_blocks(ks), to_blocks(vs)
    nc = Q // sel_chunk
    qs = q.reshape(N, nc, sel_chunk, G_B, R_B, DH_B).swapaxes(0, 1)
    ids = idx.reshape(N, G_B, nc, sel_chunk, K).transpose(2, 0, 1, 3, 4)
    ps = q_pos.reshape(nc, sel_chunk)
    o_sel = lax.map(lambda a: sel_attend(a[0], a[1], a[2], kb, vb), (qs, ps, ids))
    o_sel = o_sel.swapaxes(0, 1).reshape(N, Q, G_B, R_B, DH_B)
    return o_cmp, o_sel

def window_attend(q, q_pos, k, v, k_pos):
    s = jnp.einsum('nqgrd,nkgd->ngrqk', q, k) * DH_B ** -0.5
    kp, qp = k_pos[None, :], q_pos[:, None]
    mask = (kp >= 0) & (kp <= qp) & (kp > qp - WINDOW)
    p = masked_softmax(s, mask)
    return jnp.einsum('ngrqk,nkgd->nqgrd', p.astype(v.dtype), v)

def even_project(h, pos, w_in):
    N, T = h.shape[0], h.shape[1]
    parts = jnp.split(h @ w_in, np.cumsum(EVEN_SIZES)[:-1].tolist(), axis=-1)
    qa = rope(parts[0].reshape(N, T, H_A, 2, DK_A), pos)
    ka = rope(parts[1].reshape(N, T, H_A, 2, DK_A), pos)
    va = parts[2].reshape(N, T, H_A, DV_A)
    qb = rope(parts[3].reshape(N, T, G_B, R_B, DH_B), pos)
    kc, vc, ks, vs, kw, vw = [p.reshape(N, T, G_B, DH_B) for p in parts[4:10]]
    kc, ks, kw = rope(kc, pos), rope(ks, pos), rope(kw, pos)
    gates = jax.nn.sigmoid(parts[10].astype(jnp.float32)).reshape(N, T, G_B, R_B, 3)
    return qa, ka, va, qb, kc, vc, ks, vs, kw, vw, gates

def even_output(oa, o_cmp, o_sel, o_win, gates, lam_init, subln_w, w_out):
    N, T = oa.shape[0], oa.shape[1]
    oa = rms_norm(oa, subln_w) * (1.0 - lam_init)
    ob = gates[..., 0:1] * o_cmp + gates[..., 1:2] * o_sel + gates[..., 2:3] * o_win
    o = jnp.concatenate([oa.reshape(N, T, -1), ob.reshape(N, T, -1).astype(oa.dtype)], axis=-1)
    return o @ w_out

def even_mixer_prompt(h, w_in, w_out, lam_w, subln_w, pe, w1, w2, lam_init):
    N, T = h.shape[0], h.shape[1]
    pos = jnp.arange(T)
    qa, ka, va, qb, kc, vc, ks, vs, kw, vw, gates = even_project(h, pos, w_in)
    oa = diff_attention(qa, pos, ka, va, pos, diff_lambda(lam_w, lam_init))
    qblk = math.gcd(T, Q_BLOCK)
    o_cmp, o_sel = nsa_cmp_sel(qb, pos, kc, vc, ks, vs, pe, w1, w2, qblk)
    nb = T // qblk
    band = (jnp.arange(nb) * qblk)[:, None] + jnp.arange(WINDOW + qblk)[None, :]
    padw = ((0, 0), (WINDOW, 0), (0, 0), (0, 0))
    kband = jnp.pad(kw, padw)[:, band]
    vband = jnp.pad(vw, padw)[:, band]
    o_win = jax.vmap(window_attend, in_axes=(1, 0, 1, 1, 0), out_axes=1)(
        qb.reshape(N, nb, qblk, G_B, R_B, DH_B), pos.reshape(nb, qblk), kband, vband, band - WINDOW)
    o_win = o_win.reshape(N, T, G_B, R_B, DH_B)
    y = even_output(oa, o_cmp, o_sel, o_win, gates, lam_init, subln_w, w_out)
    wl = min(WINDOW, T)
    return y, (ka, va, jnp.stack([kc, vc], axis=2), jnp.stack([ks, vs], axis=2),
               jnp.stack([kw, vw], axis=2)[:, T - wl:])

def even_mixer_sample(h, c_dk, c_dv, c_cmp, c_sel, win_buf, page_table, w_in, w_out, lam_w, subln_w, pe, w1, w2, lam_init):
    N, S = h.shape[0], h.shape[1]
    P = page_table.shape[1] * c_dk.shape[1]
    pos = P + jnp.arange(S)
    qa, ka, va, qb, kc, vc, ks, vs, kw, vw, gates = even_project(h, pos, w_in)

    def past(pool):
        return pool[page_table].reshape((N, P) + pool.shape[2:])

    k_pos = jnp.arange(P + S)
    oa = diff_attention(qa, pos, jnp.concatenate([past(c_dk), ka], axis=1),
                        jnp.concatenate([past(c_dv), va], axis=1), k_pos, diff_lambda(lam_w, lam_init))
    cmp_new = jnp.stack([kc, vc], axis=2)
    sel_new = jnp.stack([ks, vs], axis=2)
    cmp_all = jnp.concatenate([past(c_cmp), cmp_new], axis=1)
    sel_all = jnp.concatenate([past(c_sel), sel_new], axis=1)
    o_cmp, o_sel = nsa_cmp_sel(qb, pos, cmp_all[:, :, 0], cmp_all[:, :, 1],
                               sel_all[:, :, 0], sel_all[:, :, 1], pe, w1, w2, 1)
    wb = win_buf.shape[1]
    win_all = jnp.concatenate([win_buf, jnp.stack([kw, vw], axis=2)], axis=1)
    o_win = window_attend(qb, pos, win_all[:, :, 0], win_all[:, :, 1], P - wb + jnp.arange(wb + S))
    y = even_output(oa, o_cmp, o_sel, o_win, gates, lam_init, subln_w, w_out)
    return y, (ka, va, cmp_new, sel_new, win_all[:, S:])

def gla_recurrence(q, k, v, log_a, s0):
    N, T = q.shape[0], q.shape[1]
    c = math.gcd(T, GLA_CHUNK)
    nc = T // c

    def chunks(x):
        return x.astype(jnp.float32).reshape(N, nc, c, H_C, x.shape[-1]).transpose(1, 0, 3, 2, 4)

    causal = jnp.tril(jnp.ones((c, c), dtype=bool))

    def step(S, inp):
        qc, kc, vc, gc = inp
        b = jnp.cumsum(gc, axis=2)
        o_inter = jnp.einsum('nhid,nhde->nhie', qc * jnp.exp(b), S)
        dec = jnp.exp(jnp.where(causal[:, :, None], b[:, :, :, None, :] - b[:, :, None, :, :], -jnp.inf))
        att = jnp.einsum('nhid,nhjd,nhijd->nhij', qc, kc, dec)
        o = o_inter + jnp.einsum('nhij,nhje->nhie', att, vc)
        b_last = b[:, :, -1:, :]
        S = jnp.exp(b_last[:, :, 0, :])[..., None] * S + jnp.einsum('nhjd,nhje->nhde', kc * jnp.exp(b_last - b), vc)
        return S, o

    s_fin, o = lax.scan(step, s0.astype(jnp.float32), (chunks(q), chunks(k), chunks(v), chunks(log_a)))
    return o.transpose(1, 0, 3, 2, 4).reshape(N, T, H_C, DV_C), s_fin

def gla_mixer(h, s0, w_in, w_gate, b_gate, norm_w, w_out):
    N, T = h.shape[0], h.shape[1]
    q, k, v, r, gl = jnp.split(h @ w_in, np.cumsum(ODD_SIZES)[:-1].tolist(), axis=-1)
    q = q.reshape(N, T, H_C, DK_C) * DK_C ** -0.5
    k = k.reshape(N, T, H_C, DK_C)
    v = v.reshape(N, T, H_C, DV_C)
    log_a = jax.nn.log_sigmoid((gl @ w_gate + b_gate).astype(jnp.float32)) / GATE_TAU
    o, s_new = gla_recurrence(q, k, v, log_a.reshape(N, T, H_C, DK_C), s0)
    o = rms_norm(o, norm_w) * jax.nn.silu(r.reshape(N, T, H_C, DV_C).astype(jnp.float32))
    return o.reshape(N, T, H_C * DV_C).astype(h.dtype) @ w_out, (s_new,)

def setup_inputs(seed: int = 0) -> dict:
    key = jax.random.key(seed)
    keys = iter(jax.random.split(key, 40))

    def nrm(shape, scale=1.0):
        return jax.random.normal(next(keys), shape, jnp.float32) * scale

    n_pages = PAST_LEN // PAGE_SIZE
    n_used = DEC_BATCH * n_pages
    n_phys = n_used + n_used // 4
    win_buf = min(WINDOW, PAST_LEN)
    return {
        "x_prompt": nrm((BATCH, SEQ, D_MODEL)),
        "x_sample": nrm((DEC_BATCH, DEC_SEQ, D_MODEL)),
        "c_prompt": nrm((BATCH, D_MODEL)),
        "c_sample": nrm((DEC_BATCH, D_MODEL)),
        "cache_diff_k": nrm((N_EVEN, n_phys, PAGE_SIZE, H_A, 2, DK_A)),
        "cache_diff_v": nrm((N_EVEN, n_phys, PAGE_SIZE, H_A, DV_A)),
        "cache_cmp_kv": nrm((N_EVEN, n_phys, PAGE_SIZE, 2, G_B, DH_B)),
        "cache_sel_kv": nrm((N_EVEN, n_phys, PAGE_SIZE, 2, G_B, DH_B)),
        "state_win_kv": nrm((N_EVEN, DEC_BATCH, win_buf, 2, G_B, DH_B)),
        "state_gla": nrm((N_ODD, DEC_BATCH, H_C, DK_C, DV_C)),
        "page_table": jax.random.permutation(next(keys), n_phys)[:n_used].reshape(DEC_BATCH, n_pages).astype(jnp.int32),
        "norm1_w": 1.0 + nrm((DEPTH, D_MODEL), 0.05),
        "norm2_w": 1.0 + nrm((DEPTH, D_MODEL), 0.05),
        "ada_w": nrm((DEPTH, D_MODEL, 6 * D_MODEL), D_MODEL ** -0.5),
        "ada_b": nrm((DEPTH, 6 * D_MODEL), 0.02),
        "even_w_in": nrm((N_EVEN, D_MODEL, EVEN_IN), D_MODEL ** -0.5),
        "even_w_out": nrm((N_EVEN, EVEN_MIX, D_MODEL), EVEN_MIX ** -0.5),
        "diff_lambda_w": nrm((N_EVEN, 4, DK_A), 0.1),
        "diff_subln_w": 1.0 + nrm((N_EVEN, DV_A), 0.05),
        "cmp_pe": nrm((N_EVEN, 2, CMP_LEN, DH_B), 0.2),
        "cmp_w1": nrm((N_EVEN, 2, CMP_LEN * DH_B, DH_B), (CMP_LEN * DH_B) ** -0.5),
        "cmp_w2": nrm((N_EVEN, 2, DH_B, DH_B), DH_B ** -0.5),
        "gla_w_in": nrm((N_ODD, D_MODEL, ODD_IN), D_MODEL ** -0.5),
        "gla_w_gate": nrm((N_ODD, GATE_RANK, H_C * DK_C), GATE_RANK ** -0.5),
        "gla_b_gate": nrm((N_ODD, H_C * DK_C), 0.1),
        "gla_norm_w": 1.0 + nrm((N_ODD, DV_C), 0.05),
        "gla_w_out": nrm((N_ODD, H_C * DV_C, D_MODEL), (H_C * DV_C) ** -0.5),
        "mlp_w1": nrm((DEPTH, D_MODEL, D_FF), D_MODEL ** -0.5),
        "mlp_w2": nrm((DEPTH, D_FF, D_MODEL), D_FF ** -0.5),
        "final_norm_w": 1.0 + nrm((D_MODEL,), 0.05),
    }

def reference(x_prompt, x_sample, c_prompt, c_sample, cache_diff_k, cache_diff_v, cache_cmp_kv, cache_sel_kv,
              state_win_kv, state_gla, page_table, norm1_w, norm2_w, ada_w, ada_b, even_w_in, even_w_out,
              diff_lambda_w, diff_subln_w, cmp_pe, cmp_w1, cmp_w2, gla_w_in, gla_w_gate, gla_b_gate, gla_norm_w,
              gla_w_out, mlp_w1, mlp_w2, final_norm_w):
    yp, ys = x_prompt, x_sample
    st_p = [[] for _ in range(6)]
    st_s = [[] for _ in range(6)]
    for l in range(DEPTH):
        mp = adaln(c_prompt, ada_w[l], ada_b[l])
        ms = adaln(c_sample, ada_w[l], ada_b[l])
        if l % 2 == 0:
            e = l // 2
            lam_init = 0.8 - 0.6 * math.exp(-0.3 * l)
            ew = (even_w_in[e], even_w_out[e], diff_lambda_w[e], diff_subln_w[e], cmp_pe[e], cmp_w1[e], cmp_w2[e], lam_init)
            mix_p = lambda h, ew=ew: even_mixer_prompt(h, *ew)
            mix_s = lambda h, ew=ew, e=e: even_mixer_sample(h, cache_diff_k[e], cache_diff_v[e], cache_cmp_kv[e],
                                                            cache_sel_kv[e], state_win_kv[e], page_table, *ew)
            slots = (0, 1, 2, 3, 4)
        else:
            o = l // 2
            gw = (gla_w_in[o], gla_w_gate[o], gla_b_gate[o], gla_norm_w[o], gla_w_out[o])
            mix_p = lambda h, gw=gw: gla_mixer(h, jnp.zeros((h.shape[0], H_C, DK_C, DV_C), jnp.float32), *gw)
            mix_s = lambda h, gw=gw, o=o: gla_mixer(h, state_gla[o], *gw)
            slots = (5,)
        yp, sp = residual_layer(yp, mp, norm1_w[l], norm2_w[l], mix_p, mlp_w1[l], mlp_w2[l])
        ys, ss = residual_layer(ys, ms, norm1_w[l], norm2_w[l], mix_s, mlp_w1[l], mlp_w2[l])
        for i, a, b in zip(slots, sp, ss):
            st_p[i].append(a)
            st_s[i].append(b)
    diff_k_p, diff_v_p, cmp_kv_p, sel_kv_p, win_kv_p, gla_p = [jnp.stack(s, axis=0) for s in st_p]
    diff_k_s, diff_v_s, cmp_kv_s, sel_kv_s, win_kv_s, gla_s = [jnp.stack(s, axis=0) for s in st_s]
    y_prompt = rms_norm(yp, final_norm_w)
    y_sample = rms_norm(ys, final_norm_w)
    return (y_prompt, y_sample, diff_k_p, diff_v_p, cmp_kv_p, sel_kv_p, win_kv_p, gla_p,
            diff_k_s, diff_v_s, cmp_kv_s, sel_kv_s, win_kv_s, gla_s)


_drawn_inputs = setup_inputs


def setup_inputs(seed=0):
    import zlib

    import numpy as np

    out = dict(_drawn_inputs(seed))
    spreads = {}
    factors = {'diff_lambda_w': 4.146, 'gla_norm_w': 4.371}
    for name, (base, spread) in spreads.items():
        noise = np.random.default_rng([zlib.crc32(name.encode()), seed]).standard_normal(out[name].shape)
        drawn = base * np.exp(spread * noise) if base else spread * noise
        out[name] = __import__('jax').numpy.asarray(drawn.astype(out[name].dtype))
    for name, factor in factors.items():
        out[name] = (out[name] * factor).astype(out[name].dtype)
    return out
```

```python
from contextlib import ExitStack
import math

import numpy as np
import concourse.bass as bass
from concourse import mybir

P = 128
D = 1024
KC = D // P
SEQ = 512
NS, DS = 8, 8
TS = NS * DS
T = SEQ + TS
NT = SEQ // P
PAST, PAGE = 256, 128
NPAGE = PAST // PAGE
HA, DKA = 4, 64
HB, GB, DHB = 4, 2, 128
CL, CS = 32, 16
SEL_BLOCK, TOP_N, WINDOW = 64, 16, 512
HC, DKC, DVC = 4, 128, 256
RANK, TAU, GCH = 16, 16.0, 64
SUB = 16
NCH = SEQ // GCH
DFF = 4096
EPS = 1e-6
LAM_INIT = 0.8 - 0.6 * math.exp(-0.3 * 0)
NB_P = (SEQ - CL) // CS + 1
NB_S = (PAST + DS - CL) // CS + 1
assert TOP_N * SEL_BLOCK >= SEQ and TOP_N * SEL_BLOCK >= PAST + DS
assert WINDOW >= SEQ and WINDOW >= PAST + DS and (NB_S - 1) * CS + CL <= PAST
C1 = D + D // 2
WSLOTS, SLOT = 4, 4096
NEG = -1e30

F32, BF16, I32 = mybir.dt.float32, mybir.dt.bfloat16, mybir.dt.int32
ALU, ACT, AX = mybir.AluOpType, mybir.ActivationFunctionType, mybir.AxisListType

V1_N1, V1_N2, V1_ADAB = 0, 16, 32
V2_FIN, V2_SUB, V2_GLAN, V2_BG, V2_C = 0, 8, 9, 11, 15
V2_ROWS = V2_C + 9 * KC


def shape_constants():
    cols, at = {}, 0
    parts = []

    def put(name, a):
        nonlocal at
        a = np.asarray(a, np.float32).reshape(P, -1)
        cols[name] = (at, a.shape[1])
        at += a.shape[1]
        parts.append(a)

    put("ident", np.eye(P))
    put("ones", np.ones((P, P)))
    put("eps", np.full((P, 1), EPS))
    pos = np.concatenate([np.arange(SEQ), np.tile(PAST + np.arange(DS), NS), np.zeros(P - TS)]).astype(np.float32)
    for name, d in (("a", DKA), ("b", DHB)):
        inv = (np.float32(10000.0) ** (-np.arange(0, d, 2, dtype=np.float32) / np.float32(d))).astype(np.float32)
        ang = (pos[:, None] * inv[None, :]).reshape(NT + 1, P, d // 2).transpose(1, 0, 2)
        put("cos" + name, np.cos(ang.astype(np.float64)))
        put("sin" + name, np.sin(ang.astype(np.float64)))
    t = np.arange(SEQ).reshape(NT, P).T
    end = CS * np.arange(NB_P) + CL - 1
    put("cmask", np.where(end[None, None, :] <= t[:, :, None], 0.0, NEG))
    put("cvalid", (t >= CL - 1).astype(np.float32))
    rows = np.arange(P) // (2 * DS)
    put("smask", np.where(np.arange(NS * NB_S)[None, :] // NB_S == rows[:, None], 0.0, NEG))
    j, i = np.arange(P)[:, None], np.arange(GCH)[None, :]
    put("tri", (j % GCH <= i).astype(np.float32))
    put("stri", ((j // DS == i // DS) & (j <= i) & (j < TS)).astype(np.float32))
    keep = np.ones(T)
    keep[0:SEQ:GCH] = 0
    keep[SEQ::DS] = 0
    put("keep", np.broadcast_to(keep, (P, T)))
    put("rowof", (np.arange(P)[:, None] // DS == np.arange(NS)[None, :]))
    f32 = np.concatenate(parts, 1)

    q, k = np.arange(P)[:, None], np.arange(P)[None, :]
    causal = np.where(k <= q, 0.0, NEG)
    c = np.arange(TS)[None, None, :]
    n = np.arange(NS)[None, :, None]
    new = np.where((c // DS == n) & (c % DS <= (np.arange(P) % DS)[:, None, None]), 0.0, NEG)
    bf = np.concatenate([np.eye(P), causal, new.reshape(P, NS * TS)], 1).astype(mybir.dt.np(BF16))
    return np.ascontiguousarray(f32), np.ascontiguousarray(bf), cols


def decoder_program(nc, a, out, const_cols):
    ctx = ExitStack()
    with ctx, nc.allow_non_contiguous_dma(reason="small vectors, gate columns"):
        def sb(name, shape, dt=F32):
            return ctx.enter_context(nc.sbuf_tensor(name, shape, dt))

        def sem(name):
            return ctx.enter_context(nc.semaphore(name))

        ps = ctx.enter_context(nc.psum_tensor("ps", [P, 8, 512], F32))
        wring = sb("wring", [P, WSLOTS, SLOT])
        xT = sb("xT", [P, KC, T])
        hT = sb("hT", [P, KC, T])
        cf = sb("cf", [P, a["const_f32"].shape[1]])
        cb = sb("cb", [P, a["const_bf16"].shape[1]], BF16)
        mod = sb("mod", [P, 48, 9])
        v1T = sb("v1T", [P, P])
        v2T = sb("v2T", [P, V2_ROWS])
        peT = sb("peT", [P, 2 * CL])
        scT = sb("scT", [P, KC, 9])
        modA = sb("modA", [P, KC, 9])
        rstd = sb("rstd", [P, T])
        gates = sb("gates", [P, NT + 1, 12])
        gcols = sb("gcols", [P, KC, 16])
        lam = sb("lam", [P, 8])
        r16 = sb("r16", [P, 2, 16])
        nm = sb("nm", [P, 4])
        sums = sb("sums", [P, 4])
        rsum = sb("rsum", [P, 4])
        xs_tmp = sb("xs_tmp", [P, TS])
        hidp = sb("hidp", [P, 2, 2 * NB_P + 1])
        hids = sb("hids", [P, 2, GB * NS * NB_S])
        kccs = sb("kccs", [P, GB, NS * NB_S])
        vccs = sb("vccs", [P, GB, P])
        kccp = sb("kccp", [P, GB, NB_P])
        vccp = sb("vccp", [P, GB, P])
        cw2 = sb("cw2", [P, 2, P])
        pagesb = sb("pagesb", [1, NS * NPAGE], I32)
        ARENA = 21560
        arena = sb("arena", [P, ARENA])

        class Carve:

            def __init__(self, at=0):
                self.at = at

            def __call__(self, *dims):
                n = int(np.prod(dims))
                v = arena[:, self.at:self.at + n]
                self.at += n
                assert self.at <= ARENA, self.at
                if len(dims) == 2:
                    v = v.rearrange("p (a b) -> p a b", a=dims[0])
                elif len(dims) == 3:
                    v = v.rearrange("p (a b c) -> p a b c", a=dims[0], b=dims[1])
                elif len(dims) == 4:
                    v = v.rearrange("p (a b c d) -> p a b c d", a=dims[0], b=dims[1], c=dims[2])
                return v

        def const(name, *dims):
            at, n = const_cols[name]
            v = cf[:, at:at + n]
            if len(dims) == 2:
                v = v.rearrange("p (a b) -> p a b", a=dims[0])
            return v

        ident, ones, eps = const("ident"), const("ones"), const("eps")
        rope_tab = {"a": (const("cosa", NT + 1, 32), const("sina", NT + 1, 32)),
                    "b": (const("cosb", NT + 1, 64), const("sinb", NT + 1, 64))}
        identb, causalb = cb[:, 0:P], cb[:, P:2 * P]
        newmask = cb[:, 2 * P:2 * P + NS * TS].rearrange("p (n c) -> p n c", n=NS)

        c0 = Carve()
        h_flat = hT[:, :, :].rearrange("p a b -> p (a b)")
        x_in = h_flat[:, 0:NT * D].rearrange("p (t d) -> p t d", t=NT)
        rows = h_flat[:, NT * D:NT * D + 3 * P].rearrange("p (a b) -> p a b", a=3)
        lprod = h_flat[:, NT * D + 3 * P:NT * D + 4 * P].rearrange("p (a b) -> p a b", a=2)
        lw = rstd[:, 0:4 * DKA].rearrange("p (a b) -> p a b", a=4)
        cexp = rstd[:, 4 * DKA:4 * DKA + 9 * KC]
        xs_in = c0(D)
        ctok = c0(NS * NPAGE, 512)
        cxs = c0(GB * NS, PAST)
        cw1 = c0(2, SLOT)
        c1 = Carve()
        qaT = c1(HA, SEQ)
        qbT = c1(HB, SEQ)
        kaT = c1(HA, T)
        skT = c1(GB, T)
        wkT = c1(GB, T)
        va = c1(NT + 1, 512)
        vs = c1(NT + 1, 256)
        vw = c1(NT + 1, 256)
        qAs = c1(NS, HA, 32)
        qBs = c1(GB, NS, 32)
        mixer_scratch = c1.at
        cxp = c1(2, 2 * SEQ + CL)
        tok = c1(3, 512)
        rt1 = c1(512)
        rt2 = c1(512)
        c2 = Carve(mixer_scratch)
        pbuf = c2(3, 512)
        diag = c2(3, P)
        ptb = Carve(mixer_scratch + 2 * (2 * SEQ + CL))(3, 512)
        c2 = Carve(mixer_scratch + 2 * (2 * SEQ + CL) + 3 * 512)
        gdiag = c2(12, TS)
        ptsc = c2(GB, P)
        gb = c2(12, TS)
        s1 = c2(16, NB_P)
        sc = c2(GB, NS * NB_S)
        c2 = Carve(0)
        kts = c2(2, 4, PAST)
        sq = Carve(0)(HA, T)
        c2 = Carve(HA * T)
        oc = c2(GB, P)
        osa = c2(NS, 4, 16)
        osb = c2(NS, 4, 16)
        qbc = c2(GB, P)
        wscr = wring[:, 0:2, :].rearrange("p a b -> p (a b)")
        ptc = wscr[:, 0:4 * 512].rearrange("p (h t) -> p h t", h=HB)
        kvb = [wscr[:, 2048 * i:2048 * (i + 1)].rearrange("p (b c) -> p b c", b=4) for i in (1, 2, 3, 0)]
        cg = Carve()
        gq, gk, gbt = cg(HC, T), cg(HC, T), cg(HC, T)
        gr = cg(KC, T)
        gv = cg(NT + 1, D)
        gla_scratch = cg.at
        gtmp = cg(HC, T)
        glT = cg(T)
        er = cg(2, T)
        wg = Carve(21040)(HC * P)
        cg = Carve(gla_scratch)
        geb = cg(T)
        gkd = cg(T)
        gqd = cg(NCH, 3 * SUB)
        gqe = cg(2, T)
        gatt = cg(2, 5, GCH)
        gkdm = cg(NS, P)
        gebl = cg(2, NCH + NS)
        s0 = wscr[:, 0:4096].rearrange("p (r n e) -> p r n e", r=2, n=NS)
        gsq = Carve(0)(KC, T)
        gstd = Carve(KC * T)(HC, T)
        fin = Carve(0)(2, D)
        sp_ = wscr[:, 4096:5120].rearrange("p (r e) -> p r e", r=4)
        gkdT = wscr[:, 5120:6400].rearrange("p (r t d) -> p r t d", r=2, t=NT + 1)
        kp_at = [6400 + NCH * SUB * i * (i + 1) // 2 for i in range(5)]
        gkp = [wscr[:, kp_at[i]:kp_at[i + 1]].rearrange("p (c j) -> p c j", c=NCH) for i in range(4)]
        gkp_s = wscr[:, kp_at[4]:kp_at[4] + TS]
        cm = Carve()
        hid = cm(DFF // P, T)
        relu = cm(2, T)

        const_loaded = sem("const_loaded")
        small_loaded = sem("small_loaded")
        x_loaded = sem("x_loaded")
        pages_loaded = sem("pages_loaded")
        cmpw_loaded = sem("cmpw_loaded")
        ctok_loaded = sem("ctok_loaded")
        gcols_loaded = sem("gcols_loaded")
        w_ready = [sem(f"w_ready{i}") for i in range(WSLOTS)]
        small_turned = sem("small_turned")
        small_kept = sem("small_kept")
        cexp_ready = sem("cexp_ready")
        silu_ready = sem("silu_ready")
        lam_sums = sem("lam_sums")
        lam_exp = sem("lam_exp")
        lam_ready = sem("lam_ready")
        x_turned = sem("x_turned")
        x_ready = sem("x_ready")
        x_evac = sem("x_evac")
        ctok_turned = sem("ctok_turned")
        cxs_ready = sem("cxs_ready")
        cmp_mm = sem("cmp_mm")
        cmp_exp = sem("cmp_exp")
        cmp_hid = sem("cmp_hid")
        cmp2_mm = sem("cmp2_mm")
        cmp2_kept = sem("cmp2_kept")
        ada_mm = sem("ada_mm")
        ada_kept = sem("ada_kept")
        norm_sq = sem("norm_sq")
        norm_sum = sem("norm_sum")
        norm_std = sem("norm_std")
        norm_x = sem("norm_x")
        h_prompt = sem("h_prompt")
        h_sample = sem("h_sample")
        pj_mm = sem("pj_mm")
        pj_dve = sem("pj_dve")
        pj_act = sem("pj_act")
        tok_ready = sem("tok_ready")
        tok_stored = [sem(f"tok_stored{i}") for i in range(3)]
        tok_turned = sem("tok_turned")
        turn_kept = sem("turn_kept")
        gate_mm = sem("gate_mm")
        gate_exp = sem("gate_exp")
        gates_ready = sem("gates_ready")
        scratch_zero = sem("scratch_zero")
        out_stored = sem("out_stored")
        pe_col = sem("pe_col")
        cmpp_mm = sem("cmpp_mm")
        cmpp_exp = sem("cmpp_exp")
        cmpp_hid = sem("cmpp_hid")
        cmpp2_mm = sem("cmpp2_mm")
        cmpp2_kept = sem("cmpp2_kept")
        gate_diag = sem("gate_diag")
        gb_mm = sem("gb_mm")
        gb_kept = sem("gb_kept")
        cs_mm = sem("cs_mm")
        cs_sub = sem("cs_sub")
        cs_exp = sem("cs_exp")
        cs_p = sem("cs_p")
        cs_turned = sem("cs_turned")
        ptc_kept = sem("ptc_kept")
        s_mm = sem("s_mm")
        nm_ready = sem("nm_ready")
        p_ready = sem("p_ready")
        diag_ready = sem("diag_ready")
        pt_mm = sem("pt_mm")
        pt_kept = sem("pt_kept")
        pv_mm = sem("pv_mm")
        o_kept = sem("o_kept")
        ss_mm = sem("ss_mm")
        qbc_ready = sem("qbc_ready")
        ss_sub = sem("ss_sub")
        ss_exp = sem("ss_exp")
        ss_p = sem("ss_p")
        ss_turned = sem("ss_turned")
        ss_kept = sem("ss_kept")
        ss_pv = sem("ss_pv")
        oc_kept = sem("oc_kept")
        kt_mm = sem("kt_mm")
        kt_kept = sem("kt_kept")
        ss2_mm = sem("ss2_mm")
        snm_ready = sem("snm_ready")
        sp_ready = sem("sp_ready")
        sdiag_ready = sem("sdiag_ready")
        spt_mm = sem("spt_mm")
        spt_kept = sem("spt_kept")
        spv_mm = sem("spv_mm")
        so_kept = sem("so_kept")
        comb_ready = sem("comb_ready")
        sub_sq = sem("sub_sq")
        sub_sum = sem("sub_sum")
        sub_std = sem("sub_std")
        mix_ready = sem("mix_ready")
        out_mm = sem("out_mm")
        resid_kept = sem("resid_kept")
        up_mm = sem("up_mm")
        up_free = sem("up_free")
        relu_free = sem("relu_free")
        down_mm = sem("down_mm")
        down_free = sem("down_free")
        v_stored = sem("v_stored")
        kv_loaded = [sem(f"kv_loaded{i}") for i in range(4)]
        gl_mm = sem("gl_mm")
        gl_kept = sem("gl_kept")
        gz_mm = sem("gz_mm")
        gz_abs = sem("gz_abs")
        gz_ln = sem("gz_ln")
        b_ready = sem("b_ready")
        gin_mm = sem("gin_mm")
        gin_kept = sem("gin_kept")
        r_exp = sem("r_exp")
        r_ready = sem("r_ready")
        eb_ready = sem("eb_ready")
        gsub_ready = sem("gsub_ready")
        ex_ready = sem("ex_ready")
        prep_ready = sem("prep_ready")
        kd_turned = sem("kd_turned")
        kd_kept = sem("kd_kept")
        att_mm = sem("att_mm")
        att_kept = sem("att_kept")
        st_mm = sem("st_mm")
        st_first = sem("st_first")
        st_kept = sem("st_kept")
        s_ready = sem("s_ready")
        go_mm = sem("go_mm")
        os_mm = sem("os_mm")
        go_kept = sem("go_kept")
        s0_new = sem("s0_new")
        gs_stored = sem("gs_stored")
        gn_sq = sem("gn_sq")
        gn_sum = sem("gn_sum")
        gn_std = sem("gn_std")
        gmix_ready = sem("gmix_ready")
        wg_loaded = sem("wg_loaded")
        fin_ready = sem("fin_ready")
        fin_mm = sem("fin_mm")
        fin_kept = sem("fin_kept")
        s0_loaded = [sem(f"s0_loaded{i}") for i in range(2)]
        s0_stored = [sem(f"s0_stored{i}") for i in range(2)]
        fin_stored = [sem(f"fin_stored{i}") for i in range(2)]
        dve_chain = sem("dve_chain")
        act_chain = sem("act_chain")

        W_ADA0, W_IN, W_CMP, W_OUT = 0, 12, 20, 22
        W_UP0 = 24
        W_DOWN0, W_ADA1, W_GIN, W_GOUT = W_UP0 + 8, W_UP0 + 16, W_UP0 + 28, W_UP0 + 34
        W_UP1 = W_GIN + 8
        W_DOWN1 = W_UP1 + 8

        def slot(n, k=KC):
            return wring[:, n % WSLOTS, :].rearrange("p (k c) -> p k c", k=k)

        QA, KA, VA, QB, CKV, SKV, WKV = range(7)
        pj_units = [(j, t) for j in range(7) for t in range(NT + 1)]

        def rows_of(t):
            return P if t < NT else TS

        has_dve = [j != VA for j, t in pj_units]
        has_act = [j in (VA, CKV, SKV, WKV) for j, t in pj_units]
        dve_upto = [sum(has_dve[:u + 1]) for u in range(len(pj_units))]
        act_upto = [sum(has_act[:u + 1]) for u in range(len(pj_units))]
        tok_use = [u for u in range(len(pj_units)) if has_dve[u]]
        use_of = {u: r for r, u in enumerate(tok_use)}
        stores_in_slot = [0, 0, 0]
        slot_stores = []
        for r, u in enumerate(tok_use):
            if pj_units[u][0] in (KA, CKV, SKV, WKV):
                stores_in_slot[r % 3] += (NS if pj_units[u] == (WKV, NT) else 1)
            slot_stores.append(16 * stores_in_slot[r % 3])
        turns = [r for r, u in enumerate(tok_use) if pj_units[u] != (CKV, NT)]
        turn_no = {r: i for i, r in enumerate(turns)}

        def tok_slot_free(eng, r):
            if r >= 3:
                if slot_stores[r - 3]:
                    eng.wait_ge(tok_stored[r % 3], slot_stores[r - 3])
                done = [i for i in turns if i <= r - 3]
                eng.wait_ge(tok_turned, len(done))


        gin = ([("q", c, 0) for c in range(4)] + [("k", c, 0) for c in range(4)]
               + [("v", g, t) for g in range(2) for t in range(NT + 1)] + [("r", c, 0) for c in range(8)])
        gin_upto = [4, 8, 8 + NT + 1, 8 + 2 * (NT + 1), 12 + 2 * (NT + 1), 16 + 2 * (NT + 1)]

        units = [(h, t, b) for h in range(HA + HB) for t in range(NT) for b in range(2)]
        group_ends = [h >= HA or b == 1 for h, t, b in units]
        group_of = [sum(group_ends[:v]) for v in range(len(units))]
        groups = [(h, t, b if h >= HA else 0) for (h, t, b), end in zip(units, group_ends) if end]
        last_unit = [max(v for v, x in enumerate(units) if x[0] == h) for h in range(HA + HB)]
        head_groups = [sum(1 for x in groups if x[0] <= h) for h in range(HA + HB)]
        kv_upto = [16 * sum(3 if x % 2 else 4 for x in range(v % 4, v + 1, 4)) for v in range(2 * NS)]

        def cached_keys(v, s, pg):
            return kvb[v % 4][:, 2 * (s // 2) + pg, s % 2 * P:(s % 2 + 1) * P] if v % 2 else kvb[v % 4][:, pg, s * P:(s + 1) * P]

        def cached_values(v, s, pg):
            if v % 2:
                return kvb[v % 4][:, 2 * (s // 2) + pg, (2 + s % 2) * P:(3 + s % 2) * P]
            return kvb[v % 4][:, 2 + pg, s * P:(s + 1) * P]

        def new_values(v, s):
            if v % 2:
                return (vw if s // 2 else vs)[0:TS, NT, s % 2 * P:(s % 2 + 1) * P]
            return va[0:TS, NT, s * P:(s + 1) * P]

        V_STORES = 2 * (NT + 1) + NT + NS

        def used_up(n):
            if n < W_IN:
                return ada_mm, n - W_ADA0 + 1
            if n < W_IN + 7:
                return pj_mm, (NT + 1) * (n - W_IN + 1)
            if n < W_CMP:
                return gate_mm, 1
            if n < W_OUT:
                return spv_mm, 2 * NS
            if n < W_UP0:
                return out_mm, 4 * (n - W_OUT + 1)
            if n < W_DOWN0:
                return up_mm, 4 * (n - W_UP0 + 1)
            if n < W_ADA1:
                return down_mm, n - W_DOWN0 + 1
            if n < W_GIN:
                return ada_mm, 12 + n - W_ADA1 + 1
            if n < W_GOUT:
                return gin_mm, gin_upto[n - W_GIN]
            if n < W_UP1:
                return out_mm, 8 + 4 * (n - W_GOUT + 1)
            if n < W_DOWN1:
                return up_mm, 32 + 4 * (n - W_UP1 + 1)
            return down_mm, 8 + n - W_DOWN1 + 1

        block = ctx.enter_context(nc.Block())

        @block.sync
        def _(sp):
            sp.dma_start(cf[:, :], a["const_f32"]).then_inc(const_loaded, 16)
            sp.dma_start(cb[:, :], a["const_bf16"]).then_inc(const_loaded, 16)
            small = [
                (rows[V1_N1:V1_N1 + 16, 0, :], a["norm1_w"].rearrange("l (k p) -> (l k) p", p=P)),
                (rows[V1_N2:V1_N2 + 16, 0, :], a["norm2_w"].rearrange("l (k p) -> (l k) p", p=P)),
                (rows[V1_ADAB:P, 0, :], a["ada_b"].rearrange("l (m p) -> (l m) p", p=P)),
                (rows[V2_FIN:V2_FIN + KC, 1, :], a["final_norm_w"].rearrange("(k p) -> k p", p=P)),
                (rows[V2_SUB:V2_SUB + 1, 1, :], a["diff_subln_w"]),
                (rows[V2_GLAN:V2_GLAN + 2, 1, :], a["gla_norm_w"].rearrange("o (k p) -> (o k) p", p=P)),
                (rows[V2_BG:V2_BG + HC, 1, :], a["gla_b_gate"].rearrange("o (k p) -> (o k) p", p=P)),
                (rows[V2_C:V2_C + KC, 1, :], a["c_prompt"].rearrange("b (k p) -> (b k) p", p=P)),
                (rows[V2_C + KC:V2_ROWS, 1, :], a["c_sample"].rearrange("b (k p) -> (b k) p", p=P)),
                (rows[0:2 * CL, 2, :], a["cmp_pe"].rearrange("o v l d -> (o v l) d")),
                (lw[:, :, :], a["diff_lambda_w"].partition_broadcast(P).rearrange("p o a b -> p (o a) b")),
                (cw2[:, :, :], a["cmp_w2"].rearrange("o v j d -> j (o v) d")),
            ]
            for dst, src in small:
                sp.dma_start(dst, src).then_inc(small_loaded, 16)
            sp.dma_start(x_in, a["x_prompt"].rearrange("b (t p) d -> p (b t) d", p=P)).then_inc(x_loaded, 16)
            sp.dma_start(xs_in[0:TS, :], a["x_sample"].rearrange("n s d -> (n s) d")).then_inc(x_loaded, 16)

            sp.dma_start(gcols[:, :, :], a["gla_w_in"][0].rearrange("(k p) c -> p k c", p=P)[:, :, 3072:3088]).then_inc(gcols_loaded, 16)

            def load(n, src, k=KC, cols=None):
                if n >= WSLOTS:
                    sp.wait_ge(*used_up(n - WSLOTS))
                dst = slot(n, k) if cols is None else slot(n, k)[:, :, 0:cols]
                sp.dma_start(dst, src).then_inc(w_ready[n % WSLOTS], 16)

            def load_adaln(base, src, done):
                for n in range(WSLOTS):
                    load(base + n, src(n))
                with sp.Fori(1, 3) as i:
                    for s in range(WSLOTS):
                        sp.wait_ge(ada_mm, i * WSLOTS + (done + s - WSLOTS + 1))
                        sp.dma_start(slot(s), src(i * WSLOTS + s)).then_inc(w_ready[s], 16)

            def by_columns(w):
                v = w.rearrange("(k p) c -> p k c", p=P)
                return lambda n: v[:, :, bass.ds(n * 512, 512)]

            ada0, ada1 = by_columns(a["ada_w"][0]), by_columns(a["ada_w"][1])
            load_adaln(W_ADA0, ada0, 0)
            w_in = by_columns(a["even_w_in"][0])
            for j in range(7):
                load(W_IN + j, w_in(j))
            load(W_IN + 7, a["even_w_in"][0].rearrange("(k p) c -> p k c", p=P)[:, :, 3584:3596], cols=12)
            for v in range(2):
                load(W_CMP + v, a["cmp_w1"][0, v].rearrange("(l d) j -> d l j", d=P), CL)

            def load_out(base, w):
                for n in range(2):
                    load(base + n, by_columns(w)(n))

            def load_mlp(up, down, layer):
                for n in range(8):
                    load(up + n, by_columns(a["mlp_w1"][layer])(n))
                w2 = a["mlp_w2"][layer].rearrange("(k p) c -> p k c", p=P)
                for n in range(8):
                    load(down + n, w2[:, n % 2 * 16:n % 2 * 16 + 16, n // 2 * 256:(n // 2 + 1) * 256], 16)

            load_out(W_OUT, a["even_w_out"][0])
            sp.wait_ge(comb_ready, 1)
            sp.dma_start(wg[0:RANK, :], a["gla_w_gate"][0]).then_inc(wg_loaded, 16)
            load_mlp(W_UP0, W_DOWN0, 0)
            load_adaln(W_ADA1, ada1, 12)
            for n in range(6):
                load(W_GIN + n, by_columns(a["gla_w_in"][0])(n))
            load_out(W_GOUT, a["gla_w_out"][0])
            for r in range(2):
                sp.wait_ge(s0_stored[r], 16 * HC // 2)
            sp.wait_ge(gs_stored, 16 * HC)
            load_mlp(W_UP1, W_DOWN1, 1)

        @block.gpsimd
        def _(pool):
            pool.dma_start(pagesb[:, :], a["page_table"].rearrange("n p -> (n p)").rearrange("(o m) -> o m", o=1)
                           ).then_inc(pages_loaded, 16)
            pool.wait_ge(pages_loaded, 16)
            page = [pool.value_load(pagesb[0:1, m:m + 1], min_val=0, max_val=a["cache_diff_k"].shape[1] - 1)
                    for m in range(NS * NPAGE)]
            cmp_pages = a["cache_cmp_kv"][0].rearrange("f t v g d -> f t (v g d)")
            for m in range(NS * NPAGE):
                pool.dma_start(ctok[:, m, :], cmp_pages[bass.ds(page[m], 1)].rearrange("o t c -> (o t) c")
                               ).then_inc(ctok_loaded, 16)
            for v in range(2):
                pool.dma_start(cw1[:, v, :].rearrange("p (l j) -> p l j", l=CL),
                               a["cmp_w1"][0, v].rearrange("(l d) j -> d l j", d=P)).then_inc(cmpw_loaded, 16)
            pool.wait_ge(cmp2_kept, 1)
            pool.wait_ge(x_evac, KC + 1)
            pool.wait_ge(lam_ready, 1)
            pool.memset(qAs[:, :, :, :], 0.0).then_inc(scratch_zero, 1)
            pool.memset(qBs[:, :, :, :], 0.0).then_inc(scratch_zero, 1)
            pool.dma_start(out[12][0][:, 0:PAST - DS], a["state_win_kv"][0][:, DS:PAST]).then_inc(out_stored, 16)

            def kv_out(o_p, o_s, t):
                if t < NT:
                    return o_p[t * P:(t + 1) * P]
                return o_s

            dk = (out[2].rearrange("e b t h m d -> (e b t) (h m d)"), out[8].rearrange("e n t h m d -> (e n t) (h m d)"))
            dv = (out[3].rearrange("e b t h d -> (e b t) (h d)"), out[9].rearrange("e n t h d -> (e n t) (h d)"))
            kv = {CKV: (out[4].rearrange("e b t v g d -> (e b t) (v g d)"), out[10].rearrange("e n t v g d -> (e n t) (v g d)")),
                  SKV: (out[5].rearrange("e b t v g d -> (e b t) (v g d)"), out[11].rearrange("e n t v g d -> (e n t) (v g d)")),
                  WKV: (out[6].rearrange("e b t v g d -> (e b t) (v g d)"), None)}
            win_s = out[12].rearrange("e n t v g d -> (e n) t (v g d)")
            for u, (j, t) in enumerate(pj_units):
                M = rows_of(t)
                if has_dve[u]:
                    pool.wait_ge(tok_ready, use_of[u] + 1)
                if has_act[u]:
                    pool.wait_ge(pj_act, act_upto[u])
                r = use_of.get(u)
                if j == KA:
                    pool.dma_start(kv_out(*dk, t), tok[0:M, r % 3, :]).then_inc(tok_stored[r % 3], 16)
                elif j == VA:
                    pool.dma_start(kv_out(*dv, t), va[0:M, t, :]).then_inc(v_stored, 16)
                elif j == CKV:
                    pool.dma_start(kv_out(*kv[j], t), tok[0:M, r % 3, :]).then_inc(tok_stored[r % 3], 16)
                elif j in (SKV, WKV):
                    v = vs if j == SKV else vw
                    if (j, t) == (WKV, NT):
                        for n in range(NS):
                            new = win_s[n, PAST - DS:PAST]
                            pool.dma_start(new[:, 0:256], tok[DS * n:DS * n + DS, r % 3, 0:256]).then_inc(tok_stored[r % 3], 16)
                            pool.dma_start(new[:, 256:512], v[DS * n:DS * n + DS, t, :]).then_inc(v_stored, 16)
                    else:
                        o = kv_out(*kv[j], t)
                        pool.dma_start(o[:, 0:256], tok[0:M, r % 3, 0:256]).then_inc(tok_stored[r % 3], 16)
                        pool.dma_start(o[:, 256:512], v[0:M, t, :]).then_inc(v_stored, 16)
            pool.wait_ge(cmpp_mm, 2)
            ck = a["cache_diff_k"][0].rearrange("f t h m d -> f t (h m d)")
            cv = a["cache_diff_v"][0].rearrange("f t h d -> f t (h d)")
            cs = a["cache_sel_kv"][0].rearrange("f t v g d -> f t (v g d)")
            win = a["state_win_kv"][0].rearrange("n (b p) v g d -> n p b (v g d)", p=P)
            for v in range(2 * NS):
                n = v // 2
                if v == 3:
                    pool.wait_ge(o_kept, HA + HB)
                if v >= 4:
                    pool.wait_ge(spv_mm, v - 3)
                if v % 2 == 0:
                    for b, cache in enumerate((ck, cv)):
                        for pg in range(NPAGE):
                            pool.dma_start(kvb[v % 4][:, 2 * b + pg, :], cache[bass.ds(page[n * NPAGE + pg], 1)].rearrange("o t c -> (o t) c")
                                           ).then_inc(kv_loaded[v % 4], 16)
                else:
                    for pg in range(NPAGE):
                        pool.dma_start(kvb[v % 4][:, pg, :], cs[bass.ds(page[n * NPAGE + pg], 1)].rearrange("o t c -> (o t) c")
                                       ).then_inc(kv_loaded[v % 4], 16)
                    pool.dma_start(kvb[v % 4][:, 2:4, :], win[n]).then_inc(kv_loaded[v % 4], 16)
            states = a["state_gla"][0].rearrange("n h d e -> h d n e")
            new_states = out[13][0].rearrange("n h d e -> h d n e")
            pool.wait_ge(gin_mm, len(gin))

            def load_state(h):
                if h >= 2:
                    pool.wait_ge(s0_stored[h % 2], 16 * (h // 2))
                pool.dma_start(s0[:, h % 2, :, :], states[h]).then_inc(s0_loaded[h % 2], 16)

            load_state(0)
            load_state(1)
            for h in range(HC):
                pool.wait_ge(s_ready, NCH * (h + 1))
                pool.dma_start(out[7][0, 0, h], sp_[:, 0, :]).then_inc(gs_stored, 16)
                pool.wait_ge(st_kept, 8 * (h + 1))
                pool.dma_start(new_states[h], s0[:, h % 2, :, :]).then_inc(s0_stored[h % 2], 16)
                if h + 2 < HC:
                    load_state(h + 2)
            for t in range(NT + 1):
                M = rows_of(t)
                pool.wait_ge(fin_kept, 2 * t + 2)
                dst = out[0][0, t * P:(t + 1) * P] if t < NT else out[1].rearrange("n s d -> (n s) d")
                pool.dma_start(dst, fin[0:M, t % 2, :]).then_inc(fin_stored[t % 2], 16)
            pool.wait_ge(gs_stored, 16 * HC)
            for r in range(2):
                pool.wait_ge(s0_stored[r], 16 * (HC // 2))
                pool.wait_ge(fin_stored[r], 16 * ((NT + 2 - r) // 2))
            OUT_STORES = 1
            pool.wait_ge(v_stored, 16 * V_STORES)
            for i in range(3):
                pool.wait_ge(tok_stored[i], 16 * stores_in_slot[i])
            pool.wait_ge(out_stored, 16 * OUT_STORES)

        @block.tensor
        def _(pe):
            pe.wait_ge(const_loaded, 32)
            pe.wait_ge(small_loaded, 16 * 12)
            pe.transpose(ps[:, 0, 0:P], rows[:, 0, :], ident[:, :])
            pe.transpose(ps[:, 0, P:P + V2_ROWS], rows[0:V2_ROWS, 1, :], ident[0:V2_ROWS, 0:V2_ROWS])
            pe.transpose(ps[:, 0, 256:256 + 2 * CL], rows[0:2 * CL, 2, :], ident[0:2 * CL, 0:2 * CL]).then_inc(small_turned, 1)
            pe.wait_ge(x_loaded, 32)
            for k in range(KC + 1):
                if k >= 3:
                    pe.wait_ge(x_evac, k - 2)
                bank = ps[:, 1 + k % 3, :]
                if k < KC:
                    for t in range(NT):
                        mm = pe.transpose(bank[:, t * P:(t + 1) * P], x_in[:, t, k * P:(k + 1) * P], ident[:, :])
                else:
                    for kk in range(KC):
                        mm = pe.transpose(bank[:, kk * TS:(kk + 1) * TS], xs_in[0:TS, kk * P:(kk + 1) * P], ident[0:TS, 0:TS])
                mm.then_inc(x_turned, 1)
            pe.wait_ge(ctok_loaded, 16 * NS * NPAGE)
            pe.wait_ge(cmpw_loaded, 32)
            pe.wait_ge(small_kept, 3)
            pe.wait_ge(x_evac, KC + 1)
            for v in range(2):
                for q in range(8):
                    g, pair = q // 4, q % 4
                    c = 8 * v + q
                    if c >= 4:
                        pe.wait_ge(cxs_ready, c - 3)
                    for w in range(4):
                        n, pg = 2 * pair + w // 2, w % 2
                        mm = pe.transpose(ps[:, 4 + c % 4, w * P:(w + 1) * P],
                                          ctok[:, n * NPAGE + pg, (2 * v + g) * P:(2 * v + g + 1) * P], ident[:, :])
                    mm.then_inc(ctok_turned, 1)
                pe.wait_ge(cxs_ready, 8 * v + 8)
                if v == 1:
                    pe.wait_ge(small_kept, 3)
                blocks = cxs[:, :, :].rearrange("p s (i r) -> p s i r", r=CS)
                for l in range(CL):
                    w1 = cw1[:, v, l * P:(l + 1) * P]
                    pe.matmul(ps[:, 2 * v, 0:16 * NB_S].rearrange("p (s i) -> p s i", s=16), w1,
                              blocks[:, :, l // CS:l // CS + NB_S, l % CS], start=l == 0, stop=l == CL - 1)
                    mm = pe.matmul(ps[:, 2 * v + 1, 0:1], w1, peT[:, v * CL + l:v * CL + l + 1], start=l == 0, stop=l == CL - 1)
                mm.then_inc(cmp_mm, 1)
            for v in range(2):
                pe.wait_ge(cmp_hid, v + 1)
                if v == 0:
                    mm = pe.matmul(ps[:, 4, 0:GB * NS * NB_S], cw2[:, 0, :], hids[:, 0, :], start=True, stop=True)
                else:
                    for g in range(GB):
                        mm = pe.matmul(ps[0:NS * NB_S, 5, g * P:(g + 1) * P], hids[:, 1, g * NS * NB_S:(g + 1) * NS * NB_S],
                                       cw2[:, 1, :], start=True, stop=True)
            mm.then_inc(cmp2_mm, 1)

            def adaln(layer, base):
                pe.wait_ge(silu_ready, 1)
                with pe.Fori(0, 3) as i:
                    for s in range(WSLOTS):
                        pe.wait_ge(ada_kept, i * WSLOTS + (16 * layer + s + 1))
                        pe.wait_ge(w_ready[s], (i + (base // WSLOTS + 1)) * 16)
                        for c in range(4):
                            for k in range(KC):
                                mm = pe.matmul(ps[:, s, c * 16:c * 16 + 9], slot(s)[:, k, c * P:(c + 1) * P], scT[:, k, :],
                                               start=k == 0, stop=k == KC - 1)
                        mm.then_inc(ada_mm, 1)

            def norm(idx):
                for k in range(KC):
                    pe.wait_ge(norm_sq, idx * KC + k + 1)
                    pe.matmul(ps[:, 0, :], ones[:, :], hT[:, k, 0:SEQ], start=k == 0, stop=k == KC - 1)
                    mm = pe.matmul(ps[:, 1, 0:TS], ones[:, :], hT[:, k, SEQ:T], start=k == 0, stop=k == KC - 1)
                mm.then_inc(norm_sum, 1)

            def weight(n):
                pe.wait_ge(w_ready[n % WSLOTS], 16 * (n // WSLOTS + 1))

            pe.wait_ge(x_evac, KC + 1)
            pe.wait_ge(cmp_hid, 2)
            adaln(0, W_ADA0)
            pe.wait_ge(ada_kept, 16)
            norm(0)
            pe.wait_ge(h_prompt, KC)
            pe.wait_ge(h_sample, 1)
            pe.wait_ge(cmp2_kept, 1)

            def turn(u):
                r = use_of.get(u)
                if r is None or r not in turn_no:
                    return
                j, t = pj_units[u]
                M, i = rows_of(t), turn_no[r]
                pe.wait_ge(tok_ready, r + 1)
                if j == CKV:
                    pe.wait_ge(pj_act, act_upto[u])
                if i >= 4:
                    pe.wait_ge(turn_kept, i - 3)
                for b in range(4 if j in (QA, KA, QB, CKV) else 2):
                    mm = pe.transpose(ps[:, 4 + i % 4, b * M:(b + 1) * M], tok[0:M, r % 3, b * P:(b + 1) * P], ident[0:M, 0:M])
                mm.then_inc(tok_turned, 1)

            for u, (j, t) in enumerate(pj_units):
                M = rows_of(t)
                if t == 0:
                    weight(W_IN + j)
                if u >= 4:
                    pe.wait_ge(pj_dve, dve_upto[u - 4])
                    if act_upto[u - 4]:
                        pe.wait_ge(pj_act, act_upto[u - 4])
                for k in range(KC):
                    mm = pe.matmul(ps[0:M, u % 4, :], hT[:, k, t * P:t * P + M], slot(W_IN + j)[:, k, :],
                                   start=k == 0, stop=k == KC - 1)
                mm.then_inc(pj_mm, 1)
                if u:
                    turn(u - 1)
            turn(len(pj_units) - 1)
            weight(W_IN + 7)
            pe.wait_ge(pj_dve, dve_upto[-1])
            pe.wait_ge(pj_act, act_upto[-1])
            for t in range(NT + 1):
                M = rows_of(t)
                for k in range(KC):
                    mm = pe.matmul(ps[0:M, 0, t * 16:t * 16 + 12], hT[:, k, t * P:t * P + M], slot(W_IN + 7)[:, k, 0:12],
                                   start=k == 0, stop=k == KC - 1)
            mm.then_inc(gate_mm, 1)
            pe.wait_ge(turn_kept, len(turns))
            pe.wait_ge(pe_col, 1)
            for v in range(2):
                weight(W_CMP + v)
                blocks = cxp[:, v, :].rearrange("p (i r) -> p i r", r=CS)
                for l in range(CL):
                    mm = pe.matmul(ps[:, 1 + v, 0:2 * (NB_P + 1) + 1], slot(W_CMP + v, CL)[:, l, :],
                                   blocks[:, l // CS:l // CS + 2 * (NB_P + 1) + 1, l % CS], start=l == 0, stop=l == CL - 1)
                mm.then_inc(cmpp_mm, 1)
            pe.wait_ge(gate_diag, 1)
            for b in range(2):
                mm = pe.matmul(ps[:, 4 + b, 0:6 * TS], ones[0:TS, :], gdiag[0:TS, 6 * b:6 * b + 6, :], start=True, stop=True)
            mm.then_inc(gb_mm, 1)
            pe.wait_ge(cmpp_hid, 2)
            pe.matmul(ps[:, 3, 0:2 * NB_P], cw2[:, 0, :], hidp[:, 0, 0:2 * NB_P], start=True, stop=True)
            for g in range(GB):
                mm = pe.matmul(ps[0:NB_P, 3, (1 + g) * P:(2 + g) * P], hidp[:, 1, g * NB_P:(g + 1) * NB_P], cw2[:, 1, :],
                               start=True, stop=True)
            mm.then_inc(cmpp2_mm, 1)
            pe.wait_ge(cmpp2_kept, 2)
            for h in range(HB):
                for t in range(NT):
                    c = (h * NT + t) * NB_P
                    mm = pe.matmul(ps[:, 6, c:c + NB_P], qbT[:, h, t * P:(t + 1) * P], kccp[:, h // 2, :], start=True, stop=True)
            mm.then_inc(cs_mm, 1)
            pe.wait_ge(cs_p, 1)
            pe.wait_ge(gb_kept, 1)
            for h in range(HB):
                for t in range(NT):
                    mm = pe.transpose(ps[0:NB_P, 4 + h, t * P:(t + 1) * P], s1[:, h * NT + t, :], ident[:, :])
                mm.then_inc(cs_turned, 1)
            pe.wait_ge(ptc_kept, HB)

            def p_scores(v):
                h, t, b = units[v]
                if v >= 3:
                    pe.wait_ge(p_ready, v - 2)
                bank, W = ps[:, v % 3, :], (t + 1) * P
                if h < HA:
                    lo = slice(64 * b, 64 * b + 64)
                    q, keys = qaT[lo, h, t * P:(t + 1) * P], kaT[lo, h, 0:W]
                else:
                    q, keys = qbT[:, h - HA, t * P:(t + 1) * P], (wkT if b else skT)[:, (h - HA) // 2, 0:W]
                pe.matmul(bank[:, W - P:W], identb, causalb, start=True, stop=True)
                pe.matmul(bank[:, 0:W], q, keys, start=False, stop=True, skip_group_check=True).then_inc(s_mm, 1)

            def p_turn(v):
                h, t, b = units[v]
                w = group_of[v]
                pe.wait_ge(diag_ready, v + 1)
                if not group_ends[v]:
                    return
                if w >= 2:
                    pe.wait_ge(pt_kept, w - 1)
                both = [v - 1, v] if h < HA else [v]
                for kb in range(t + 1):
                    for u in both:
                        mm = pe.matmul(ps[:, 3 + w % 2, kb * P:(kb + 1) * P], pbuf[:, u % 3, kb * P:(kb + 1) * P], diag[:, u % 3, :],
                                       start=u == both[0], stop=u == v)
                mm.then_inc(pt_mm, 1)

            def p_values(w):
                h, t, b = groups[w]
                pe.wait_ge(pt_kept, w + 1)
                if t == 0 and b == 0 and h >= 2:
                    pe.wait_ge(o_kept, h - 1)
                o = ps[:, 5 + h % 2, t * P:(t + 1) * P]
                for kb in range(t + 1):
                    if h < HA:
                        vals = va[:, kb, h * P:(h + 1) * P]
                    else:
                        vals = (vw if b else vs)[:, kb, (h - HA) // 2 * P:((h - HA) // 2 + 1) * P]
                    mm = pe.matmul(o, vals, ptb[:, w % 3, kb * P:(kb + 1) * P], start=kb == 0 and b == 0, stop=kb == t and h < HA)
                if h >= HA and b == 1:
                    mm = pe.matmul(o, vccp[0:NB_P, (h - HA) // 2, :], ptc[0:NB_P, h - HA, t * P:(t + 1) * P], start=False, stop=True)
                mm.then_inc(pv_mm, 1)

            for v in range(len(units) + 4):
                if v < len(units):
                    p_scores(v)
                if 2 <= v < len(units) + 2:
                    p_turn(v - 2)
                if v >= 4 and group_ends[v - 4]:
                    p_values(group_of[v - 4])

            pe.wait_ge(o_kept, HA + HB)
            pe.wait_ge(qbc_ready, 1)
            for g in range(GB):
                mm = pe.matmul(ps[:, 7, g * P:g * P + NS * NB_S], qbc[:, g, :], kccs[:, g, :], start=True, stop=True)
            mm.then_inc(ss_mm, 1)
            pe.wait_ge(ss_p, 1)
            for g in range(GB):
                mm = pe.transpose(ps[0:NS * NB_S, 6, g * P:(g + 1) * P], sc[:, g, :], ident[:, :])
            mm.then_inc(ss_turned, 1)
            pe.wait_ge(ss_kept, 1)
            for g in range(GB):
                mm = pe.matmul(ps[:, 7, g * P:(g + 1) * P], vccs[0:NS * NB_S, g, :], ptsc[0:NS * NB_S, g, :], start=True, stop=True)
            mm.then_inc(ss_pv, 1)

            def s_keys(v):
                pe.wait_ge(kv_loaded[v % 4], kv_upto[v])
                for half in range(2):
                    c = 2 * v + half
                    if c >= 3:
                        pe.wait_ge(kt_kept, c - 2)
                    for w in range(4):
                        s, pg = 2 * half + w // 2, w % 2
                        mm = pe.transpose(ps[:, c % 3, w * P:(w + 1) * P], cached_keys(v, s, pg), ident[:, :])
                    mm.then_inc(kt_mm, 1)

            def s_scores(v):
                n, kind = v // 2, v % 2
                pe.wait_ge(kt_kept, 2 * v + 2)
                if v >= 2:
                    pe.wait_ge(sp_ready, v - 1)
                bank = ps[:, 3 + v % 2, :]
                pe.matmul(bank[:, PAST:PAST + TS], identb, newmask[:, n, :], start=True, stop=True)
                for s in range(4):
                    q = qBs[:, s % 2, n, :] if kind else qAs[:, n, s, :]
                    new = (wkT if s // 2 else skT)[:, s % 2, SEQ:T] if kind else kaT[:, s, SEQ:T]
                    pe.matmul(bank[32 * s:32 * s + 32, 0:PAST], q, kts[:, v % 2, s, :], start=False, stop=True, skip_group_check=True)
                    mm = pe.matmul(bank[32 * s:32 * s + 32, PAST:PAST + TS], q, new, start=False, stop=True, skip_group_check=True)
                mm.then_inc(ss2_mm, 1)

            def s_turn(v):
                pe.wait_ge(sdiag_ready, v + 1)
                if v >= 1:
                    pe.wait_ge(spt_kept, v)
                for b in range(3):
                    m = P if b < 2 else TS
                    mm = pe.matmul(ps[0:m, 5, b * P:(b + 1) * P], pbuf[:, v % 3, b * P:b * P + m], diag[:, v % 3, :], start=True, stop=True)
                mm.then_inc(spt_mm, 1)

            def s_values(v):
                pe.wait_ge(spt_kept, v + 1)
                if v >= 2:
                    pe.wait_ge(so_kept, v - 1)
                for s in range(4):
                    for b in range(3):
                        m = P if b < 2 else TS
                        vals = cached_values(v, s, b) if b < 2 else new_values(v, s)
                        mm = pe.matmul(ps[:, 6 + v % 2, 32 * s:32 * s + 32], vals, ptb[0:m, v % 3, b * P + 32 * s:b * P + 32 * s + 32],
                                       start=b == 0, stop=b == 2)
                mm.then_inc(spv_mm, 1)

            pe.wait_ge(oc_kept, 1)
            for v in range(2 * NS + 3):
                if v < 2 * NS:
                    s_keys(v)
                if 1 <= v <= 2 * NS:
                    s_scores(v - 1)
                if 2 <= v <= 2 * NS + 1:
                    s_turn(v - 2)
                if v >= 3:
                    s_values(v - 3)

            for h in range(HA):
                pe.wait_ge(sub_sq, h + 1)
                pe.matmul(ps[:, h, :], ones[:, :], sq[:, h, 0:SEQ], start=True, stop=True)
                mm = pe.matmul(ps[:, 4, h * TS:(h + 1) * TS], ones[:, :], sq[:, h, SEQ:T], start=True, stop=True)
            mm.then_inc(sub_sum, 1)
            pe.wait_ge(mix_ready, 1)

            def out_projection(layer):
                for m in range(KC):
                    if m % 4 == 0:
                        weight((W_GOUT if layer else W_OUT) + m // 4)
                    if m >= 4:
                        pe.wait_ge(resid_kept, layer * KC + m - 3)
                    w = slot((W_GOUT if layer else W_OUT) + m // 4)
                    for k in range(KC):
                        lhs = w[:, k, m % 4 * P:(m % 4 + 1) * P]
                        pe.matmul(ps[:, m % 4, :], lhs, hT[:, k, 0:SEQ], start=k == 0, stop=k == KC - 1)
                        mm = pe.matmul(ps[:, 4 + m % 4, 0:TS], lhs, hT[:, k, SEQ:T], start=k == 0, stop=k == KC - 1)
                    mm.then_inc(out_mm, 1)

            def mlp(layer):
                base = (W_UP1 if layer else W_UP0) // WSLOTS + 1
                with pe.Fori(0, 2) as i:
                    for s in range(WSLOTS):
                        pe.wait_ge(w_ready[s], (i + base) * 16)
                        for c in range(4):
                            pe.wait_ge(up_free, i * 16 + (4 * s + c + 1 + (DFF // P + 4) * layer))
                            for k in range(KC):
                                lhs = slot(s)[:, k, c * P:(c + 1) * P]
                                pe.matmul(ps[:, c, :], lhs, hT[:, k, 0:SEQ], start=k == 0, stop=k == KC - 1)
                                mm = pe.matmul(ps[:, 4 + c, 0:TS], lhs, hT[:, k, SEQ:T], start=k == 0, stop=k == KC - 1)
                            mm.then_inc(up_mm, 1)
                base = (W_DOWN1 if layer else W_DOWN0) // WSLOTS + 1
                pe.wait_ge(relu_free, (DFF // P + 2) * (layer + 1))
                pe.wait_ge(up_free, (DFF // P + 4) * (layer + 1))
                with pe.Fori(0, 2) as i:
                    for s in range(WSLOTS):
                        q, kh = s // 2, s % 2
                        pe.wait_ge(w_ready[s], (i + base) * 16)
                        if kh == 0:
                            pe.wait_ge(down_free, i * 2 + (q + 1 + 6 * layer))
                        for m in range(2):
                            for k in range(16):
                                lhs = slot(s, 16)[:, k, m * P:(m + 1) * P]
                                first, last = kh == 0 and k == 0, kh == 1 and k == 15
                                pe.matmul(ps[:, 3 * q + m, :], lhs, hid[:, 16 * kh + k, 0:SEQ], start=first, stop=last,
                                          skip_group_check=True)
                                mm = pe.matmul(ps[:, 3 * q + 2, m * TS:(m + 1) * TS], lhs, hid[:, 16 * kh + k, SEQ:T],
                                               start=first and m == 0, stop=last, skip_group_check=True)
                        mm.then_inc(down_mm, 1)

            out_projection(0)
            norm(1)
            pe.wait_ge(h_prompt, 2 * KC)
            pe.wait_ge(h_sample, 2)
            mlp(0)

            adaln(1, W_ADA1)
            pe.wait_ge(ada_kept, 32)
            norm(2)
            pe.wait_ge(h_prompt, 3 * KC)
            pe.wait_ge(h_sample, 3)
            pe.wait_ge(gcols_loaded, 16)
            for k in range(KC):
                pe.matmul(ps[0:RANK, 0, :], gcols[:, k, :], hT[:, k, 0:SEQ], start=k == 0, stop=k == KC - 1)
                mm = pe.matmul(ps[0:RANK, 4, 0:TS], gcols[:, k, :], hT[:, k, SEQ:T], start=k == 0, stop=k == KC - 1)
            mm.then_inc(gl_mm, 1)
            pe.wait_ge(gl_kept, 1)
            pe.wait_ge(wg_loaded, 16)
            for h in range(HC):
                lhs = wg[0:RANK, h * P:(h + 1) * P]
                pe.matmul(ps[:, h, :], lhs, glT[0:RANK, 0:SEQ], start=True, stop=True)
                pe.matmul(ps[:, 4 + h, 0:TS], lhs, glT[0:RANK, SEQ:T], start=True, stop=True).then_inc(gz_mm, 1)
            pe.wait_ge(gz_abs, 2 * HC)
            for u, (kind, c, t) in enumerate(gin):
                if u in [0] + gin_upto[:-1]:
                    weight(W_GIN + ([0] + gin_upto[:-1]).index(u))
                w = slot(W_GIN + sum(u >= x for x in gin_upto))
                if u >= 4:
                    pe.wait_ge(gin_kept, u - 3)
                M = rows_of(t)
                for k in range(KC):
                    first, last = k == 0, k == KC - 1
                    if kind == "v":
                        mm = pe.matmul(ps[0:M, u % 4, :], hT[:, k, t * P:t * P + M], w[:, k, :], start=first, stop=last)
                    else:
                        lhs = w[:, k, c % 4 * P:(c % 4 + 1) * P]
                        pe.matmul(ps[:, u % 4, :], lhs, hT[:, k, 0:SEQ], start=first, stop=last)
                        mm = pe.matmul(ps[:, 4 + u % 4, 0:TS], lhs, hT[:, k, SEQ:T], start=first, stop=last)
                mm.then_inc(gin_mm, 1)

            def g_prepare(h):
                pe.wait_ge(prep_ready, h + 1)
                if h == 0:
                    pe.wait_ge(gin_kept, len(gin))
                if h:
                    pe.wait_ge(att_kept, h)
                    pe.wait_ge(kd_kept, h)
                for t in range(NT):
                    pe.transpose(ps[:, 1, t * P:(t + 1) * P], gkd[:, t * P:(t + 1) * P], ident[:, :])
                pe.transpose(ps[0:TS, 0, 384:512], gkd[:, SEQ:T], ident[:, :]).then_inc(kd_turned, 1)
                for c in range(NCH):
                    lo = 64 * (c % 2)
                    for i in range(4):
                        rhs = gqd[:, c, (i - 1) * SUB:i * SUB] if i else gqe[:, h % 2, c * GCH:c * GCH + SUB]
                        pe.matmul(ps[lo:lo + (i + 1) * SUB, 0, c // 2 * GCH + i * SUB:c // 2 * GCH + (i + 1) * SUB],
                                  gkp[i][:, c, :], rhs, start=True, stop=True)
                pe.matmul(ps[0:TS, 0, 4 * GCH:5 * GCH], gkp_s, gqe[:, h % 2, SEQ:T], start=True, stop=True).then_inc(att_mm, 1)

            def g_states(h, p):
                x = 8 * h + p
                if x >= 3:
                    pe.wait_ge(st_kept, x - 2)
                for w in range(2):
                    if p < 4:
                        lo = slice(64 * w, 64 * w + 64)
                        lhs, rhs = gkdT[lo, h % 2, p, :], gv[lo, p, h * DVC:(h + 1) * DVC]
                    else:
                        lhs, rhs = gkdm[0:TS, 2 * (p - 4) + w, :], gv[0:TS, NT, h * DVC:(h + 1) * DVC]
                    if p < 4 and w:
                        pe.wait_ge(st_first, 4 * h + p + 1)
                    mm = pe.matmul(ps[:, 5 + x % 3, w * DVC:(w + 1) * DVC], lhs, rhs, start=True, stop=True)
                    if p < 4 and w == 0:
                        mm.then_inc(st_first, 1)
                mm.then_inc(st_mm, 1)

            def g_out(h, c):
                if c:
                    pe.wait_ge(s_ready, NCH * h + c)
                    pe.wait_ge(go_mm, NCH * h + c)
                lo = slice(64 * (c % 2), 64 * (c % 2) + 64)
                for e in range(2):
                    o = ps[:, 3 + e, c * GCH:(c + 1) * GCH]
                    if c:
                        pe.matmul(o, sp_[:, c % 4, e * P:(e + 1) * P], gqe[:, h % 2, c * GCH:(c + 1) * GCH], start=True, stop=False)
                    mm = pe.matmul(o, gv[lo, c // 2, h * DVC + e * P:h * DVC + (e + 1) * P], gatt[lo, h % 2, c // 2, :],
                                   start=c == 0, stop=True)
                mm.then_inc(go_mm, 1)

            def g_core(h):
                pe.wait_ge(att_kept, h + 1)
                pe.wait_ge(kd_kept, h + 1)
                if h:
                    pe.wait_ge(go_kept, h)
                for p in range(3):
                    g_states(h, p)
                g_out(h, 0)
                g_out(h, 1)
                g_states(h, 3)
                for c in range(2, NCH):
                    g_out(h, c)
                pe.wait_ge(s0_loaded[h % 2], 16 * (h // 2 + 1))
                for e in range(2):
                    o = ps[:, 2, e * TS:(e + 1) * TS]
                    pe.matmul(o, gv[0:TS, NT, h * DVC + e * P:h * DVC + (e + 1) * P], gatt[0:TS, h % 2, 4, :], start=True, stop=True)
                    for n in range(NS):
                        mm = pe.matmul(o[:, DS * n:DS * n + DS], s0[:, h % 2, n, e * P:(e + 1) * P],
                                       gqe[:, h % 2, SEQ + DS * n:SEQ + DS * n + DS], start=False, stop=True, skip_group_check=True)
                mm.then_inc(os_mm, 1)
                for p in range(4, 8):
                    g_states(h, p)

            g_prepare(0)
            for h in range(HC):
                if h + 1 < HC:
                    g_prepare(h + 1)
                g_core(h)
            pe.wait_ge(st_kept, 8 * HC)
            for h in range(HC):
                pe.wait_ge(gn_sq, 2 * h + 2)
                for e in range(2):
                    pe.matmul(ps[:, h, :], ones[:, :], gsq[:, 2 * h + e, 0:SEQ], start=e == 0, stop=e == 1)
                    mm = pe.matmul(ps[:, 4 + h, 0:TS], ones[:, :], gsq[:, 2 * h + e, SEQ:T], start=e == 0, stop=e == 1)
            mm.then_inc(gn_sum, 1)
            pe.wait_ge(gmix_ready, 1)
            out_projection(1)
            norm(3)
            pe.wait_ge(h_prompt, 4 * KC)
            pe.wait_ge(h_sample, 4)
            mlp(1)
            norm(4)
            for t in range(NT + 1):
                M = rows_of(t)
                for half in range(2):
                    c = 2 * t + half
                    pe.wait_ge(fin_ready, KC)
                    if c >= 4:
                        pe.wait_ge(fin_kept, c - 3)
                    for w in range(4):
                        k = 4 * half + w
                        mm = pe.transpose(ps[0:M, 2 + c % 4, w * P:(w + 1) * P], hT[:, k, t * P:t * P + M], ident[:, :])
                    mm.then_inc(fin_mm, 1)

        @block.scalar
        def _(act):
            act.wait_ge(small_kept, 2)
            act.activation(cexp, v2T[:, V2_C:V2_ROWS], ACT.Exp, scale=-1.0).then_inc(cexp_ready, 1)
            act.wait_ge(lam_sums, 1)
            act.activation(lam[:, 2:4], lam[:, 0:2], ACT.Exp).then_inc(lam_exp, 1)
            for c in range(16):
                if c == 8:
                    act.wait_ge(cmp_mm, 1)
                act.wait_ge(ctok_turned, c + 1)
                q = c % 8
                dst = cxs[:, 8 * (q // 4) + 2 * (q % 4):8 * (q // 4) + 2 * (q % 4) + 2, :]
                act.activation(dst, ps[:, 4 + c % 4, :].rearrange("p (s t) -> p s t", s=2), ACT.Copy).then_inc(cxs_ready, 1)
            for v in range(2):
                act.wait_ge(cmp_exp, v + 1)
                act.activation(hids[:, v, :], hids[:, v, :], ACT.Exp, scale=-1.0).then_inc(act_chain, 1)

            def norm(idx, ready, count):
                act.wait_ge(ready, count)
                for k in range(KC):
                    act.activation(hT[:, k, :], xT[:, k, :], ACT.Square).then_inc(norm_sq, 1)
                act.wait_ge(norm_sum, idx + 1)
                act.activation(rstd[:, 0:SEQ], ps[:, 0, :], ACT.Sqrt, scale=1.0 / D, bias=eps[:, 0:1])
                act.activation(rstd[:, SEQ:T], ps[:, 1, 0:TS], ACT.Sqrt, scale=1.0 / D, bias=eps[:, 0:1]).then_inc(norm_std, 1)

            def modulate(idx, term):
                for k in range(KC):
                    act.wait_ge(norm_x, idx * KC + k + 1)
                    act.activation(hT[:, k, 0:SEQ], hT[:, k, 0:SEQ], ACT.Identity, scale=modA[:, k, 0:1],
                                   bias=mod[:, term * KC + k, 0:1]).then_inc(h_prompt, 1)

            norm(0, x_evac, KC + 1)
            modulate(0, 0)

            def keep_turn(u):
                r = use_of.get(u)
                if r is None or r not in turn_no:
                    return
                j, t = pj_units[u]
                M, i = rows_of(t), turn_no[r]
                act.wait_ge(tok_turned, i + 1)
                bank = ps[:, 4 + i % 4, :]
                blocks = bank[:, 0:4 * M].rearrange("p (b m) -> p b m", b=4)
                if (j, t) == (QA, NT):
                    act.wait_ge(scratch_zero, 2)
                    for m in range(2):
                        src = bank[64 * m:64 * m + 64, 0:4 * M].rearrange("p (h n s) -> p h n s", h=HA, n=NS)
                        for h in range(HA):
                            ins = act.activation(qAs[64 * m:64 * m + 64, :, h, DS * m:DS * m + DS], src[:, h], ACT.Copy, scale=DKA ** -0.5)
                elif (j, t) == (QB, NT):
                    for h in range(HB):
                        ins = act.activation(qBs[:, h // 2, :, DS * (h % 2):DS * (h % 2) + DS],
                                             bank[:, h * TS:(h + 1) * TS].rearrange("p (n s) -> p n s", n=NS), ACT.Copy, scale=DHB ** -0.5)
                elif j == QA:
                    ins = act.activation(qaT[:, :, t * P:(t + 1) * P], blocks, ACT.Copy, scale=DKA ** -0.5)
                elif j == QB:
                    ins = act.activation(qbT[:, :, t * P:(t + 1) * P], blocks, ACT.Copy, scale=DHB ** -0.5)
                elif j == KA:
                    ins = act.activation(kaT[:, :, t * P:t * P + M], blocks, ACT.Copy)
                elif j == CKV:
                    dst = cxp[:, :, 0:2 * SEQ].rearrange("p v (g c) -> p v g c", g=GB)
                    for v in range(2):
                        ins = act.activation(dst[:, v, :, t * P:(t + 1) * P], blocks[:, 2 * v:2 * v + 2, :], ACT.Copy)
                else:
                    dst = skT if j == SKV else wkT
                    ins = act.activation(dst[:, :, t * P:t * P + M], bank[:, 0:2 * M].rearrange("p (b m) -> p b m", b=2), ACT.Copy)
                ins.then_inc(turn_kept, 1)

            for u, (j, t) in enumerate(pj_units):
                M = rows_of(t)
                if has_act[u]:
                    act.wait_ge(pj_mm, u + 1)
                    if has_dve[u]:
                        act.wait_ge(pj_dve, dve_upto[u])
                    bank = ps[0:M, u % 4, :]
                    if j == VA:
                        ins = act.activation(va[0:M, t, :], bank, ACT.Copy)
                    elif j == CKV:
                        tok_slot_free(act, use_of[u])
                        ins = act.activation(tok[0:M, use_of[u] % 3, 256:512], bank[:, 256:512], ACT.Copy)
                    else:
                        ins = act.activation((vs if j == SKV else vw)[0:M, t, :], bank[:, 256:512], ACT.Copy)
                    ins.then_inc(pj_act, 1)
                if u:
                    keep_turn(u - 1)
            keep_turn(len(pj_units) - 1)
            act.wait_ge(gate_mm, 1)
            act.activation(gates[:, 0:NT, :], ps[:, 0, 0:NT * 16].rearrange("p (t c) -> p t c", t=NT)[:, :, 0:12], ACT.Exp, scale=-1.0).then_inc(gate_exp, 1)
            act.activation(gates[0:TS, NT, :], ps[0:TS, 0, NT * 16:NT * 16 + 12], ACT.Exp, scale=-1.0).then_inc(gate_exp, 1)
            for v in range(2):
                act.wait_ge(cmpp_exp, v + 1)
                act.activation(hidp[:, v, 0:2 * NB_P], hidp[:, v, 0:2 * NB_P], ACT.Exp, scale=-1.0).then_inc(act_chain, 1)
            act.wait_ge(gb_mm, 1)
            act.activation(gb[:, :, :].rearrange("p (b c) t -> p b (c t)", b=2), ps[:, 4:6, 0:6 * TS], ACT.Copy).then_inc(gb_kept, 1)
            act.wait_ge(cs_sub, 1)
            act.activation(s1[:, :, :], s1[:, :, :], ACT.Exp).then_inc(cs_exp, 1)
            for h in range(HB):
                act.wait_ge(cs_turned, h + 1)
                act.activation(ptc[0:NB_P, h, :], ps[0:NB_P, 4 + h, :], ACT.Copy).then_inc(ptc_kept, 1)

            def p_exp(v):
                h, t, b = units[v]
                act.wait_ge(nm_ready, v + 1)
                if v >= 3:
                    act.wait_ge(pt_mm, group_of[v - 3] + 1)
                if v >= 4:
                    act.wait_ge(diag_ready, v - 3)
                W = (t + 1) * P
                act.activation(pbuf[:, v % 3, 0:W], ps[:, v % 3, 0:W], ACT.Exp, bias=nm[:, v % 4:v % 4 + 1],
                               accum_out=sums[:, v % 4:v % 4 + 1]).then_inc(p_ready, 1)

            def p_keep(w):
                h, t, b = groups[w]
                act.wait_ge(pt_mm, w + 1)
                if w >= 3:
                    act.wait_ge(pv_mm, w - 2)
                act.activation(ptb[:, w % 3, 0:(t + 1) * P], ps[:, 3 + w % 2, 0:(t + 1) * P], ACT.Copy).then_inc(pt_kept, 1)

            for i in range(3):
                act.wait_ge(tok_stored[i], 16 * stores_in_slot[i])
            for v in range(len(units) + 2):
                if v < len(units):
                    p_exp(v)
                if v >= 2 and group_ends[v - 2]:
                    p_keep(group_of[v - 2])

            act.wait_ge(ss_sub, 1)
            act.activation(sc[:, :, :], sc[:, :, :], ACT.Exp).then_inc(ss_exp, 1)
            act.wait_ge(ss_turned, 1)
            act.activation(ptsc[0:NS * NB_S, :, :], ps[0:NS * NB_S, 6, 0:GB * P].rearrange("p (g c) -> p g c", g=GB), ACT.Copy).then_inc(ss_kept, 1)

            def s_keep_keys(v):
                for half in range(2):
                    c = 2 * v + half
                    act.wait_ge(kt_mm, c + 1)
                    if v >= 2:
                        act.wait_ge(ss2_mm, v - 1)
                    act.activation(kts[:, v % 2, 2 * half:2 * half + 2, :], ps[:, c % 3, :].rearrange("p (s t) -> p s t", s=2),
                                   ACT.Copy).then_inc(kt_kept, 1)

            def s_exp(v):
                act.wait_ge(snm_ready, v + 1)
                if v >= 3:
                    act.wait_ge(spt_mm, v - 2)
                act.activation(pbuf[:, v % 3, 0:PAST + TS], ps[:, 3 + v % 2, 0:PAST + TS], ACT.Exp, bias=nm[:, v % 4:v % 4 + 1],
                               accum_out=sums[:, v % 4:v % 4 + 1]).then_inc(sp_ready, 1)

            def s_keep_turn(v):
                act.wait_ge(spt_mm, v + 1)
                if v >= 3:
                    act.wait_ge(spv_mm, v - 2)
                act.activation(ptb[:, v % 3, 0:PAST], ps[:, 5, 0:PAST], ACT.Copy)
                act.activation(ptb[0:TS, v % 3, PAST:PAST + P], ps[0:TS, 5, PAST:PAST + P], ACT.Copy).then_inc(spt_kept, 1)

            for v in range(2 * NS + 2):
                if v < 2 * NS:
                    s_keep_keys(v)
                if 1 <= v <= 2 * NS:
                    s_exp(v - 1)
                if 2 <= v:
                    s_keep_turn(v - 2)
            act.wait_ge(comb_ready, 1)
            for h in range(HA):
                act.activation(sq[:, h, :], hT[:, h, :], ACT.Square).then_inc(sub_sq, 1)
            act.wait_ge(sub_sum, 1)
            act.activation(sq[:, :, 0:SEQ], ps[:, 0:HA, :], ACT.Sqrt, scale=1.0 / P, bias=eps[:, 0:1])
            act.activation(sq[:, :, SEQ:T], ps[:, 4, 0:HA * TS].rearrange("p (h c) -> p h c", h=HA), ACT.Sqrt, scale=1.0 / P,
                           bias=eps[:, 0:1]).then_inc(sub_std, 1)
            norm(1, x_ready, 1)
            modulate(1, 3)

            def mlp(layer):
                act.sem_inc(up_free, 4)
                with act.Fori(0, DFF // P // 4) as i:
                    for c in range(4):
                        act.wait_ge(up_mm, i * 4 + (c + 1 + DFF // P * layer))
                        act.wait_ge(relu_free, i * 4 + (c + 1 + (DFF // P + 2) * layer))
                        act.activation(relu[:, c % 2, 0:SEQ], ps[:, c, :], ACT.Relu)
                        act.activation(relu[:, c % 2, SEQ:T], ps[:, 4 + c, 0:TS], ACT.Relu).then_inc(up_free, 1)

            mlp(0)

            norm(2, x_ready, 2)
            modulate(2, 0)
            act.wait_ge(gl_mm, 1)
            act.activation(glT[0:RANK, 0:SEQ], ps[0:RANK, 0, :], ACT.Copy)
            act.activation(glT[0:RANK, SEQ:T], ps[0:RANK, 4, 0:TS], ACT.Copy).then_inc(gl_kept, 1)
            act.wait_ge(gz_abs, 2 * HC)
            act.activation(gtmp[:, :, :], gtmp[:, :, :], ACT.Abs).then_inc(act_chain, 1)
            act.wait_ge(act_chain, 5)
            act.activation(gtmp[:, :, :], gtmp[:, :, :], ACT.Exp, scale=-1.0).then_inc(act_chain, 1)
            act.wait_ge(act_chain, 6)
            act.activation(gtmp[:, :, :], gtmp[:, :, :], ACT.Ln, bias=ones[:, 0:1]).then_inc(gz_ln, 1)
            for u, (kind, c, t) in enumerate(gin):
                act.wait_ge(gin_mm, u + 1)
                M = rows_of(t)
                if kind == "v":
                    ins = act.activation(gv[0:M, t, c * 512:(c + 1) * 512], ps[0:M, u % 4, :], ACT.Copy)
                else:
                    dst = {"q": gq, "k": gk, "r": gr}[kind][:, c, :]
                    scale = DKC ** -0.5 if kind == "q" else 1.0
                    act.activation(dst[:, 0:SEQ], ps[:, u % 4, :], ACT.Copy, scale=scale)
                    ins = act.activation(dst[:, SEQ:T], ps[:, 4 + u % 4, 0:TS], ACT.Copy, scale=scale)
                ins.then_inc(gin_kept, 1)
                if kind == "r":
                    act.wait_ge(gin_kept, u + 1)
                    if c >= 2:
                        act.wait_ge(r_ready, c - 1)
                    act.activation(er[:, c % 2, :], dst, ACT.Exp, scale=-1.0).then_inc(r_exp, 1)

            def g_exps(h):
                b = gbt[:, h, :]
                bp = b[:, 0:SEQ].rearrange("p (c t) -> p c t", c=NCH)
                if h == 0:
                    act.wait_ge(b_ready, HC)
                    act.wait_ge(r_ready, KC)
                else:
                    act.wait_ge(prep_ready, h)
                    act.wait_ge(att_mm, h)
                act.activation(geb, b, ACT.Exp, scale=1.0 / TAU).then_inc(eb_ready, 1)
                act.activation(gkp[0], bp[:, :, 0:SUB], ACT.Exp, scale=-1.0 / TAU)
                act.activation(gkp_s, b[:, SEQ:T], ACT.Exp, scale=-1.0 / TAU).then_inc(eb_ready, 1)
                act.wait_ge(gsub_ready, h + 1)
                act.activation(gqd, gqd, ACT.Exp, scale=1.0 / TAU)
                later = wscr[:, kp_at[1]:kp_at[4]]
                act.activation(later, later, ACT.Exp, scale=1.0 / TAU)
                act.activation(gkd, gkd, ACT.Exp, scale=1.0 / TAU).then_inc(ex_ready, 1)

            def g_keep_turn(h):
                act.wait_ge(kd_turned, h + 1)
                if h >= 2:
                    act.wait_ge(st_mm, 8 * (h - 1))
                act.activation(gkdT[:, h % 2, 0:NT, :], ps[:, 1, :].rearrange("p (t d) -> p t d", t=NT), ACT.Copy).then_inc(kd_kept, 1)

            def g_keep_out(h):
                act.wait_ge(go_mm, NCH * (h + 1))
                for e in range(2):
                    act.activation(hT[:, 2 * h + e, 0:SEQ], ps[:, 3 + e, :], ACT.Copy)
                act.wait_ge(os_mm, h + 1)
                act.activation(hT[:, 2 * h:2 * h + 2, SEQ:T], ps[:, 2, 0:2 * TS].rearrange("p (e t) -> p e t", e=2), ACT.Copy).then_inc(go_kept, 1)

            g_exps(0)
            g_keep_turn(0)
            for h in range(HC):
                if h + 1 < HC:
                    g_exps(h + 1)
                    g_keep_turn(h + 1)
                g_keep_out(h)
            act.wait_ge(go_kept, HC)
            for k in range(KC):
                act.activation(gsq[:, k, :], hT[:, k, :], ACT.Square).then_inc(gn_sq, 1)
            act.wait_ge(gn_sum, 1)
            act.activation(gstd[:, :, 0:SEQ], ps[:, 0:HC, :], ACT.Sqrt, scale=1.0 / DVC, bias=eps[:, 0:1])
            act.activation(gstd[:, :, SEQ:T], ps[:, 4:4 + HC, 0:TS], ACT.Sqrt, scale=1.0 / DVC, bias=eps[:, 0:1]).then_inc(gn_std, 1)
            norm(3, x_ready, 3)
            modulate(3, 3)
            mlp(1)
            norm(4, x_ready, 4)
            for k in range(KC):
                act.wait_ge(norm_x, 4 * KC + k + 1)
                act.activation(hT[:, k, :], hT[:, k, :], ACT.Copy, scale=v2T[:, V2_FIN + k:V2_FIN + k + 1]).then_inc(fin_ready, 1)
            for c in range(2 * (NT + 1)):
                t, half = c // 2, c % 2
                M = rows_of(t)
                act.wait_ge(fin_mm, c + 1)
                if half == 0 and t >= 2:
                    act.wait_ge(fin_stored[t % 2], 16 * (t // 2))
                act.activation(fin[0:M, t % 2, half * 512:(half + 1) * 512], ps[0:M, 2 + c % 4, :], ACT.Copy).then_inc(fin_kept, 1)

        @block.vector
        def _(dve):
            chain = [0]

            def step(ins):
                chain[0] += 1
                ins.then_inc(dve_chain, 1)
                dve.wait_ge(dve_chain, chain[0])

            dve.wait_ge(small_turned, 1)
            dve.tensor_copy(v1T[:, :], ps[:, 0, 0:P]).then_inc(small_kept, 1)
            dve.tensor_copy(v2T[:, :], ps[:, 0, P:P + V2_ROWS]).then_inc(small_kept, 1)
            dve.tensor_copy(peT[:, :], ps[:, 0, 256:256 + 2 * CL]).then_inc(small_kept, 1)
            dve.wait_ge(small_kept, 3)
            dve.wait_ge(cexp_ready, 1)
            step(dve.tensor_scalar(cexp, cexp, 1.0, None, ALU.add))
            step(dve.reciprocal(cexp, cexp))
            dve.tensor_tensor(scT[:, :, :], v2T[:, V2_C:V2_ROWS].rearrange("p (b k) -> p k b", k=KC),
                              cexp.rearrange("p (b k) -> p k b", k=KC), ALU.mult).then_inc(silu_ready, 1)
            lwp = lw[:, :, :].rearrange("p (a b) d -> p a b d", b=2)
            step(dve.tensor_tensor(lprod[:, :, :], lwp[:, :, 0, :], lwp[:, :, 1, :], ALU.mult))
            dve.tensor_reduce(lam[:, 0:2], lprod[:, :, :], AX.X, ALU.add).then_inc(lam_sums, 1)
            dve.wait_ge(lam_exp, 1)
            step(dve.tensor_tensor(lam[:, 4:5], lam[:, 3:4], lam[:, 2:3], ALU.subtract))
            dve.tensor_scalar(lam[:, 5:6], lam[:, 4:5], -LAM_INIT, None, ALU.add).then_inc(lam_ready, 1)
            for k in range(KC + 1):
                dve.wait_ge(x_turned, k + 1)
                bank = ps[:, 1 + k % 3, :]
                if k < KC:
                    ins = dve.tensor_copy(xT[:, k, 0:SEQ], bank)
                else:
                    ins = dve.tensor_copy(xT[:, :, SEQ:T], bank.rearrange("p (k c) -> p k c", k=KC))
                ins.then_inc(x_evac, 1)
            dve.wait_ge(x_evac, KC + 1)
            for v in range(2):
                dve.wait_ge(cmp_mm, v + 1)
                step(dve.tensor_copy(lam[:, 6 + v:7 + v], ps[:, 2 * v + 1, 0:1]))
                dve.tensor_scalar(hids[:, v, :], ps[:, 2 * v, 0:16 * NB_S], lam[:, 6 + v:7 + v], None, ALU.add).then_inc(cmp_exp, 1)
            for v in range(2):
                dve.wait_ge(act_chain, v + 1)
                step(dve.tensor_scalar(hids[:, v, :], hids[:, v, :], 1.0, None, ALU.add))
                step(dve.reciprocal(hids[:, v, :], hids[:, v, :]))
                dve.scalar_tensor_tensor(out=hids[:, v, :], in0=ps[:, 2 * v, 0:16 * NB_S], scalar=lam[:, 6 + v:7 + v],
                                         in1=hids[:, v, :], op0=ALU.add, op1=ALU.mult).then_inc(cmp_hid, 1)
            dve.wait_ge(cmp2_mm, 1)
            step(dve.tensor_copy(kccs[:, :, :], ps[:, 4, 0:GB * NS * NB_S].rearrange("p (g c) -> p g c", g=GB)))
            dve.tensor_copy(vccs[0:NS * NB_S, :, :], ps[0:NS * NB_S, 5, 0:GB * P].rearrange("p (g c) -> p g c", g=GB)
                            ).then_inc(cmp2_kept, 1)

            def adaln(layer):
                dve.sem_inc(ada_kept, WSLOTS)
                bias = v1T[:, V1_ADAB + 48 * layer:V1_ADAB + 48 * layer + 48]
                for n in range(12):
                    dve.wait_ge(ada_mm, 12 * layer + n + 1)
                    dve.tensor_tensor(mod[:, 4 * n:4 * n + 4, :],
                                      ps[:, n % WSLOTS, 0:64].rearrange("p (c b) -> p c b", c=4)[:, :, 0:9],
                                      bias[:, 4 * n:4 * n + 4].unsqueeze(2).to_broadcast([P, 4, 9]), ALU.add).then_inc(ada_kept, 1)
                dve.wait_ge(ada_kept, 16 * (layer + 1))

            def norm(idx, term, w):
                if term is not None:
                    step(dve.scalar_tensor_tensor(out=modA[:, :, :], in0=mod[:, (term + 1) * KC:(term + 2) * KC, :], scalar=1.0,
                                                  in1=w.unsqueeze(2).to_broadcast([P, KC, 9]), op0=ALU.add, op1=ALU.mult))
                dve.wait_ge(norm_std, idx + 1)
                step(dve.reciprocal(rstd[:, :], rstd[:, :]))
                for k in range(KC):
                    dve.tensor_tensor(hT[:, k, :], xT[:, k, :], rstd[:, :], ALU.mult).then_inc(norm_x, 1)
                dve.wait_ge(norm_x, (idx + 1) * KC)
                if term is not None:
                    for n in range(NS):
                        cols = hT[:, :, SEQ + DS * n:SEQ + DS * (n + 1)]
                        ins = dve.tensor_tensor(cols, cols, modA[:, :, 1 + n:2 + n].to_broadcast([P, KC, DS]), ALU.mult)
                    step(ins)
                    for n in range(NS):
                        cols = hT[:, :, SEQ + DS * n:SEQ + DS * (n + 1)]
                        ins = dve.tensor_tensor(cols, cols, mod[:, term * KC:(term + 1) * KC, 1 + n:2 + n].to_broadcast([P, KC, DS]), ALU.add)
                    ins.then_inc(h_sample, 1)

            adaln(0)
            dve.wait_ge(x_evac, KC + 1)
            norm(0, 0, v1T[:, V1_N1:V1_N1 + KC])

            def rope(src, dst, t, M, kind, blocks):
                cos, sin = rope_tab[kind]
                w = 32 if kind == "a" else 64
                n = blocks * 2 * w
                x = src[:, 0:n].rearrange("p (b h w) -> p b h w", b=blocks, h=2)
                t1 = rt1[0:M, 0:n].rearrange("p (b h w) -> p b h w", b=blocks, h=2)
                t2 = rt2[0:M, 0:n].rearrange("p (b h w) -> p b h w", b=blocks, h=2)
                c = cos[0:M, t, :].unsqueeze(1).to_broadcast([M, blocks, w])
                s = sin[0:M, t, :].unsqueeze(1).to_broadcast([M, blocks, w])
                dve.tensor_tensor(t1[:, :, 0, :], x[:, :, 0, :], c, ALU.mult)
                dve.tensor_tensor(t1[:, :, 1, :], x[:, :, 1, :], c, ALU.mult)
                dve.tensor_tensor(t2[:, :, 0, :], x[:, :, 1, :], s, ALU.mult)
                dve.tensor_tensor(t2[:, :, 1, :], x[:, :, 0, :], s, ALU.mult).then_inc(pj_dve, 1)
                return t1, t2

            uses = 0
            for u, (j, t) in enumerate(pj_units):
                if not has_dve[u]:
                    continue
                M, r = rows_of(t), use_of[u]
                dve.wait_ge(pj_mm, u + 1)
                kind, blocks = ("a", 8) if j in (QA, KA) else ("b", 4 if j == QB else 2)
                t1, t2 = rope(ps[0:M, u % 4, :], None, t, M, kind, blocks)
                tok_slot_free(dve, r)
                dve.wait_ge(pj_dve, r + 1)
                w = t1.shape[3]
                o = tok[0:M, r % 3, 0:blocks * 2 * w].rearrange("p (b h w) -> p b h w", b=blocks, h=2)
                step(dve.tensor_tensor(o[:, :, 0, :], t1[:, :, 0, :], t2[:, :, 0, :], ALU.subtract))
                dve.tensor_tensor(o[:, :, 1, :], t1[:, :, 1, :], t2[:, :, 1, :], ALU.add).then_inc(tok_ready, 1)
                dve.wait_ge(tok_ready, r + 1)
            for v in range(2):
                ins = dve.tensor_copy(cxp[:, v, 2 * SEQ:2 * SEQ + CL], peT[:, v * CL:(v + 1) * CL])
            ins.then_inc(pe_col, 1)
            dve.wait_ge(gate_exp, 2)
            dve.tensor_scalar(gates[:, 0:NT, :], gates[:, 0:NT, :], 1.0, None, ALU.add)
            step(dve.tensor_scalar(gates[0:TS, NT, :], gates[0:TS, NT, :], 1.0, None, ALU.add))
            dve.reciprocal(gates[:, 0:NT, :], gates[:, 0:NT, :])
            step(dve.reciprocal(gates[0:TS, NT, :], gates[0:TS, NT, :]))
            dve.wait_ge(turn_kept, len(turns))
            dve.tensor_tensor(gdiag[0:TS, :, :], gates[0:TS, NT, :].unsqueeze(2).to_broadcast([TS, 12, TS]),
                              ident[0:TS, 0:TS].unsqueeze(1).to_broadcast([TS, 12, TS]), ALU.mult).then_inc(gate_diag, 1)
            for v in range(2):
                dve.wait_ge(cmpp_mm, v + 1)
                step(dve.tensor_copy(lam[:, 6 + v:7 + v], ps[:, 1 + v, 64:65]))
                z = ps[:, 1 + v, 0:64].rearrange("p (g i) -> p g i", g=GB)[:, :, 0:NB_P]
                dve.tensor_scalar(hidp[:, v, 0:2 * NB_P].rearrange("p (g i) -> p g i", g=GB), z, lam[:, 6 + v:7 + v], None, ALU.add).then_inc(cmpp_exp, 1)
            for v in range(2):
                z = ps[:, 1 + v, 0:64].rearrange("p (g i) -> p g i", g=GB)[:, :, 0:NB_P]
                hv = hidp[:, v, 0:2 * NB_P]
                dve.wait_ge(act_chain, 3 + v)
                step(dve.tensor_scalar(hv, hv, 1.0, None, ALU.add))
                step(dve.reciprocal(hv, hv))
                hg = hv.rearrange("p (g i) -> p g i", g=GB)
                dve.scalar_tensor_tensor(out=hg, in0=z, scalar=lam[:, 6 + v:7 + v], in1=hg, op0=ALU.add, op1=ALU.mult).then_inc(cmpp_hid, 1)
            dve.wait_ge(cmpp2_mm, 1)
            dve.tensor_copy(kccp[:, :, :], ps[:, 3, 0:2 * NB_P].rearrange("p (g i) -> p g i", g=GB)).then_inc(cmpp2_kept, 1)
            dve.tensor_copy(vccp[0:NB_P, :, :], ps[0:NB_P, 3, P:3 * P].rearrange("p (g i) -> p g i", g=GB)).then_inc(cmpp2_kept, 1)
            dve.wait_ge(cs_mm, 1)
            step(dve.tensor_tensor(s1[:, :, :].rearrange("p (h t) i -> p h (t i)", h=HB),
                                   ps[:, 6, 0:16 * NB_P].rearrange("p (h c) -> p h c", h=HB),
                                   const("cmask").unsqueeze(1).to_broadcast([P, HB, NT * NB_P]), ALU.add))
            step(dve.tensor_reduce(r16[:, 0, :], s1[:, :, :], AX.X, ALU.max))
            dve.tensor_tensor(s1[:, :, :], s1[:, :, :], r16[:, 0, :].unsqueeze(2).to_broadcast([P, 16, NB_P]), ALU.subtract).then_inc(cs_sub, 1)
            dve.wait_ge(cs_exp, 1)
            step(dve.tensor_reduce(r16[:, 1, :], s1[:, :, :], AX.X, ALU.add))
            step(dve.reciprocal(r16[:, 1, :], r16[:, 1, :]))
            rr = r16[:, 1, :].rearrange("p (h t) -> p h t", h=HB)
            step(dve.tensor_tensor(rr, rr, gates[:, 0:NT, 0:12:3].rearrange("p t h -> p h t"), ALU.mult))
            step(dve.tensor_tensor(rr, rr, const("cvalid").unsqueeze(1).to_broadcast([P, HB, NT]), ALU.mult))
            dve.tensor_tensor(s1[:, :, :], s1[:, :, :], r16[:, 1, :].unsqueeze(2).to_broadcast([P, 16, NB_P]), ALU.mult).then_inc(cs_p, 1)

            def p_max(v):
                h, t, b = units[v]
                dve.wait_ge(s_mm, v + 1)
                if v >= 4:
                    dve.wait_ge(p_ready, v - 3)
                dve.tensor_reduce(nm[:, v % 4:v % 4 + 1], ps[:, v % 3, 0:(t + 1) * P], AX.X, ALU.max, negate=True).then_inc(nm_ready, 1)

            def p_factor(v):
                h, t, b = units[v]
                dve.wait_ge(p_ready, v + 1)
                step(dve.reciprocal(rsum[:, v % 4:v % 4 + 1], sums[:, v % 4:v % 4 + 1]))
                if v >= 3:
                    dve.wait_ge(pt_mm, group_of[v - 3] + 1)
                if h < HA:
                    f = lam[:, 5:6] if b else ones[:, 0:1]
                else:
                    c = 3 * (h - HA) + 1 + b
                    f = gates[:, t, c:c + 1]
                dve.tensor_scalar(diag[:, v % 3, :], ident[:, :], rsum[:, v % 4:v % 4 + 1], f, ALU.mult, ALU.mult).then_inc(diag_ready, 1)

            def o_keep(h):
                dve.wait_ge(pv_mm, head_groups[h])
                dve.tensor_copy(hT[:, h, 0:SEQ], ps[:, 5 + h % 2, :]).then_inc(o_kept, 1)

            due = {last_unit[h] + 6: h for h in range(HA + HB)}
            for v in range(len(units) + 8):
                if v < len(units):
                    p_max(v)
                if 1 <= v <= len(units):
                    p_factor(v - 1)
                if v in due:
                    o_keep(due[v])

            dve.tensor_copy(qbc[:, :, :].rearrange("p g (n c) -> p g n c", n=NS), qBs[:, :, :, 0:16]).then_inc(qbc_ready, 1)
            dve.wait_ge(ss_mm, 1)
            step(dve.tensor_tensor(sc[:, :, :], ps[:, 7, 0:GB * P].rearrange("p (g c) -> p g c", g=GB)[:, :, 0:NS * NB_S],
                                   const("smask").unsqueeze(1).to_broadcast([P, GB, NS * NB_S]), ALU.add))
            step(dve.tensor_reduce(r16[:, 0, 0:GB], sc[:, :, :], AX.X, ALU.max))
            dve.tensor_tensor(sc[:, :, :], sc[:, :, :], r16[:, 0, 0:GB].unsqueeze(2).to_broadcast([P, GB, NS * NB_S]), ALU.subtract).then_inc(ss_sub, 1)
            dve.wait_ge(ss_exp, 1)
            step(dve.tensor_reduce(r16[:, 1, 0:GB], sc[:, :, :], AX.X, ALU.add))
            step(dve.reciprocal(r16[:, 1, 0:GB], r16[:, 1, 0:GB]))
            dve.tensor_tensor(sc[:, :, :], sc[:, :, :], r16[:, 1, 0:GB].unsqueeze(2).to_broadcast([P, GB, NS * NB_S]), ALU.mult).then_inc(ss_p, 1)
            dve.wait_ge(ss_pv, 1)
            dve.tensor_copy(oc[:, :, :], ps[:, 7, 0:GB * P].rearrange("p (g c) -> p g c", g=GB)).then_inc(oc_kept, 1)

            def s_max(v):
                dve.wait_ge(ss2_mm, v + 1)
                if v >= 4:
                    dve.wait_ge(sp_ready, v - 3)
                dve.tensor_reduce(nm[:, v % 4:v % 4 + 1], ps[:, 3 + v % 2, 0:PAST + TS], AX.X, ALU.max, negate=True).then_inc(snm_ready, 1)

            def s_factor(v):
                dve.wait_ge(sp_ready, v + 1)
                step(dve.reciprocal(rsum[:, v % 4:v % 4 + 1], sums[:, v % 4:v % 4 + 1]))
                if v >= 3:
                    dve.wait_ge(spt_mm, v - 2)
                dve.tensor_scalar(diag[:, v % 3, :], ident[:, :], rsum[:, v % 4:v % 4 + 1], None, ALU.mult).then_inc(sdiag_ready, 1)

            def so_keep(v):
                dve.wait_ge(spv_mm, v + 1)
                dve.tensor_copy((osb if v % 2 else osa)[:, v // 2, :, :],
                                ps[:, 6 + v % 2, 0:P].rearrange("p (s c) -> p s c", s=4)[:, :, 0:16]).then_inc(so_kept, 1)

            for v in range(2 * NS + 3):
                if v < 2 * NS:
                    s_max(v)
                    s_factor(v)
                if v >= 3:
                    so_keep(v - 3)
            dve.wait_ge(so_kept, 2 * NS)
            dve.wait_ge(gb_kept, 1)
            for h in range(HA):
                dve.scalar_tensor_tensor(out=hT[:, h, SEQ:T].rearrange("p (n s) -> p n s", n=NS), in0=osa[:, :, h, DS:2 * DS],
                                         scalar=lam[:, 5:6], in1=osa[:, :, h, 0:DS], op0=ALU.mult, op1=ALU.add)
            for h in range(HB):
                g, r = h // 2, h % 2
                parts = [oc[:, g, :].rearrange("p (n r s) -> p n r s", n=NS, r=2)[:, :, r, :],
                         osb[:, :, g, DS * r:DS * r + DS], osb[:, :, 2 + g, DS * r:DS * r + DS]]
                for b, part in enumerate(parts):
                    ins = dve.tensor_tensor(part, part, gb[:, 3 * h + b, :].rearrange("p (n s) -> p n s", n=NS), ALU.mult)
            step(ins)
            for h in range(HB):
                g, r = h // 2, h % 2
                ins = dve.tensor_tensor(osb[:, :, g, DS * r:DS * r + DS], osb[:, :, g, DS * r:DS * r + DS],
                                        osb[:, :, 2 + g, DS * r:DS * r + DS], ALU.add)
            step(ins)
            for h in range(HB):
                g, r = h // 2, h % 2
                ins = dve.tensor_tensor(hT[:, HA + h, SEQ:T].rearrange("p (n s) -> p n s", n=NS),
                                        oc[:, g, :].rearrange("p (n r s) -> p n r s", n=NS, r=2)[:, :, r, :],
                                        osb[:, :, g, DS * r:DS * r + DS], ALU.add)
            ins.then_inc(comb_ready, 1)
            step(dve.tensor_scalar(lam[:, 4:5], v2T[:, V2_SUB:V2_SUB + 1], 1.0 - LAM_INIT, None, ALU.mult))
            dve.wait_ge(sub_std, 1)
            for h in range(HA):
                ins = dve.reciprocal(sq[:, h, :], sq[:, h, :])
            step(ins)
            for h in range(HA):
                ins = dve.scalar_tensor_tensor(out=hT[:, h, :], in0=hT[:, h, :], scalar=lam[:, 4:5], in1=sq[:, h, :],
                                               op0=ALU.mult, op1=ALU.mult)
            ins.then_inc(mix_ready, 1)

            def residual(m, main, side, term):
                g = mod[:, term * KC + m, :]
                dve.scalar_tensor_tensor(out=xT[:, m, 0:SEQ], in0=main, scalar=g[:, 0:1], in1=xT[:, m, 0:SEQ], op0=ALU.mult, op1=ALU.add)
                t8 = xs_tmp[:, :].rearrange("p (n s) -> p n s", n=NS)
                step(dve.tensor_tensor(t8, side.rearrange("p (n s) -> p n s", n=NS), g[:, 1:9].unsqueeze(2).to_broadcast([P, NS, DS]), ALU.mult))
                return dve.tensor_tensor(xT[:, m, SEQ:T], xT[:, m, SEQ:T], xs_tmp[:, :], ALU.add)

            def out_projection(layer):
                for m in range(KC):
                    dve.wait_ge(out_mm, layer * KC + m + 1)
                    residual(m, ps[:, m % 4, :], ps[:, 4 + m % 4, 0:TS], 2).then_inc(resid_kept, 1)
                    dve.wait_ge(resid_kept, layer * KC + m + 1)
                dve.sem_inc(x_ready, 1)

            def mlp(layer):
                dve.sem_inc(relu_free, 2)
                dve.sem_inc(down_free, 2)
                if layer == 0:
                    dve.wait_ge(v_stored, 16 * V_STORES)
                with dve.Fori(0, DFF // P // 4) as i:
                    for c in range(4):
                        dve.wait_ge(up_free, i * 4 + (c + 5 + (DFF // P + 4) * layer))
                        dve.tensor_tensor(hid[:, bass.ds(i * 4 + c, 1), :], relu[:, c % 2:c % 2 + 1, :], relu[:, c % 2:c % 2 + 1, :], ALU.mult
                                          ).then_inc(relu_free, 1)
                for pair in range(4):
                    dve.wait_ge(down_mm, 8 * layer + 2 * pair + 2)
                    for m in range(2):
                        q = pair % 2
                        ins = residual(2 * pair + m, ps[:, 3 * q + m, :], ps[:, 3 * q + 2, m * TS:(m + 1) * TS], 5)
                        if m == 0:
                            step(ins)
                    ins.then_inc(down_free, 1)
                    dve.wait_ge(down_free, 6 * layer + 3 + pair)
                dve.sem_inc(x_ready, 1)

            out_projection(0)
            norm(1, 3, v1T[:, V1_N2:V1_N2 + KC])
            mlp(0)

            adaln(1)
            norm(2, 0, v1T[:, V1_N1 + KC:V1_N1 + 2 * KC])
            for h in range(HC):
                dve.wait_ge(gz_mm, h + 1)
                bg = v2T[:, V2_BG + h:V2_BG + h + 1]
                for src, lo, hi in ((ps[:, h, :], 0, SEQ), (ps[:, 4 + h, 0:TS], SEQ, T)):
                    dve.tensor_scalar(gtmp[:, h, lo:hi], src, bg, None, ALU.add)
                    dve.tensor_scalar(gbt[:, h, lo:hi], src, bg, 0.0, ALU.add, ALU.min).then_inc(gz_abs, 1)
            dve.wait_ge(gz_abs, 2 * HC)
            dve.wait_ge(gz_ln, 1)
            step(dve.tensor_tensor(gtmp[:, :, :], gbt[:, :, :], gtmp[:, :, :], ALU.subtract))
            for h in range(HC):
                dve.tensor_tensor_scan(gbt[:, h, :], const("keep"), gtmp[:, h, :], 0.0, ALU.mult, ALU.add).then_inc(b_ready, 1)
            dve.wait_ge(b_ready, HC)
            for c in range(KC):
                dve.wait_ge(r_exp, c + 1)
                step(dve.tensor_scalar(er[:, c % 2, :], er[:, c % 2, :], 1.0, None, ALU.add))
                step(dve.reciprocal(er[:, c % 2, :], er[:, c % 2, :]))
                dve.tensor_tensor(gr[:, c, :], gr[:, c, :], er[:, c % 2, :], ALU.mult).then_inc(r_ready, 1)
            dve.wait_ge(r_ready, KC)
            step(dve.memset(gatt[:, :, :, :], 0.0))

            def g_prepare(h):
                b, q, k = gbt[:, h, :], gq[:, h, :], gk[:, h, :]
                bp = b[:, 0:SEQ].rearrange("p (c t) -> p c t", c=NCH)
                qp = q[:, 0:SEQ].rearrange("p (c t) -> p c t", c=NCH)
                kk = k[:, 0:SEQ].rearrange("p (c t) -> p c t", c=NCH)
                bs = b[:, SEQ:T].rearrange("p (n t) -> p n t", n=NS)
                if h:
                    dve.wait_ge(att_mm, h)
                    dve.wait_ge(kd_turned, h)
                for i in range(1, 4):
                    start = bp[:, :, i * SUB - 1:i * SUB]
                    n = (i + 1) * SUB
                    dve.tensor_tensor(gqd[:, :, (i - 1) * SUB:i * SUB], bp[:, :, i * SUB:n], start.to_broadcast([P, NCH, SUB]), ALU.subtract)
                    dve.tensor_tensor(gkp[i], start.to_broadcast([P, NCH, n]), bp[:, :, 0:n], ALU.subtract)
                dve.tensor_tensor(gkd[:, 0:SEQ].rearrange("p (c t) -> p c t", c=NCH), bp[:, :, GCH - 1:GCH].to_broadcast([P, NCH, GCH]), bp, ALU.subtract)
                dve.tensor_tensor(gkd[:, SEQ:T].rearrange("p (n t) -> p n t", n=NS), bs[:, :, DS - 1:DS].to_broadcast([P, NS, DS]), bs, ALU.subtract
                                  ).then_inc(gsub_ready, 1)
                dve.wait_ge(eb_ready, 2 * h + 2)
                if h >= 2:
                    dve.wait_ge(os_mm, h - 1)
                dve.tensor_tensor(gqe[:, h % 2, :], q, geb, ALU.mult)
                dve.tensor_copy(gebl[:, h % 2, 0:NCH], geb[:, GCH - 1:SEQ:GCH])
                dve.tensor_copy(gebl[:, h % 2, NCH:NCH + NS], geb[:, SEQ + DS - 1:T:DS])
                dve.tensor_tensor(gkp[0], gkp[0], kk[:, :, 0:SUB], ALU.mult)
                dve.tensor_tensor(gkp_s, gkp_s, k[:, SEQ:T], ALU.mult)
                dve.wait_ge(ex_ready, h + 1)
                dve.tensor_tensor(gqd, gqd, qp[:, :, SUB:GCH], ALU.mult)
                for i in range(1, 4):
                    dve.tensor_tensor(gkp[i], gkp[i], kk[:, :, 0:(i + 1) * SUB], ALU.mult)
                dve.tensor_tensor(gkd, gkd, k, ALU.mult).then_inc(prep_ready, 1)
                dve.wait_ge(prep_ready, h + 1)

            def g_scores(h):
                dve.wait_ge(att_mm, h + 1)
                if h >= 2:
                    dve.wait_ge(os_mm, h - 1)
                if h:
                    dve.wait_ge(st_mm, 8 * h)
                step(dve.tensor_copy(gkdT[0:TS, h % 2, NT, :], ps[0:TS, 0, 384:512]))
                tri = const("tri")
                for i in range(4):
                    m = (i + 1) * SUB
                    cols = slice(i * SUB, m)
                    for lo in ((0, 64) if i < 3 else (0,)):
                        r = slice(lo, lo + m) if i < 3 else slice(0, P)
                        n = m if i < 3 else P
                        dve.tensor_tensor(gatt[r, h % 2, 0:4, cols], ps[r, 0, 0:4 * GCH].rearrange("p (t c) -> p t c", t=4)[:, :, cols],
                                          tri[r, cols].unsqueeze(1).to_broadcast([n, 4, SUB]), ALU.mult)
                dve.tensor_tensor(gatt[0:TS, h % 2, 4, :], ps[0:TS, 0, 4 * GCH:5 * GCH], const("stri")[0:TS, :], ALU.mult)
                dve.tensor_tensor(gkdm[0:TS, :, :], gkdT[0:TS, h % 2, NT, :].unsqueeze(1).to_broadcast([TS, NS, P]),
                                  const("rowof")[0:TS, :].unsqueeze(2).to_broadcast([TS, NS, P]), ALU.mult).then_inc(att_kept, 1)

            def g_chain(h):
                for p in range(4):
                    dve.wait_ge(st_mm, 8 * h + p + 1)
                    for w in range(2):
                        c = 2 * p + w
                        kv = ps[:, 5 + (8 * h + p) % 3, w * DVC:(w + 1) * DVC]
                        if NCH * h + c + 1 >= 4:
                            last = NCH * h + c + 1 - 4
                            dve.wait_ge(go_mm, last + 1)
                        if c + 1 == 4 and h:
                            dve.wait_ge(gs_stored, 16 * h)
                        if c == 0:
                            ins = dve.tensor_copy(sp_[:, 1, :], kv)
                        else:
                            ins = dve.scalar_tensor_tensor(out=sp_[:, (c + 1) % 4, :], in0=sp_[:, c % 4, :], scalar=gebl[:, h % 2, c:c + 1],
                                                           in1=kv, op0=ALU.mult, op1=ALU.add)
                        ins.then_inc(s_ready, 1)
                        dve.wait_ge(s_ready, NCH * h + c + 1)
                    dve.sem_inc(st_kept, 1)

            def g_sample_states(h):
                dve.wait_ge(os_mm, h + 1)
                for p in range(4, 8):
                    dve.wait_ge(st_mm, 8 * h + p + 1)
                    for w in range(2):
                        n = 2 * (p - 4) + w
                        ins = dve.scalar_tensor_tensor(out=s0[:, h % 2, n, :], in0=s0[:, h % 2, n, :], scalar=gebl[:, h % 2, NCH + n:NCH + n + 1],
                                                       in1=ps[:, 5 + (8 * h + p) % 3, w * DVC:(w + 1) * DVC], op0=ALU.mult, op1=ALU.add)
                    ins.then_inc(st_kept, 1)

            g_prepare(0)
            g_scores(0)
            for h in range(HC):
                if h + 1 < HC:
                    g_prepare(h + 1)
                g_chain(h)
                g_sample_states(h)
                if h + 1 < HC:
                    g_scores(h + 1)
            dve.wait_ge(gn_std, 1)
            for h in range(HC):
                ins = dve.reciprocal(gstd[:, h, :], gstd[:, h, :])
            step(ins)
            for k in range(KC):
                ins = dve.scalar_tensor_tensor(out=hT[:, k, :], in0=hT[:, k, :], scalar=v2T[:, V2_GLAN + k % 2:V2_GLAN + k % 2 + 1],
                                               in1=gstd[:, k // 2, :], op0=ALU.mult, op1=ALU.mult)
            step(ins)
            for k in range(KC):
                ins = dve.tensor_tensor(hT[:, k, :], hT[:, k, :], gr[:, k, :], ALU.mult)
            ins.then_inc(gmix_ready, 1)
            out_projection(1)
            norm(3, 3, v1T[:, V1_N2 + KC:V1_N2 + 2 * KC])
            mlp(1)
            norm(4, None, None)


_INS = ["x_prompt", "x_sample", "c_prompt", "c_sample", "cache_diff_k", "cache_diff_v", "cache_cmp_kv", "cache_sel_kv",
        "state_win_kv", "state_gla", "page_table", "norm1_w", "norm2_w", "ada_w", "ada_b", "even_w_in", "even_w_out",
        "diff_lambda_w", "diff_subln_w", "cmp_pe", "cmp_w1", "cmp_w2", "gla_w_in", "gla_w_gate", "gla_b_gate",
        "gla_norm_w", "gla_w_out", "mlp_w1", "mlp_w2", "final_norm_w"]
_OUTS = [(1, SEQ, D), (NS, DS, D), (1, 1, SEQ, HA, 2, DKA), (1, 1, SEQ, HA, 2 * DKA), (1, 1, SEQ, 2, GB, DHB),
         (1, 1, SEQ, 2, GB, DHB), (1, 1, SEQ, 2, GB, DHB), (1, 1, HC, DKC, DVC), (1, NS, DS, HA, 2, DKA),
         (1, NS, DS, HA, 2 * DKA), (1, NS, DS, 2, GB, DHB), (1, NS, DS, 2, GB, DHB), (1, NS, PAST, 2, GB, DHB),
         (1, NS, HC, DKC, DVC)]


def kernel(**inputs):
    import concourse.bacc as _bacc
    from concourse.bass_utils import run_bass_kernel_spmd as _run

    nc = _bacc.Bacc("TRN2", target_bir_lowering=False, num_devices=1)
    arrays, aps = {}, {}
    const_f32, const_bf16, const_cols = shape_constants()
    given = {name: np.ascontiguousarray(inputs[name]) for name in _INS}
    given["const_f32"], given["const_bf16"] = const_f32, const_bf16
    for name, v in given.items():
        arrays[f"in_{name}"] = v
        aps[name] = nc.dram_tensor(f"in_{name}", v.shape, mybir.dt.from_np(v.dtype), kind="ExternalInput").ap()
    outs = [nc.dram_tensor(f"out_{i}", s, F32, kind="ExternalOutput").ap() for i, s in enumerate(_OUTS)]
    decoder_program(nc, aps, outs, const_cols)
    r = _run(nc, [arrays], core_ids=[0])
    return tuple(r.results[0][f"out_{i}"] for i in range(len(_OUTS)))
```

```python
from contextlib import ExitStack
import math

import numpy as np
import concourse.bass as bass
from concourse import mybir

P = 128
D = 1024
KC = D // P
SEQ = 512
NS, DS = 8, 8
TS = NS * DS
T = SEQ + TS
NT = SEQ // P
PAST, PAGE = 256, 128
NPAGE = PAST // PAGE
HA, DKA = 4, 64
HB, GB, DHB = 4, 2, 128
CL, CS = 32, 16
SEL_BLOCK, TOP_N, WINDOW = 64, 16, 512
HC, DKC, DVC = 4, 128, 256
RANK, TAU, GCH = 16, 16.0, 64
SUB = 16
NCH = SEQ // GCH
DFF = 4096
EPS = 1e-6
LAM_INIT = 0.8 - 0.6 * math.exp(-0.3 * 0)
NB_P = (SEQ - CL) // CS + 1
NB_S = (PAST + DS - CL) // CS + 1
assert TOP_N * SEL_BLOCK >= SEQ and TOP_N * SEL_BLOCK >= PAST + DS
assert WINDOW >= SEQ and WINDOW >= PAST + DS and (NB_S - 1) * CS + CL <= PAST
WSLOTS, SLOT = 4, 4096
NEG = -1e30

F32, BF16, I32 = mybir.dt.float32, mybir.dt.bfloat16, mybir.dt.int32
F32R = mybir.dt.float32r
ALU, ACT, AX = mybir.AluOpType, mybir.ActivationFunctionType, mybir.AxisListType

V1_N1, V1_N2, V1_ADAB = 0, 16, 32
V2_FIN, V2_SUB, V2_GLAN, V2_BG, V2_C = 0, 8, 9, 11, 15
V2_ROWS = V2_C + 9 * KC


def shape_constants():
    cols, at = {}, 0
    parts = []

    def put(name, a):
        nonlocal at
        a = np.asarray(a, np.float32).reshape(P, -1)
        cols[name] = (at, a.shape[1])
        at += a.shape[1]
        parts.append(a)

    put("ident", np.eye(P))
    put("ones", np.ones((P, P)))
    put("fold", np.tile(np.eye(32)[:, 0:9], (4, 1)))
    put("eps", np.full((P, 1), EPS))
    pos = np.concatenate([np.arange(SEQ), np.tile(PAST + np.arange(DS), NS), np.zeros(P - TS)]).astype(np.float32)
    for name, d in (("a", DKA), ("b", DHB)):
        inv = (np.float32(10000.0) ** (-np.arange(0, d, 2, dtype=np.float32) / np.float32(d))).astype(np.float32)
        ang = (pos[:, None] * inv[None, :]).reshape(NT + 1, P, d // 2).transpose(1, 0, 2)
        put("cos" + name, np.cos(ang.astype(np.float64)))
        put("sin" + name, np.sin(ang.astype(np.float64)))
    t = np.arange(SEQ).reshape(NT, P).T
    end = CS * np.arange(NB_P) + CL - 1
    put("cmask", np.where(end[None, None, :] <= t[:, :, None], 0.0, NEG))
    put("cvalid", (t >= CL - 1).astype(np.float32))
    rows = np.arange(P) // (2 * DS)
    put("smask", np.where(np.arange(NS * NB_S)[None, :] // NB_S == rows[:, None], 0.0, NEG))
    j, i = np.arange(P)[:, None], np.arange(GCH)[None, :]
    put("tri", (j % GCH <= i).astype(np.float32))
    put("stri", ((j // DS == i // DS) & (j <= i) & (j < TS)).astype(np.float32))
    keep = np.ones(T)
    keep[0:SEQ:GCH] = 0
    keep[SEQ::DS] = 0
    put("keep", np.broadcast_to(keep, (P, T)))
    put("rowof", (np.arange(P)[:, None] // DS == np.arange(NS)[None, :]))
    f32 = np.concatenate(parts, 1)

    q, k = np.arange(P)[:, None], np.arange(P)[None, :]
    causal = np.where(k <= q, 0.0, NEG)
    c = np.arange(TS)[None, None, :]
    n = np.arange(NS)[None, :, None]
    new = np.where((c // DS == n) & (c % DS <= (np.arange(P) % DS)[:, None, None]), 0.0, NEG)
    bf = np.concatenate([np.eye(P), causal, new.reshape(P, NS * TS)], 1).astype(mybir.dt.np(BF16))
    return np.ascontiguousarray(f32), np.ascontiguousarray(bf), cols


def decoder_program(nc, a, out, const_cols):
    ctx = ExitStack()
    with ctx, nc.allow_non_contiguous_dma(reason="small vectors, gate columns"):
        def sb(name, shape, dt=F32):
            return ctx.enter_context(nc.sbuf_tensor(name, shape, dt))

        def sem(name):
            return ctx.enter_context(nc.semaphore(name))

        ARENA = 21560
        ps = ctx.enter_context(nc.psum_tensor("ps", [P, 8, 512], F32))
        shapes = (("wring", [P, WSLOTS, SLOT]),
                  ("hT", [P, KC, T]),
                  ("arena", [P, ARENA]))
        with ExitStack() as first:
            wring, hT, arena = [first.enter_context(nc.sbuf_tensor(name, shape, F32)) for name, shape in shapes]
        wring_r, hT_r, arena_r = [sb(name + "_r", shape, F32R) for name, shape in shapes]
        xT = sb("xT", [P, KC, T])
        cf = sb("cf", [P, a["const_f32"].shape[1]])
        cb = sb("cb", [P, a["const_bf16"].shape[1]], BF16)
        mod = sb("mod", [P, 48, 9])
        v1T = sb("v1T", [P, P])
        v2T = sb("v2T", [P, V2_ROWS])
        peT = sb("peT", [P, 2 * CL])
        scT = sb("scT", [P, KC, 9])
        modA = sb("modA", [P, KC, 9])
        rstd = sb("rstd", [P, T])
        gates = sb("gates", [P, NT + 1, 12])
        gcols = sb("gcols", [P, KC, 16])
        lam = sb("lam", [P, 8])
        r16 = sb("r16", [P, 2, 16])
        nm = sb("nm", [P, 4])
        sums = sb("sums", [P, 4])
        rsum = sb("rsum", [P, 4])
        xs_tmp = sb("xs_tmp", [P, TS])
        hidp = sb("hidp", [P, 2, 2 * NB_P + 1])
        hids = sb("hids", [P, 2, GB * NS * NB_S])
        kccs = sb("kccs", [P, GB, NS * NB_S])
        vccs = sb("vccs", [P, GB, P])
        kccp = sb("kccp", [P, GB, NB_P])
        vccp = sb("vccp", [P, GB, P])
        cw2 = sb("cw2", [P, 2, P])
        pagesb = sb("pagesb", [1, NS * NPAGE], I32)

        class Carve:

            def __init__(self, at=0):
                self.at = at

            def __call__(self, *dims):
                n = int(np.prod(dims))
                v = arena[:, self.at:self.at + n]
                self.at += n
                assert self.at <= ARENA, self.at
                if len(dims) == 2:
                    v = v.rearrange("p (a b) -> p a b", a=dims[0])
                elif len(dims) == 3:
                    v = v.rearrange("p (a b c) -> p a b c", a=dims[0], b=dims[1])
                elif len(dims) == 4:
                    v = v.rearrange("p (a b c d) -> p a b c d", a=dims[0], b=dims[1], c=dims[2])
                return v

        def const(name, *dims):
            at, n = const_cols[name]
            v = cf[:, at:at + n]
            if len(dims) == 2:
                v = v.rearrange("p (a b) -> p a b", a=dims[0])
            return v

        ident, ones, eps = const("ident"), const("ones"), const("eps")
        rope_tab = {"a": (const("cosa", NT + 1, 32), const("sina", NT + 1, 32)),
                    "b": (const("cosb", NT + 1, 64), const("sinb", NT + 1, 64))}
        identb, causalb = cb[:, 0:P], cb[:, P:2 * P]
        newmask = cb[:, 2 * P:2 * P + NS * TS].rearrange("p (n c) -> p n c", n=NS)

        c0 = Carve()
        h_flat = hT[:, :, :].rearrange("p a b -> p (a b)")
        x_in = h_flat[:, 0:NT * D].rearrange("p (t d) -> p t d", t=NT)
        rows = h_flat[:, NT * D:NT * D + 3 * P].rearrange("p (a b) -> p a b", a=3)
        lprod = h_flat[:, NT * D + 3 * P:NT * D + 4 * P].rearrange("p (a b) -> p a b", a=2)
        lw = rstd[:, 0:4 * DKA].rearrange("p (a b) -> p a b", a=4)
        cexp = rstd[:, 4 * DKA:4 * DKA + 9 * KC]
        xs_in = c0(D)
        ctok = c0(NS * NPAGE, 512)
        cxs = c0(GB * NS, PAST)
        cw1 = c0(2, SLOT)
        c1 = Carve()
        qaT = c1(HA, SEQ)
        qbT = c1(HB, SEQ)
        kaT = c1(HA, T)
        skT = c1(GB, T)
        wkT = c1(GB, T)
        va = c1(NT + 1, 512)
        vs = c1(NT + 1, 256)
        vw = c1(NT + 1, 256)
        qAs = c1(NS, HA, 32)
        qBs = c1(GB, NS, 32)
        mixer_scratch = c1.at
        cxp = c1(2, 2 * SEQ + CL)
        tok = c1(3, 512)
        rt1 = c1(512)
        rt2 = c1(512)
        c2 = Carve(mixer_scratch)
        pbuf = c2(3, 512)
        diag = c2(3, P)
        ptb = Carve(mixer_scratch + 2 * (2 * SEQ + CL))(3, 512)
        c2 = Carve(mixer_scratch + 2 * (2 * SEQ + CL) + 3 * 512)
        gdiag = c2(12, TS)
        ptsc = c2(GB, P)
        gb = c2(12, TS)
        s1 = c2(16, NB_P)
        sc = c2(GB, NS * NB_S)
        c2 = Carve(0)
        kts = c2(2, 4, PAST)
        sq = Carve(0)(HA, T)
        c2 = Carve(HA * T)
        oc = c2(GB, P)
        osa = c2(NS, 4, 16)
        osb = c2(NS, 4, 16)
        qbc = c2(GB, P)
        wscr = wring[:, 0:2, :].rearrange("p a b -> p (a b)")
        ptc = wscr[:, 0:4 * 512].rearrange("p (h t) -> p h t", h=HB)
        kvb = [wring[:, i // 2, i % 2 * 2048:(i % 2 + 1) * 2048].rearrange("p (b c) -> p b c", b=4) for i in (4, 5, 6, 7, 1, 2, 3, 0)]
        KV_PLACES = 8
        gscr = wring[:, 2:4, :].rearrange("p a b -> p (a b)")
        cg = Carve()
        gq, gk, gbt = cg(HC, T), cg(HC, T), cg(HC, T)
        gr = cg(KC, T)
        gv = cg(NT + 1, D)
        gla_scratch = cg.at
        gtmp = cg(HC, T)
        glT = cg(T)
        er = cg(2, T)
        wg = Carve(21040)(HC * P)
        cg = Carve(gla_scratch)
        geb = cg(T)
        gkd = cg(T)
        gqd = cg(NCH, 3 * SUB)
        gqe = cg(2, T)
        gatt = cg(2, 5, GCH)
        gkdm = cg(NS, P)
        gebl = cg(2, NCH + NS)
        s0 = gscr[:, 0:4096].rearrange("p (r n e) -> p r n e", r=2, n=NS)
        gsq = Carve(0)(KC, T)
        gstd = Carve(KC * T)(HC, T)
        fin = Carve(0)(NT + 1, D)
        sp_ = gscr[:, 4096:5120].rearrange("p (r e) -> p r e", r=4)
        gkdT = gscr[:, 5120:6400].rearrange("p (r t d) -> p r t d", r=2, t=NT + 1)
        kp_at = [6400 + NCH * SUB * i * (i + 1) // 2 for i in range(5)]
        gkp = [gscr[:, kp_at[i]:kp_at[i + 1]].rearrange("p (c j) -> p c j", c=NCH) for i in range(4)]
        gkp_s = gscr[:, kp_at[4]:kp_at[4] + TS]
        hid_hi = arena_r[:, 0:KC * T].rearrange("p (k t) -> p k t", k=KC)
        hid_lo = arena_r[:, KC * T:2 * KC * T].rearrange("p (k t) -> p k t", k=KC)
        hid_new = arena[:, 2 * KC * T:(2 * KC + 2) * T].rearrange("p (c t) -> p c t", c=2)
        mixed = arena[:, 0:KC * T].rearrange("p (k t) -> p k t", k=KC)
        norm_squares = [hT, mixed, hT, mixed, hT]
        ada_row = arena[:, 0:2 * 512].rearrange("p (r c) -> p r c", r=2)
        xs_new = arena[:, (2 * KC + 2) * T:(2 * KC + 2) * T + 2 * TS].rearrange("p (c t) -> p c t", c=2)
        h_hi = arena_r[:, 16384:16384 + KC * T].rearrange("p (k t) -> p k t", k=KC)
        HALF = T // 2
        MLP_UNITS = 2 * DFF // 256
        QUARTER = 8

        def unit(n):
            half = SLOT // 2
            raw, high, low = wring[:, n % WSLOTS, 0:half], wring_r[:, n % WSLOTS, half:SLOT], wring_r[:, n % WSLOTS, 0:half]
            return [v.rearrange("p (k c) -> p k c", k=KC) for v in (raw, high, low)]

        small_loaded = sem("small_loaded")
        x_loaded = sem("x_loaded")
        pages_loaded = sem("pages_loaded")
        cmpw_loaded = sem("cmpw_loaded")
        ctok_loaded = sem("ctok_loaded")
        gcols_loaded = sem("gcols_loaded")
        w_ready = [sem(f"w_ready{i}") for i in range(WSLOTS)]
        small_turned = sem("small_turned")
        small_kept = sem("small_kept")
        cexp_ready = sem("cexp_ready")
        silu_ready = sem("silu_ready")
        lam_sums = sem("lam_sums")
        lam_exp = sem("lam_exp")
        lam_ready = sem("lam_ready")
        x_turned = sem("x_turned")
        x_evac = sem("x_evac")
        ctok_turned = sem("ctok_turned")
        cxs_ready = sem("cxs_ready")
        cmp_mm = sem("cmp_mm")
        cmp_exp = sem("cmp_exp")
        cmp_hid = sem("cmp_hid")
        cmp2_mm = sem("cmp2_mm")
        cmp2_kept = sem("cmp2_kept")
        ada_mm = sem("ada_mm")
        ada_kept = sem("ada_kept")
        ada_rows = sem("ada_rows")
        ada_turned = sem("ada_turned")
        norm_sq = sem("norm_sq")
        norm_sum = sem("norm_sum")
        norm_std = sem("norm_std")
        norm_x = sem("norm_x")
        h_prompt = sem("h_prompt")
        h_sample = sem("h_sample")
        pj_mm = sem("pj_mm")
        pj_dve = sem("pj_dve")
        pj_act = sem("pj_act")
        tok_ready = sem("tok_ready")
        tok_stored = [sem(f"tok_stored{i}") for i in range(3)]
        tok_turned = sem("tok_turned")
        turn_kept = sem("turn_kept")
        gate_mm = sem("gate_mm")
        gate_exp = sem("gate_exp")
        scratch_zero = sem("scratch_zero")
        out_stored = sem("out_stored")
        pe_col = sem("pe_col")
        cmpp_mm = sem("cmpp_mm")
        cmpp_exp = sem("cmpp_exp")
        cmpp_hid = sem("cmpp_hid")
        cmpp2_mm = sem("cmpp2_mm")
        cmpp2_kept = sem("cmpp2_kept")
        gate_diag = sem("gate_diag")
        gb_mm = sem("gb_mm")
        gb_kept = sem("gb_kept")
        cs_mm = sem("cs_mm")
        cs_sub = sem("cs_sub")
        cs_exp = sem("cs_exp")
        cs_p = sem("cs_p")
        cs_turned = sem("cs_turned")
        ptc_kept = sem("ptc_kept")
        s_mm = sem("s_mm")
        nm_ready = sem("nm_ready")
        p_ready = sem("p_ready")
        diag_ready = sem("diag_ready")
        pt_mm = sem("pt_mm")
        pt_kept = sem("pt_kept")
        pv_mm = sem("pv_mm")
        o_kept = sem("o_kept")
        ss_mm = sem("ss_mm")
        qbc_ready = sem("qbc_ready")
        ss_sub = sem("ss_sub")
        ss_exp = sem("ss_exp")
        ss_p = sem("ss_p")
        ss_turned = sem("ss_turned")
        ss_kept = sem("ss_kept")
        ss_pv = sem("ss_pv")
        oc_kept = sem("oc_kept")
        kt_mm = sem("kt_mm")
        kt_kept = sem("kt_kept")
        ss2_mm = sem("ss2_mm")
        snm_ready = sem("snm_ready")
        sp_ready = sem("sp_ready")
        sdiag_ready = sem("sdiag_ready")
        spt_mm = sem("spt_mm")
        spt_kept = sem("spt_kept")
        spv_mm = sem("spv_mm")
        so_kept = sem("so_kept")
        comb_ready = sem("comb_ready")
        sub_sq = sem("sub_sq")
        sub_sum = sem("sub_sum")
        sub_std = sem("sub_std")
        mix_ready = sem("mix_ready")
        out_mm = sem("out_mm")
        resid_kept = sem("resid_kept")
        up_mm = sem("up_mm")
        up_free = sem("up_free")
        down_mm = sem("down_mm")
        down_free = sem("down_free")
        w_high = sem("w_high")
        w_split = sem("w_split")
        h_high = sem("h_high")
        h_split = sem("h_split")
        hid_high = sem("hid_high")
        hid_ready = sem("hid_ready")
        mlp_added = sem("mlp_added")
        v_stored = sem("v_stored")
        kv_loaded = [sem(f"kv_loaded{i}") for i in range(4)]
        gl_mm = sem("gl_mm")
        gl_kept = sem("gl_kept")
        gz_mm = sem("gz_mm")
        gz_abs = sem("gz_abs")
        gz_ln = sem("gz_ln")
        b_ready = sem("b_ready")
        gin_mm = sem("gin_mm")
        gin_kept = sem("gin_kept")
        r_exp = sem("r_exp")
        r_ready = sem("r_ready")
        eb_ready = sem("eb_ready")
        gsub_ready = sem("gsub_ready")
        ex_ready = sem("ex_ready")
        prep_ready = sem("prep_ready")
        kd_turned = sem("kd_turned")
        kd_kept = sem("kd_kept")
        att_mm = sem("att_mm")
        att_kept = sem("att_kept")
        st_mm = sem("st_mm")
        st_first = sem("st_first")
        gkdm_ready = sem("gkdm_ready")
        st_kept = sem("st_kept")
        s_ready = sem("s_ready")
        go_mm = sem("go_mm")
        os_mm = sem("os_mm")
        go_kept = sem("go_kept")
        gs_stored = sem("gs_stored")
        gn_sq = sem("gn_sq")
        gn_sum = sem("gn_sum")
        gn_std = sem("gn_std")
        gmix_ready = sem("gmix_ready")
        wg_loaded = sem("wg_loaded")
        fin_mm = sem("fin_mm")
        fin_kept = sem("fin_kept")
        s0_loaded = [sem(f"s0_loaded{i}") for i in range(2)]
        s0_stored = [sem(f"s0_stored{i}") for i in range(2)]
        fin_stored = sem("fin_stored")
        dve_chain = sem("dve_chain")
        act_chain = sem("act_chain")

        W_ADA0, W_IN, W_CMP, W_OUT = 0, 12, 20, 22
        W_MLP0 = W_OUT + 2
        W_ADA1 = W_MLP0 + MLP_UNITS
        W_GIN, W_GOUT = W_ADA1 + 12, W_ADA1 + 18
        W_MLP1 = W_GOUT + 2

        def slot(n, k=KC):
            return wring[:, n % WSLOTS, :].rearrange("p (k c) -> p k c", k=k)

        QA, KA, VA, QB, CKV, SKV, WKV = range(7)
        pj_units = [(j, t) for j in range(7) for t in range(NT + 1)]

        def rows_of(t):
            return P if t < NT else TS

        has_dve = [j != VA for j, t in pj_units]
        has_act = [j in (VA, CKV, SKV, WKV) for j, t in pj_units]
        dve_upto = [sum(has_dve[:u + 1]) for u in range(len(pj_units))]
        act_upto = [sum(has_act[:u + 1]) for u in range(len(pj_units))]
        tok_use = [u for u in range(len(pj_units)) if has_dve[u]]
        use_of = {u: r for r, u in enumerate(tok_use)}
        stores_in_slot = [0, 0, 0]
        slot_stores = []
        for r, u in enumerate(tok_use):
            if pj_units[u][0] in (KA, CKV, SKV, WKV):
                stores_in_slot[r % 3] += (NS if pj_units[u] == (WKV, NT) else 1)
            slot_stores.append(16 * stores_in_slot[r % 3])
        turns = [r for r, u in enumerate(tok_use) if pj_units[u] != (CKV, NT)]
        turn_no = {r: i for i, r in enumerate(turns)}

        def tok_slot_free(eng, r):
            if r >= 3:
                if slot_stores[r - 3]:
                    eng.wait_ge(tok_stored[r % 3], slot_stores[r - 3])
                done = [i for i in turns if i <= r - 3]
                eng.wait_ge(tok_turned, len(done))


        gin = ([("r", c, 0) for c in range(8)] + [("q", c, 0) for c in range(4)] + [("k", c, 0) for c in range(4)]
               + [("v", g, t) for g in range(2) for t in range(NT + 1)])
        gin_upto = [4, 8, 12, 16, 16 + NT + 1, 16 + 2 * (NT + 1)]

        units = [(h, t, b) for h in range(HA + HB) for t in range(NT) for b in range(2)]
        group_ends = [h >= HA or b == 1 for h, t, b in units]
        group_of = [sum(group_ends[:v]) for v in range(len(units))]
        groups = [(h, t, b if h >= HA else 0) for (h, t, b), end in zip(units, group_ends) if end]
        last_unit = [max(v for v, x in enumerate(units) if x[0] == h) for h in range(HA + HB)]
        head_groups = [sum(1 for x in groups if x[0] <= h) for h in range(HA + HB)]
        kv_upto = [16 * 7 * (v // KV_PLACES + 1) for v in range(2 * NS)]

        def cached_keys(v, s, pg):
            place = kvb[v % KV_PLACES]
            return place[:, 2 * (s // 2) + pg, s % 2 * P:(s % 2 + 1) * P] if v % 2 else place[:, pg, s * P:(s + 1) * P]

        def cached_values(v, s, pg):
            if v % 2:
                return kvb[v % KV_PLACES][:, 2 * (s // 2) + pg, (2 + s % 2) * P:(3 + s % 2) * P]
            return kvb[v % KV_PLACES][:, 2 + pg, s * P:(s + 1) * P]

        def new_values(v, s):
            if v % 2:
                return (vw if s // 2 else vs)[0:TS, NT, s % 2 * P:(s % 2 + 1) * P]
            return va[0:TS, NT, s * P:(s + 1) * P]

        V_STORES = 2 * (NT + 1) + NT + NS

        def norm_steps(idx, k):
            return (KC + 1) * idx + idx % 2 + k + 1

        def mlp_unit_used(layer, u):
            q, j = divmod(u, 8)
            return (up_mm if j < 4 else down_mm), 32 * layer + QUARTER * q + 2 * (j % 4 + 1)

        def used_up(n):
            if n < W_IN:
                return ada_mm, n - W_ADA0 + 1
            if n < W_OUT - WSLOTS:
                return pj_mm, (NT + 1) * (n - W_IN + 1)
            if n < W_OUT:
                return spv_mm, 2 * NS
            if n < W_MLP0:
                return out_mm, 4 * (n - W_OUT + 1)
            if n < W_ADA1:
                return mlp_unit_used(0, n - W_MLP0)
            if n < W_GIN:
                return ada_mm, 12 + n - W_ADA1 + 1
            if n < W_GOUT:
                return gin_mm, gin_upto[n - W_GIN]
            if n < W_MLP1:
                return out_mm, 8 + 4 * (n - W_GOUT + 1)
            return mlp_unit_used(1, n - W_MLP1)

        block = ctx.enter_context(nc.Block())

        @block.sync
        def _(sp):
            sp.dma_start(cf[:, :], a["const_f32"]).then_inc(small_loaded, 16)
            sp.dma_start(cb[:, :], a["const_bf16"]).then_inc(small_loaded, 16)
            small = [
                (rows[V1_N1:V1_N1 + 16, 0, :], a["norm1_w"].rearrange("l (k p) -> (l k) p", p=P)),
                (rows[V1_N2:V1_N2 + 16, 0, :], a["norm2_w"].rearrange("l (k p) -> (l k) p", p=P)),
                (rows[V1_ADAB:P, 0, :], a["ada_b"].rearrange("l (m p) -> (l m) p", p=P)),
                (rows[V2_FIN:V2_FIN + KC, 1, :], a["final_norm_w"].rearrange("(k p) -> k p", p=P)),
                (rows[V2_SUB:V2_SUB + 1, 1, :], a["diff_subln_w"]),
                (rows[V2_GLAN:V2_GLAN + 2, 1, :], a["gla_norm_w"].rearrange("o (k p) -> (o k) p", p=P)),
                (rows[V2_BG:V2_BG + HC, 1, :], a["gla_b_gate"].rearrange("o (k p) -> (o k) p", p=P)),
                (rows[V2_C:V2_C + KC, 1, :], a["c_prompt"].rearrange("b (k p) -> (b k) p", p=P)),
                (rows[V2_C + KC:V2_ROWS, 1, :], a["c_sample"].rearrange("b (k p) -> (b k) p", p=P)),
                (rows[0:2 * CL, 2, :], a["cmp_pe"].rearrange("o v l d -> (o v l) d")),
                (lw[:, :, :], a["diff_lambda_w"].partition_broadcast(P).rearrange("p o a b -> p (o a) b")),
                (cw2[:, :, :], a["cmp_w2"].rearrange("o v j d -> j (o v) d")),
            ]
            for dst, src in small:
                sp.dma_start(dst, src).then_inc(small_loaded, 16)
            sp.dma_start(x_in, a["x_prompt"].rearrange("b (t p) d -> p (b t) d", p=P)).then_inc(x_loaded, 16)
            sp.dma_start(xs_in[0:TS, :], a["x_sample"].rearrange("n s d -> (n s) d")).then_inc(x_loaded, 16)

            sp.dma_start(gcols[:, :, :], a["gla_w_in"][0].rearrange("(k p) c -> p k c", p=P)[:, :, 3072:3088]).then_inc(gcols_loaded, 16)

            def load(n, src, k=KC, cols=None):
                if n >= WSLOTS:
                    sp.wait_ge(*used_up(n - WSLOTS))
                dst = slot(n, k) if cols is None else slot(n, k)[:, :, 0:cols]
                sp.dma_start(dst, src).then_inc(w_ready[n % WSLOTS], 16)

            def load_adaln(base, src, done):
                for n in range(WSLOTS):
                    load(base + n, src(n))
                with sp.Fori(1, 3) as i:
                    for s in range(WSLOTS):
                        sp.wait_ge(ada_mm, i * WSLOTS + (done + s - WSLOTS + 1))
                        sp.dma_start(slot(s), src(i * WSLOTS + s)).then_inc(w_ready[s], 16)

            def by_columns(w):
                v = w.rearrange("(k p) c -> p k c", p=P)
                return lambda n: v[:, :, bass.ds(n * 512, 512)]

            ada0, ada1 = by_columns(a["ada_w"][0]), by_columns(a["ada_w"][1])
            load_adaln(W_ADA0, ada0, 0)
            w_in = by_columns(a["even_w_in"][0])
            for j in range(7):
                load(W_IN + j, w_in(j))
            load(W_IN + 7, a["even_w_in"][0].rearrange("(k p) c -> p k c", p=P)[:, :, 3584:3596], cols=12)
            for v in range(2):
                load(W_CMP + v, a["cmp_w1"][0, v].rearrange("(l d) j -> d l j", d=P), CL)

            def load_out(base, w):
                for n in range(2):
                    load(base + n, by_columns(w)(n))

            def load_mlp(base, layer):
                w1 = a["mlp_w1"][layer].rearrange("(k p) c -> p k c", p=P)
                w2 = a["mlp_w2"][layer].rearrange("(k p) c -> p k c", p=P)
                for u in range(MLP_UNITS):
                    q, j = divmod(u, 8)
                    cols = slice(j % 4 * 256, (j % 4 + 1) * 256)
                    src = w2[:, q * KC:(q + 1) * KC, cols] if j >= 4 else w1[:, :, q * D:(q + 1) * D][:, :, cols]
                    sp.wait_ge(*used_up(base + u - WSLOTS))
                    sp.dma_start(unit(base + u)[0], src).then_inc(w_ready[(base + u) % WSLOTS], 16)

            load_out(W_OUT, a["even_w_out"][0])
            sp.wait_ge(comb_ready, 1)
            sp.dma_start(wg[0:RANK, :], a["gla_w_gate"][0]).then_inc(wg_loaded, 16)
            load_mlp(W_MLP0, 0)
            load_adaln(W_ADA1, ada1, 12)
            for n, group in enumerate((4, 5, 0, 1, 2, 3)):
                load(W_GIN + n, by_columns(a["gla_w_in"][0])(group))
            for r in range(2):
                sp.wait_ge(s0_stored[r], 16 * HC // 2)
            sp.wait_ge(gs_stored, 16 * HC)
            load_out(W_GOUT, a["gla_w_out"][0])
            load_mlp(W_MLP1, 1)
            for t in range(NT + 1):
                M = rows_of(t)
                sp.wait_ge(fin_kept, 2 * t + 2)
                dst = out[0][0, t * P:(t + 1) * P] if t < NT else out[1].rearrange("n s d -> (n s) d")
                sp.dma_start(dst, fin[0:M, t, :]).then_inc(fin_stored, 16)
            sp.wait_ge(fin_stored, 16 * (NT + 1))

        @block.gpsimd
        def _(pool):
            pool.dma_start(pagesb[:, :], a["page_table"].rearrange("n p -> (n p)").rearrange("(o m) -> o m", o=1)
                           ).then_inc(pages_loaded, 16)
            pool.wait_ge(pages_loaded, 16)
            page = [pool.value_load(pagesb[0:1, m:m + 1], min_val=0, max_val=a["cache_diff_k"].shape[1] - 1)
                    for m in range(NS * NPAGE)]
            cmp_pages = a["cache_cmp_kv"][0].rearrange("f t v g d -> f t (v g d)")
            for m in range(NS * NPAGE):
                pool.dma_start(ctok[:, m, :], cmp_pages[bass.ds(page[m], 1)].rearrange("o t c -> (o t) c")
                               ).then_inc(ctok_loaded, 16)
            for v in range(2):
                pool.dma_start(cw1[:, v, :].rearrange("p (l j) -> p l j", l=CL),
                               a["cmp_w1"][0, v].rearrange("(l d) j -> d l j", d=P)).then_inc(cmpw_loaded, 16)
            pool.wait_ge(cmp2_kept, 1)
            pool.wait_ge(x_evac, KC + 1)
            pool.wait_ge(lam_ready, 1)
            pool.memset(qAs[:, :, :, :], 0.0).then_inc(scratch_zero, 1)
            pool.memset(qBs[:, :, :, :], 0.0).then_inc(scratch_zero, 1)
            pool.dma_start(out[12][0][:, 0:PAST - DS], a["state_win_kv"][0][:, DS:PAST]).then_inc(out_stored, 16)

            def kv_out(o_p, o_s, t):
                if t < NT:
                    return o_p[t * P:(t + 1) * P]
                return o_s

            dk = (out[2].rearrange("e b t h m d -> (e b t) (h m d)"), out[8].rearrange("e n t h m d -> (e n t) (h m d)"))
            dv = (out[3].rearrange("e b t h d -> (e b t) (h d)"), out[9].rearrange("e n t h d -> (e n t) (h d)"))
            kv = {CKV: (out[4].rearrange("e b t v g d -> (e b t) (v g d)"), out[10].rearrange("e n t v g d -> (e n t) (v g d)")),
                  SKV: (out[5].rearrange("e b t v g d -> (e b t) (v g d)"), out[11].rearrange("e n t v g d -> (e n t) (v g d)")),
                  WKV: (out[6].rearrange("e b t v g d -> (e b t) (v g d)"), None)}
            win_s = out[12].rearrange("e n t v g d -> (e n) t (v g d)")
            for u, (j, t) in enumerate(pj_units):
                M = rows_of(t)
                if has_dve[u]:
                    pool.wait_ge(tok_ready, use_of[u] + 1)
                if has_act[u]:
                    pool.wait_ge(pj_act, act_upto[u])
                r = use_of.get(u)
                if j == KA:
                    pool.dma_start(kv_out(*dk, t), tok[0:M, r % 3, :]).then_inc(tok_stored[r % 3], 16)
                elif j == VA:
                    pool.dma_start(kv_out(*dv, t), va[0:M, t, :]).then_inc(v_stored, 16)
                elif j == CKV:
                    pool.dma_start(kv_out(*kv[j], t), tok[0:M, r % 3, :]).then_inc(tok_stored[r % 3], 16)
                elif j in (SKV, WKV):
                    v = vs if j == SKV else vw
                    if (j, t) == (WKV, NT):
                        for n in range(NS):
                            new = win_s[n, PAST - DS:PAST]
                            pool.dma_start(new[:, 0:256], tok[DS * n:DS * n + DS, r % 3, 0:256]).then_inc(tok_stored[r % 3], 16)
                            pool.dma_start(new[:, 256:512], v[DS * n:DS * n + DS, t, :]).then_inc(v_stored, 16)
                    else:
                        o = kv_out(*kv[j], t)
                        pool.dma_start(o[:, 0:256], tok[0:M, r % 3, 0:256]).then_inc(tok_stored[r % 3], 16)
                        pool.dma_start(o[:, 256:512], v[0:M, t, :]).then_inc(v_stored, 16)
            pool.wait_ge(gate_mm, 1)
            ck = a["cache_diff_k"][0].rearrange("f t h m d -> f t (h m d)")
            cv = a["cache_diff_v"][0].rearrange("f t h d -> f t (h d)")
            cs = a["cache_sel_kv"][0].rearrange("f t v g d -> f t (v g d)")
            win = a["state_win_kv"][0].rearrange("n (b p) v g d -> n p b (v g d)", p=P)
            for v in range(2 * NS):
                n = v // 2
                if v == 4:
                    pool.wait_ge(cmpp_mm, 2)
                if v == KV_PLACES - 1:
                    pool.wait_ge(o_kept, HA + HB)
                if v >= KV_PLACES:
                    pool.wait_ge(spv_mm, v - KV_PLACES + 1)
                if v % 2 == 0:
                    for b, cache in enumerate((ck, cv)):
                        for pg in range(NPAGE):
                            pool.dma_start(kvb[v % KV_PLACES][:, 2 * b + pg, :], cache[bass.ds(page[n * NPAGE + pg], 1)].rearrange("o t c -> (o t) c")
                                           ).then_inc(kv_loaded[v % KV_PLACES // 2], 16)
                else:
                    for pg in range(NPAGE):
                        pool.dma_start(kvb[v % KV_PLACES][:, pg, :], cs[bass.ds(page[n * NPAGE + pg], 1)].rearrange("o t c -> (o t) c")
                                       ).then_inc(kv_loaded[v % KV_PLACES // 2], 16)
                    pool.dma_start(kvb[v % KV_PLACES][:, 2:4, :], win[n]).then_inc(kv_loaded[v % KV_PLACES // 2], 16)
            states = a["state_gla"][0].rearrange("n h d e -> h d n e")
            new_states = out[13][0].rearrange("n h d e -> h d n e")
            pool.wait_ge(gin_mm, gin_upto[3])

            def load_state(h):
                if h >= 2:
                    pool.wait_ge(s0_stored[h % 2], 16 * (h // 2))
                pool.dma_start(s0[:, h % 2, :, :], states[h]).then_inc(s0_loaded[h % 2], 16)

            load_state(0)
            load_state(1)
            for h in range(HC):
                pool.wait_ge(s_ready, NCH * (h + 1))
                pool.dma_start(out[7][0, 0, h], sp_[:, 0, :]).then_inc(gs_stored, 16)
                pool.wait_ge(st_kept, 8 * (h + 1))
                pool.dma_start(new_states[h], s0[:, h % 2, :, :]).then_inc(s0_stored[h % 2], 16)
                if h + 2 < HC:
                    load_state(h + 2)
            pool.wait_ge(gs_stored, 16 * HC)
            for r in range(2):
                pool.wait_ge(s0_stored[r], 16 * (HC // 2))
            pool.wait_ge(v_stored, 16 * V_STORES)
            for i in range(3):
                pool.wait_ge(tok_stored[i], 16 * stores_in_slot[i])
            pool.wait_ge(out_stored, 16)

        @block.tensor
        def _(pe):
            pe.wait_ge(small_loaded, 16 * 14)
            pe.transpose(ps[:, 0, 0:P], rows[:, 0, :], ident[:, :])
            pe.transpose(ps[:, 0, P:P + V2_ROWS], rows[0:V2_ROWS, 1, :], ident[0:V2_ROWS, 0:V2_ROWS])
            pe.transpose(ps[:, 0, 256:256 + 2 * CL], rows[0:2 * CL, 2, :], ident[0:2 * CL, 0:2 * CL]).then_inc(small_turned, 1)
            pe.wait_ge(x_loaded, 32)
            for k in range(KC + 1):
                if k >= 3:
                    pe.wait_ge(x_evac, k - 2)
                bank = ps[:, 1 + k % 3, :]
                if k < KC:
                    for t in range(NT):
                        mm = pe.transpose(bank[:, t * P:(t + 1) * P], x_in[:, t, k * P:(k + 1) * P], ident[:, :])
                else:
                    for kk in range(KC):
                        mm = pe.transpose(bank[:, kk * TS:(kk + 1) * TS], xs_in[0:TS, kk * P:(kk + 1) * P], ident[0:TS, 0:TS])
                mm.then_inc(x_turned, 1)
            def adaln_round(layer, base, i):
                for s in range(WSLOTS + 1):
                    if s < WSLOTS:
                        pe.wait_ge(ada_rows, i * WSLOTS + (16 * layer + s + 1))
                        pe.wait_ge(w_ready[s], (i + (base // WSLOTS + 1)) * 16)
                        for k in range(KC):
                            rows_k = slice(32 * (k % 4), 32 * (k % 4) + 9)
                            mm = pe.matmul(ps[rows_k, s, :], scT[:, k, :], slot(s)[:, k, :], start=k < 4, stop=k >= 4)
                        mm.then_inc(ada_mm, 1)
                    if s:
                        pe.wait_ge(ada_rows, i * WSLOTS + (16 * layer + s + 4))
                        pe.wait_ge(ada_kept, i * WSLOTS + (16 * layer + s))
                        for c in range(4):
                            mm = pe.matmul(ps[:, WSLOTS + s - 1, c * 16:c * 16 + 9],
                                           ada_row[:, (s - 1) % 2, c * P:(c + 1) * P], const("fold"), start=True, stop=True)
                        mm.then_inc(ada_turned, 1)

            def compress_samples(v):
                pe.wait_ge(ctok_loaded, 16 * NS * NPAGE)
                pe.wait_ge(cmpw_loaded, 32)
                for q in range(8):
                    g, pair = q // 4, q % 4
                    c = 8 * v + q
                    if c >= 4:
                        pe.wait_ge(cxs_ready, c - 3)
                    for w in range(4):
                        n, pg = 2 * pair + w // 2, w % 2
                        mm = pe.transpose(ps[:, 4 + c % 4, w * P:(w + 1) * P],
                                          ctok[:, n * NPAGE + pg, (2 * v + g) * P:(2 * v + g + 1) * P], ident[:, :])
                    mm.then_inc(ctok_turned, 1)
                pe.wait_ge(cxs_ready, 8 * v + 8)
                blocks = cxs[:, :, :].rearrange("p s (i r) -> p s i r", r=CS)
                for l in range(CL):
                    w1 = cw1[:, v, l * P:(l + 1) * P]
                    pe.matmul(ps[:, 2 * v, 0:16 * NB_S].rearrange("p (s i) -> p s i", s=16), w1,
                              blocks[:, :, l // CS:l // CS + NB_S, l % CS], start=l == 0, stop=l == CL - 1)
                    mm = pe.matmul(ps[:, 2 * v + 1, 0:1], w1, peT[:, v * CL + l:v * CL + l + 1], start=l == 0, stop=l == CL - 1)
                mm.then_inc(cmp_mm, 1)

            def norm(idx):
                for k in range(KC):
                    pe.wait_ge(norm_sq, idx * KC + k + 1)
                    squares = norm_squares[idx]
                    pe.matmul(ps[:, 0, :], ones[:, :], squares[:, k, 0:SEQ], start=k == 0, stop=k == KC - 1)
                    mm = pe.matmul(ps[:, 1, 0:TS], ones[:, :], squares[:, k, SEQ:T], start=k == 0, stop=k == KC - 1)
                mm.then_inc(norm_sum, 1)

            def weight(n):
                pe.wait_ge(w_ready[n % WSLOTS], 16 * (n // WSLOTS + 1))

            pe.wait_ge(x_evac, KC + 1)
            pe.wait_ge(small_kept, 3)
            norm(0)
            pe.wait_ge(silu_ready, 1)
            for i in range(3):
                adaln_round(0, W_ADA0, i)
                pe.wait_ge(ada_kept, WSLOTS * (i + 2))
                if i < 2:
                    compress_samples(i)
                    pe.wait_ge(cmp_hid, i + 1)
            for v in range(2):
                pe.wait_ge(cmp_hid, v + 1)
                if v == 0:
                    mm = pe.matmul(ps[:, 4, 0:GB * NS * NB_S], cw2[:, 0, :], hids[:, 0, :], start=True, stop=True)
                else:
                    for g in range(GB):
                        mm = pe.matmul(ps[0:NS * NB_S, 5, g * P:(g + 1) * P], hids[:, 1, g * NS * NB_S:(g + 1) * NS * NB_S],
                                       cw2[:, 1, :], start=True, stop=True)
            mm.then_inc(cmp2_mm, 1)

            pe.wait_ge(cmp_hid, 2)
            pe.wait_ge(h_prompt, KC)
            pe.wait_ge(h_sample, 1)
            pe.wait_ge(cmp2_kept, 1)

            def turn(u):
                r = use_of.get(u)
                if r is None or r not in turn_no:
                    return
                j, t = pj_units[u]
                M, i = rows_of(t), turn_no[r]
                pe.wait_ge(tok_ready, r + 1)
                if j == CKV:
                    pe.wait_ge(pj_act, act_upto[u])
                if i >= 4:
                    pe.wait_ge(turn_kept, i - 3)
                for b in range(4 if j in (QA, KA, QB, CKV) else 2):
                    mm = pe.transpose(ps[:, 4 + i % 4, b * M:(b + 1) * M], tok[0:M, r % 3, b * P:(b + 1) * P], ident[0:M, 0:M])
                mm.then_inc(tok_turned, 1)

            for u, (j, t) in enumerate(pj_units):
                M = rows_of(t)
                if t == 0:
                    weight(W_IN + j)
                if u >= 4:
                    pe.wait_ge(pj_dve, dve_upto[u - 4])
                    if act_upto[u - 4]:
                        pe.wait_ge(pj_act, act_upto[u - 4])
                for k in range(KC):
                    mm = pe.matmul(ps[0:M, u % 4, :], hT[:, k, t * P:t * P + M], slot(W_IN + j)[:, k, :],
                                   start=k == 0, stop=k == KC - 1)
                mm.then_inc(pj_mm, 1)
                if u:
                    turn(u - 1)
            turn(len(pj_units) - 1)
            weight(W_IN + 7)
            pe.wait_ge(pj_dve, dve_upto[-1])
            pe.wait_ge(pj_act, act_upto[-1])
            for t in range(NT + 1):
                M = rows_of(t)
                for k in range(KC):
                    mm = pe.matmul(ps[0:M, 0, t * 16:t * 16 + 12], hT[:, k, t * P:t * P + M], slot(W_IN + 7)[:, k, 0:12],
                                   start=k == 0, stop=k == KC - 1)
            mm.then_inc(gate_mm, 1)
            pe.wait_ge(turn_kept, len(turns))
            pe.wait_ge(pe_col, 1)
            for v in range(2):
                weight(W_CMP + v)
                blocks = cxp[:, v, :].rearrange("p (i r) -> p i r", r=CS)
                for l in range(CL):
                    mm = pe.matmul(ps[:, 1 + v, 0:2 * (NB_P + 1) + 1], slot(W_CMP + v, CL)[:, l, :],
                                   blocks[:, l // CS:l // CS + 2 * (NB_P + 1) + 1, l % CS], start=l == 0, stop=l == CL - 1)
                mm.then_inc(cmpp_mm, 1)
            pe.wait_ge(gate_diag, 1)
            for b in range(2):
                mm = pe.matmul(ps[:, 4 + b, 0:6 * TS], ones[0:TS, :], gdiag[0:TS, 6 * b:6 * b + 6, :], start=True, stop=True)
            mm.then_inc(gb_mm, 1)
            pe.wait_ge(cmpp_hid, 2)
            pe.matmul(ps[:, 3, 0:2 * NB_P], cw2[:, 0, :], hidp[:, 0, 0:2 * NB_P], start=True, stop=True)
            for g in range(GB):
                mm = pe.matmul(ps[0:NB_P, 3, (1 + g) * P:(2 + g) * P], hidp[:, 1, g * NB_P:(g + 1) * NB_P], cw2[:, 1, :],
                               start=True, stop=True)
            mm.then_inc(cmpp2_mm, 1)
            pe.wait_ge(cmpp2_kept, 2)
            for h in range(HB):
                for t in range(NT):
                    c = (h * NT + t) * NB_P
                    mm = pe.matmul(ps[:, 6, c:c + NB_P], qbT[:, h, t * P:(t + 1) * P], kccp[:, h // 2, :], start=True, stop=True)
            mm.then_inc(cs_mm, 1)
            pe.wait_ge(cs_p, 1)
            pe.wait_ge(gb_kept, 1)
            for h in range(HB):
                for t in range(NT):
                    mm = pe.transpose(ps[0:NB_P, 4 + h, t * P:(t + 1) * P], s1[:, h * NT + t, :], ident[:, :])
                mm.then_inc(cs_turned, 1)
            pe.wait_ge(ptc_kept, HB)

            def p_scores(v):
                h, t, b = units[v]
                if v >= 3:
                    pe.wait_ge(p_ready, v - 2)
                bank, W = ps[:, v % 3, :], (t + 1) * P
                if h < HA:
                    lo = slice(64 * b, 64 * b + 64)
                    q, keys = qaT[lo, h, t * P:(t + 1) * P], kaT[lo, h, 0:W]
                else:
                    q, keys = qbT[:, h - HA, t * P:(t + 1) * P], (wkT if b else skT)[:, (h - HA) // 2, 0:W]
                pe.matmul(bank[:, W - P:W], identb, causalb, start=True, stop=True)
                pe.matmul(bank[:, 0:W], q, keys, start=False, stop=True, skip_group_check=True).then_inc(s_mm, 1)

            def p_turn(v):
                h, t, b = units[v]
                w = group_of[v]
                pe.wait_ge(diag_ready, v + 1)
                if not group_ends[v]:
                    return
                if w >= 2:
                    pe.wait_ge(pt_kept, w - 1)
                both = [v - 1, v] if h < HA else [v]
                for kb in range(t + 1):
                    for u in both:
                        mm = pe.matmul(ps[:, 3 + w % 2, kb * P:(kb + 1) * P], pbuf[:, u % 3, kb * P:(kb + 1) * P], diag[:, u % 3, :],
                                       start=u == both[0], stop=u == v)
                mm.then_inc(pt_mm, 1)

            def p_values(w):
                h, t, b = groups[w]
                pe.wait_ge(pt_kept, w + 1)
                if t == 0 and b == 0 and h >= 2:
                    pe.wait_ge(o_kept, h - 1)
                o = ps[:, 5 + h % 2, t * P:(t + 1) * P]
                for kb in range(t + 1):
                    if h < HA:
                        vals = va[:, kb, h * P:(h + 1) * P]
                    else:
                        vals = (vw if b else vs)[:, kb, (h - HA) // 2 * P:((h - HA) // 2 + 1) * P]
                    mm = pe.matmul(o, vals, ptb[:, w % 3, kb * P:(kb + 1) * P], start=kb == 0 and b == 0, stop=kb == t and h < HA)
                if h >= HA and b == 1:
                    mm = pe.matmul(o, vccp[0:NB_P, (h - HA) // 2, :], ptc[0:NB_P, h - HA, t * P:(t + 1) * P], start=False, stop=True)
                mm.then_inc(pv_mm, 1)

            for v in range(len(units) + 4):
                if v < len(units):
                    p_scores(v)
                if 2 <= v < len(units) + 2:
                    p_turn(v - 2)
                if v >= 4 and group_ends[v - 4]:
                    p_values(group_of[v - 4])

            pe.wait_ge(o_kept, HA + HB)
            pe.wait_ge(qbc_ready, 1)
            for g in range(GB):
                mm = pe.matmul(ps[:, 7, g * P:g * P + NS * NB_S], qbc[:, g, :], kccs[:, g, :], start=True, stop=True)
            mm.then_inc(ss_mm, 1)
            pe.wait_ge(ss_p, 1)
            for g in range(GB):
                mm = pe.transpose(ps[0:NS * NB_S, 6, g * P:(g + 1) * P], sc[:, g, :], ident[:, :])
            mm.then_inc(ss_turned, 1)
            pe.wait_ge(ss_kept, 1)
            for g in range(GB):
                mm = pe.matmul(ps[:, 7, g * P:(g + 1) * P], vccs[0:NS * NB_S, g, :], ptsc[0:NS * NB_S, g, :], start=True, stop=True)
            mm.then_inc(ss_pv, 1)

            def s_keys(v):
                pe.wait_ge(kv_loaded[v % KV_PLACES // 2], kv_upto[v])
                for half in range(2):
                    c = 2 * v + half
                    if c >= 3:
                        pe.wait_ge(kt_kept, c - 2)
                    for w in range(4):
                        s, pg = 2 * half + w // 2, w % 2
                        mm = pe.transpose(ps[:, c % 3, w * P:(w + 1) * P], cached_keys(v, s, pg), ident[:, :])
                    mm.then_inc(kt_mm, 1)

            def s_scores(v):
                n, kind = v // 2, v % 2
                pe.wait_ge(kt_kept, 2 * v + 2)
                if v >= 2:
                    pe.wait_ge(sp_ready, v - 1)
                bank = ps[:, 3 + v % 2, :]
                pe.matmul(bank[:, PAST:PAST + TS], identb, newmask[:, n, :], start=True, stop=True)
                for s in range(4):
                    q = qBs[:, s % 2, n, :] if kind else qAs[:, n, s, :]
                    new = (wkT if s // 2 else skT)[:, s % 2, SEQ:T] if kind else kaT[:, s, SEQ:T]
                    pe.matmul(bank[32 * s:32 * s + 32, 0:PAST], q, kts[:, v % 2, s, :], start=False, stop=True, skip_group_check=True)
                    mm = pe.matmul(bank[32 * s:32 * s + 32, PAST:PAST + TS], q, new, start=False, stop=True, skip_group_check=True)
                mm.then_inc(ss2_mm, 1)

            def s_turn(v):
                pe.wait_ge(sdiag_ready, v + 1)
                if v >= 1:
                    pe.wait_ge(spt_kept, v)
                for b in range(3):
                    m = P if b < 2 else TS
                    mm = pe.matmul(ps[0:m, 5, b * P:(b + 1) * P], pbuf[:, v % 3, b * P:b * P + m], diag[:, v % 3, :], start=True, stop=True)
                mm.then_inc(spt_mm, 1)

            def s_values(v):
                pe.wait_ge(spt_kept, v + 1)
                if v >= 2:
                    pe.wait_ge(so_kept, v - 1)
                for s in range(4):
                    for b in range(3):
                        m = P if b < 2 else TS
                        vals = cached_values(v, s, b) if b < 2 else new_values(v, s)
                        mm = pe.matmul(ps[:, 6 + v % 2, 32 * s:32 * s + 32], vals, ptb[0:m, v % 3, b * P + 32 * s:b * P + 32 * s + 32],
                                       start=b == 0, stop=b == 2)
                mm.then_inc(spv_mm, 1)

            pe.wait_ge(oc_kept, 1)
            for v in range(2 * NS + 3):
                if v < 2 * NS:
                    s_keys(v)
                if 1 <= v <= 2 * NS:
                    s_scores(v - 1)
                if 2 <= v <= 2 * NS + 1:
                    s_turn(v - 2)
                if v >= 3:
                    s_values(v - 3)

            for h in range(HA):
                pe.wait_ge(sub_sq, h + 1)
                pe.matmul(ps[:, h, :], ones[:, :], sq[:, h, 0:SEQ], start=True, stop=True)
                mm = pe.matmul(ps[:, 4, h * TS:(h + 1) * TS], ones[:, :], sq[:, h, SEQ:T], start=True, stop=True)
            mm.then_inc(sub_sum, 1)
            pe.wait_ge(sub_std, 1)

            def out_projection(layer):
                come = list(range(HA, KC)) + list(range(HA)) if layer == 0 else list(range(KC))
                order = [(m, k) for k in come for m in range(4)] + [(m, k) for m in range(4, KC) for k in come]
                for m, k in order:
                    if m % 4 == 0 and k == come[0]:
                        weight((W_GOUT if layer else W_OUT) + m // 4)
                    if m >= 4 and k == come[0]:
                        pe.wait_ge(resid_kept, layer * KC + m - 3)
                    if m == 0 and layer:
                        pe.wait_ge(gmix_ready, k + 1)
                    elif m == 0 and k < HA:
                        pe.wait_ge(mix_ready, k + 1)
                    lhs = slot((W_GOUT if layer else W_OUT) + m // 4)[:, k, m % 4 * P:(m % 4 + 1) * P]
                    first, last = k == come[0], k == come[-1]
                    pe.matmul(ps[:, m % 4, :], lhs, hT[:, k, 0:SEQ], start=first, stop=last)
                    mm = pe.matmul(ps[:, 4 + m % 4, 0:TS], lhs, hT[:, k, SEQ:T], start=first, stop=last)
                    if last:
                        mm.then_inc(out_mm, 1)
                pe.wait_ge(resid_kept, layer * KC + 6)

            def mlp(layer):
                with pe.Fori(0, 4) as q:
                    for j in range(8):
                        pe.wait_ge(w_split, q * 8 + (j + 1 + MLP_UNITS * layer))
                        _, w_hi, w_lo = unit(j)
                        x_hi, x_lo = (h_hi, hT_r) if j < 4 else (hid_hi, hid_lo)
                        for c in range(2):
                            g = 2 * j + c
                            if g < 4:
                                pe.wait_ge(down_free, q * QUARTER + (g + 1 + 36 * layer))
                            elif g < 12:
                                pe.wait_ge(up_free, q * QUARTER + (g - 3 + 32 * layer))
                            else:
                                pe.wait_ge(down_free, q * QUARTER + (g - 7 + 36 * layer))
                            banks = [ps[:, 2 * (g % 4) + i, 0:HALF] for i in range(2)]
                            for k in range(KC):
                                if g == 0:
                                    pe.wait_ge(h_split, KC * layer + k + 1)
                                if g == 8:
                                    pe.wait_ge(hid_ready, q * QUARTER + (k + 1 + 32 * layer))
                                hi, lo = w_hi[:, k, c * P:(c + 1) * P], w_lo[:, k, c * P:(c + 1) * P]
                                halves = [slice(i * HALF, (i + 1) * HALF) for i in range(2)]
                                for bank, cols in zip(banks, halves):
                                    pe.matmul(bank, hi, x_hi[:, k, cols], start=k == 0, stop=False)
                                    pe.matmul(bank, hi, x_lo[:, k, cols], start=False, stop=False)
                                for bank, cols in zip(banks, halves):
                                    mm = pe.matmul(bank, lo, x_hi[:, k, cols], start=False, stop=k == KC - 1)
                            mm.then_inc(up_mm if j < 4 else down_mm, 1)
                pe.wait_ge(down_free, 36 * (layer + 1))

            out_projection(0)
            norm(1)
            mlp(0)

            norm(2)
            with pe.Fori(0, 3) as i:
                adaln_round(1, W_ADA1, i)
            pe.wait_ge(ada_kept, 32)
            pe.wait_ge(h_prompt, 3 * KC)
            pe.wait_ge(h_sample, 3)
            pe.wait_ge(gcols_loaded, 16)
            for k in range(KC):
                pe.matmul(ps[0:RANK, 0, :], gcols[:, k, :], hT[:, k, 0:SEQ], start=k == 0, stop=k == KC - 1)
                mm = pe.matmul(ps[0:RANK, 4, 0:TS], gcols[:, k, :], hT[:, k, SEQ:T], start=k == 0, stop=k == KC - 1)
            mm.then_inc(gl_mm, 1)
            pe.wait_ge(gl_kept, 1)
            pe.wait_ge(wg_loaded, 16)
            for h in range(HC):
                lhs = wg[0:RANK, h * P:(h + 1) * P]
                pe.matmul(ps[:, h, :], lhs, glT[0:RANK, 0:SEQ], start=True, stop=True)
                pe.matmul(ps[:, 4 + h, 0:TS], lhs, glT[0:RANK, SEQ:T], start=True, stop=True).then_inc(gz_mm, 1)
            pe.wait_ge(gz_abs, 2 * HC)
            for u, (kind, c, t) in enumerate(gin):
                if u in [0] + gin_upto[:-1]:
                    weight(W_GIN + ([0] + gin_upto[:-1]).index(u))
                w = slot(W_GIN + sum(u >= x for x in gin_upto))
                if u >= 4:
                    pe.wait_ge(gin_kept, u - 3)
                M = rows_of(t)
                for k in range(KC):
                    first, last = k == 0, k == KC - 1
                    if kind == "v":
                        mm = pe.matmul(ps[0:M, u % 4, :], hT[:, k, t * P:t * P + M], w[:, k, :], start=first, stop=last)
                    else:
                        lhs = w[:, k, c % 4 * P:(c % 4 + 1) * P]
                        pe.matmul(ps[:, u % 4, :], lhs, hT[:, k, 0:SEQ], start=first, stop=last)
                        mm = pe.matmul(ps[:, 4 + u % 4, 0:TS], lhs, hT[:, k, SEQ:T], start=first, stop=last)
                mm.then_inc(gin_mm, 1)

            def g_prepare(h):
                pe.wait_ge(prep_ready, h + 1)
                if h == 0:
                    pe.wait_ge(gin_kept, len(gin))
                if h:
                    pe.wait_ge(att_kept, h)
                    pe.wait_ge(kd_kept, h)
                for t in range(NT):
                    pe.transpose(ps[:, 1, t * P:(t + 1) * P], gkd[:, t * P:(t + 1) * P], ident[:, :])
                pe.transpose(ps[0:TS, 0, 384:512], gkd[:, SEQ:T], ident[:, :]).then_inc(kd_turned, 1)
                for c in range(NCH):
                    lo = 64 * (c % 2)
                    for i in range(4):
                        rhs = gqd[:, c, (i - 1) * SUB:i * SUB] if i else gqe[:, h % 2, c * GCH:c * GCH + SUB]
                        pe.matmul(ps[lo:lo + (i + 1) * SUB, 0, c // 2 * GCH + i * SUB:c // 2 * GCH + (i + 1) * SUB],
                                  gkp[i][:, c, :], rhs, start=True, stop=True)
                pe.matmul(ps[0:TS, 0, 4 * GCH:5 * GCH], gkp_s, gqe[:, h % 2, SEQ:T], start=True, stop=True).then_inc(att_mm, 1)

            def g_states(h, p):
                x = 8 * h + p
                if x >= 3:
                    pe.wait_ge(st_kept, x - 2)
                for w in range(2):
                    if p < 4:
                        lo = slice(64 * w, 64 * w + 64)
                        lhs, rhs = gkdT[lo, h % 2, p, :], gv[lo, p, h * DVC:(h + 1) * DVC]
                    else:
                        lhs, rhs = gkdm[0:TS, 2 * (p - 4) + w, :], gv[0:TS, NT, h * DVC:(h + 1) * DVC]
                    if p < 4 and w:
                        pe.wait_ge(st_first, 4 * h + p + 1)
                    mm = pe.matmul(ps[:, 5 + x % 3, w * DVC:(w + 1) * DVC], lhs, rhs, start=True, stop=True)
                    if p < 4 and w == 0:
                        mm.then_inc(st_first, 1)
                mm.then_inc(st_mm, 1)

            def g_out(h, c):
                if c:
                    pe.wait_ge(s_ready, NCH * h + c)
                    pe.wait_ge(go_mm, NCH * h + c)
                lo = slice(64 * (c % 2), 64 * (c % 2) + 64)
                for e in range(2):
                    o = ps[:, 3 + e, c * GCH:(c + 1) * GCH]
                    if c:
                        pe.matmul(o, sp_[:, c % 4, e * P:(e + 1) * P], gqe[:, h % 2, c * GCH:(c + 1) * GCH], start=True, stop=False)
                    mm = pe.matmul(o, gv[lo, c // 2, h * DVC + e * P:h * DVC + (e + 1) * P], gatt[lo, h % 2, c // 2, :],
                                   start=c == 0, stop=True)
                mm.then_inc(go_mm, 1)

            def g_prompt(h):
                pe.wait_ge(att_kept, h + 1)
                pe.wait_ge(kd_kept, h + 1)
                if h:
                    pe.wait_ge(go_kept, h)
                for p in range(3):
                    g_states(h, p)
                g_out(h, 0)
                g_out(h, 1)
                g_states(h, 3)
                for c in range(2, NCH):
                    g_out(h, c)

            def g_samples(h):
                pe.wait_ge(s0_loaded[h % 2], 16 * (h // 2 + 1))
                for e in range(2):
                    o = ps[:, 2, e * TS:(e + 1) * TS]
                    pe.matmul(o, gv[0:TS, NT, h * DVC + e * P:h * DVC + (e + 1) * P], gatt[0:TS, h % 2, 4, :], start=True, stop=True)
                    for n in range(NS):
                        mm = pe.matmul(o[:, DS * n:DS * n + DS], s0[:, h % 2, n, e * P:(e + 1) * P],
                                       gqe[:, h % 2, SEQ + DS * n:SEQ + DS * n + DS], start=False, stop=True, skip_group_check=True)
                mm.then_inc(os_mm, 1)
                pe.wait_ge(gkdm_ready, h + 1)
                for p in range(4, 8):
                    g_states(h, p)

            g_prepare(0)
            for h in range(HC):
                g_prompt(h)
                if h + 1 < HC:
                    g_prepare(h + 1)
                g_samples(h)
            pe.wait_ge(st_kept, 8 * HC)
            for h in range(HC):
                pe.wait_ge(gn_sq, 2 * h + 2)
                for e in range(2):
                    pe.matmul(ps[:, h, :], ones[:, :], gsq[:, 2 * h + e, 0:SEQ], start=e == 0, stop=e == 1)
                    mm = pe.matmul(ps[:, 4 + h, 0:TS], ones[:, :], gsq[:, 2 * h + e, SEQ:T], start=e == 0, stop=e == 1)
            mm.then_inc(gn_sum, 1)
            out_projection(1)
            norm(3)
            mlp(1)
            norm(4)
            for t in range(NT + 1):
                M = rows_of(t)
                for half in range(2):
                    c = 2 * t + half
                    if c >= 4:
                        pe.wait_ge(fin_kept, c - 3)
                    for w in range(4):
                        k = 4 * half + w
                        if t == 0:
                            pe.wait_ge(norm_x, norm_steps(4, k))
                        mm = pe.transpose(ps[0:M, 2 + c % 4, w * P:(w + 1) * P], hT[:, k, t * P:t * P + M], ident[:, :])
                    mm.then_inc(fin_mm, 1)

        @block.scalar
        def _(act):
            act.wait_ge(small_kept, 2)
            act.activation(cexp, v2T[:, V2_C:V2_ROWS], ACT.Exp, scale=-1.0).then_inc(cexp_ready, 1)
            act.wait_ge(lam_sums, 1)
            act.activation(lam[:, 2:4], lam[:, 0:2], ACT.Exp).then_inc(lam_exp, 1)
            def norm(idx, ready, count):
                for k in range(KC):
                    act.wait_ge(ready, count + k + 1)
                    act.activation(norm_squares[idx][:, k, :], xT[:, k, :], ACT.Square).then_inc(norm_sq, 1)
                act.wait_ge(norm_sum, idx + 1)
                act.activation(rstd[:, 0:SEQ], ps[:, 0, :], ACT.Sqrt, scale=1.0 / D, bias=eps[:, 0:1])
                act.activation(rstd[:, SEQ:T], ps[:, 1, 0:TS], ACT.Sqrt, scale=1.0 / D, bias=eps[:, 0:1]).then_inc(norm_std, 1)

            def modulate(idx, term):
                for k in range(KC):
                    act.wait_ge(norm_x, norm_steps(idx, k) if idx % 2 else (KC + 1) * (idx + 1))
                    act.activation(hT[:, k, 0:SEQ], hT[:, k, 0:SEQ], ACT.Identity, scale=modA[:, k, 0:1],
                                   bias=mod[:, term * KC + k, 0:1]).then_inc(h_prompt, 1)

            def adaln_begin(layer):
                act.wait_ge(norm_std, 2 * layer + 1)
                act.wait_ge(ada_kept, 16 * layer + WSLOTS)
                act.sem_inc(ada_rows, WSLOTS)

            def adaln_round(layer, i):
                for n in range(WSLOTS * i, WSLOTS * (i + 1)):
                    act.wait_ge(ada_mm, 12 * layer + n + 1)
                    if n >= 2:
                        act.wait_ge(ada_turned, 12 * layer + n - 1)
                    for j in range(4):
                        share = slice(32 * j, 32 * j + 9)
                        ins = act.activation(ada_row[share, n % 2, :], ps[share, n % WSLOTS, :], ACT.Copy)
                    ins.then_inc(ada_rows, 1)

            def compress_samples(v):
                if v == 1:
                    act.wait_ge(cmp_mm, 1)
                for q in range(8):
                    c = 8 * v + q
                    act.wait_ge(ctok_turned, c + 1)
                    dst = cxs[:, 8 * (q // 4) + 2 * (q % 4):8 * (q // 4) + 2 * (q % 4) + 2, :]
                    act.activation(dst, ps[:, 4 + c % 4, :].rearrange("p (s t) -> p s t", s=2), ACT.Copy).then_inc(cxs_ready, 1)
                act.wait_ge(cmp_exp, v + 1)
                act.activation(hids[:, v, :], hids[:, v, :], ACT.Exp, scale=-1.0).then_inc(act_chain, 1)

            act.wait_ge(x_evac, KC + 1)
            norm(0, x_evac, 0)
            adaln_begin(0)
            for i in range(3):
                adaln_round(0, i)
                if i < 2:
                    compress_samples(i)
            modulate(0, 0)

            def keep_turn(u):
                r = use_of.get(u)
                if r is None or r not in turn_no:
                    return
                j, t = pj_units[u]
                M, i = rows_of(t), turn_no[r]
                act.wait_ge(tok_turned, i + 1)
                bank = ps[:, 4 + i % 4, :]
                blocks = bank[:, 0:4 * M].rearrange("p (b m) -> p b m", b=4)
                if (j, t) == (QA, NT):
                    act.wait_ge(scratch_zero, 2)
                    for m in range(2):
                        src = bank[64 * m:64 * m + 64, 0:4 * M].rearrange("p (h n s) -> p h n s", h=HA, n=NS)
                        for h in range(HA):
                            ins = act.activation(qAs[64 * m:64 * m + 64, :, h, DS * m:DS * m + DS], src[:, h], ACT.Copy, scale=DKA ** -0.5)
                elif (j, t) == (QB, NT):
                    for h in range(HB):
                        ins = act.activation(qBs[:, h // 2, :, DS * (h % 2):DS * (h % 2) + DS],
                                             bank[:, h * TS:(h + 1) * TS].rearrange("p (n s) -> p n s", n=NS), ACT.Copy, scale=DHB ** -0.5)
                elif j == QA:
                    ins = act.activation(qaT[:, :, t * P:(t + 1) * P], blocks, ACT.Copy, scale=DKA ** -0.5)
                elif j == QB:
                    ins = act.activation(qbT[:, :, t * P:(t + 1) * P], blocks, ACT.Copy, scale=DHB ** -0.5)
                elif j == KA:
                    ins = act.activation(kaT[:, :, t * P:t * P + M], blocks, ACT.Copy)
                elif j == CKV:
                    dst = cxp[:, :, 0:2 * SEQ].rearrange("p v (g c) -> p v g c", g=GB)
                    for v in range(2):
                        ins = act.activation(dst[:, v, :, t * P:(t + 1) * P], blocks[:, 2 * v:2 * v + 2, :], ACT.Copy)
                else:
                    dst = skT if j == SKV else wkT
                    ins = act.activation(dst[:, :, t * P:t * P + M], bank[:, 0:2 * M].rearrange("p (b m) -> p b m", b=2), ACT.Copy)
                ins.then_inc(turn_kept, 1)

            for u, (j, t) in enumerate(pj_units):
                M = rows_of(t)
                if has_act[u]:
                    act.wait_ge(pj_mm, u + 1)
                    if has_dve[u]:
                        act.wait_ge(pj_dve, dve_upto[u])
                    bank = ps[0:M, u % 4, :]
                    if j == VA:
                        ins = act.activation(va[0:M, t, :], bank, ACT.Copy)
                    elif j == CKV:
                        tok_slot_free(act, use_of[u])
                        ins = act.activation(tok[0:M, use_of[u] % 3, 256:512], bank[:, 256:512], ACT.Copy)
                    else:
                        ins = act.activation((vs if j == SKV else vw)[0:M, t, :], bank[:, 256:512], ACT.Copy)
                    ins.then_inc(pj_act, 1)
                if u:
                    keep_turn(u - 1)
            keep_turn(len(pj_units) - 1)
            act.wait_ge(gate_mm, 1)
            act.activation(gates[:, 0:NT, :], ps[:, 0, 0:NT * 16].rearrange("p (t c) -> p t c", t=NT)[:, :, 0:12], ACT.Exp, scale=-1.0).then_inc(gate_exp, 1)
            act.activation(gates[0:TS, NT, :], ps[0:TS, 0, NT * 16:NT * 16 + 12], ACT.Exp, scale=-1.0).then_inc(gate_exp, 1)
            for v in range(2):
                act.wait_ge(cmpp_exp, v + 1)
                act.activation(hidp[:, v, 0:2 * NB_P], hidp[:, v, 0:2 * NB_P], ACT.Exp, scale=-1.0).then_inc(act_chain, 1)
            act.wait_ge(gb_mm, 1)
            act.activation(gb[:, :, :].rearrange("p (b c) t -> p b (c t)", b=2), ps[:, 4:6, 0:6 * TS], ACT.Copy).then_inc(gb_kept, 1)
            act.wait_ge(cs_sub, 1)
            act.activation(s1[:, :, :], s1[:, :, :], ACT.Exp).then_inc(cs_exp, 1)
            for h in range(HB):
                act.wait_ge(cs_turned, h + 1)
                act.activation(ptc[0:NB_P, h, :], ps[0:NB_P, 4 + h, :], ACT.Copy).then_inc(ptc_kept, 1)

            def p_exp(v):
                h, t, b = units[v]
                act.wait_ge(nm_ready, v + 1)
                if v >= 3:
                    act.wait_ge(pt_mm, group_of[v - 3] + 1)
                if v >= 4:
                    act.wait_ge(diag_ready, v - 3)
                W = (t + 1) * P
                act.activation(pbuf[:, v % 3, 0:W], ps[:, v % 3, 0:W], ACT.Exp, bias=nm[:, v % 4:v % 4 + 1],
                               accum_out=sums[:, v % 4:v % 4 + 1]).then_inc(p_ready, 1)

            def p_keep(w):
                h, t, b = groups[w]
                act.wait_ge(pt_mm, w + 1)
                if w >= 3:
                    act.wait_ge(pv_mm, w - 2)
                act.activation(ptb[:, w % 3, 0:(t + 1) * P], ps[:, 3 + w % 2, 0:(t + 1) * P], ACT.Copy).then_inc(pt_kept, 1)

            for i in range(3):
                act.wait_ge(tok_stored[i], 16 * stores_in_slot[i])
            for v in range(len(units) + 2):
                if v < len(units):
                    p_exp(v)
                if v >= 2 and group_ends[v - 2]:
                    p_keep(group_of[v - 2])

            act.wait_ge(ss_sub, 1)
            act.activation(sc[:, :, :], sc[:, :, :], ACT.Exp).then_inc(ss_exp, 1)
            act.wait_ge(ss_turned, 1)
            act.activation(ptsc[0:NS * NB_S, :, :], ps[0:NS * NB_S, 6, 0:GB * P].rearrange("p (g c) -> p g c", g=GB), ACT.Copy).then_inc(ss_kept, 1)

            def s_keep_keys(v):
                for half in range(2):
                    c = 2 * v + half
                    act.wait_ge(kt_mm, c + 1)
                    if v >= 2:
                        act.wait_ge(ss2_mm, v - 1)
                    act.activation(kts[:, v % 2, 2 * half:2 * half + 2, :], ps[:, c % 3, :].rearrange("p (s t) -> p s t", s=2),
                                   ACT.Copy).then_inc(kt_kept, 1)

            def s_exp(v):
                act.wait_ge(snm_ready, v + 1)
                if v >= 3:
                    act.wait_ge(spt_mm, v - 2)
                act.activation(pbuf[:, v % 3, 0:PAST + TS], ps[:, 3 + v % 2, 0:PAST + TS], ACT.Exp, bias=nm[:, v % 4:v % 4 + 1],
                               accum_out=sums[:, v % 4:v % 4 + 1]).then_inc(sp_ready, 1)

            def s_keep_turn(v):
                act.wait_ge(spt_mm, v + 1)
                if v >= 3:
                    act.wait_ge(spv_mm, v - 2)
                act.activation(ptb[:, v % 3, 0:PAST], ps[:, 5, 0:PAST], ACT.Copy)
                act.activation(ptb[0:TS, v % 3, PAST:PAST + P], ps[0:TS, 5, PAST:PAST + P], ACT.Copy).then_inc(spt_kept, 1)

            for v in range(2 * NS + 2):
                if v < 2 * NS:
                    s_keep_keys(v)
                if 1 <= v <= 2 * NS:
                    s_exp(v - 1)
                if 2 <= v:
                    s_keep_turn(v - 2)
            act.wait_ge(comb_ready, 1)
            for h in range(HA):
                act.activation(sq[:, h, :], hT[:, h, :], ACT.Square).then_inc(sub_sq, 1)
            act.wait_ge(sub_sum, 1)
            act.activation(sq[:, :, 0:SEQ], ps[:, 0:HA, :], ACT.Sqrt, scale=1.0 / P, bias=eps[:, 0:1])
            act.activation(sq[:, :, SEQ:T], ps[:, 4, 0:HA * TS].rearrange("p (h c) -> p h c", h=HA), ACT.Sqrt, scale=1.0 / P,
                           bias=eps[:, 0:1]).then_inc(sub_std, 1)
            def w_round(layer, u):
                at, more = u if isinstance(u, tuple) else (u, 0)
                base = W_MLP1 if layer else W_MLP0
                raw, high, _ = unit(at)
                act.wait_ge(w_ready[at % WSLOTS], more + 16 * ((base + at) // WSLOTS + 1))
                act.activation(high, raw, ACT.Copy).then_inc(w_high, 1)

            def h_round(layer):
                act.wait_ge(h_prompt, (2 * layer + 2) * KC)
                act.wait_ge(h_sample, 2 * layer + 2)
                if layer == 0:
                    act.wait_ge(v_stored, 16 * V_STORES)
                for k in range(KC):
                    act.activation(h_hi[:, k, :], hT[:, k, :], ACT.Copy).then_inc(h_high, 1)

            def mlp(layer):
                with act.Fori(0, 3) as q:
                    for j in range(8):
                        w_round(layer, (j + 2, q * 32))
                for j in range(6):
                    w_round(layer, 24 + j + 2)

            w_round(0, 0)
            w_round(0, 1)
            norm(1, resid_kept, 0)
            modulate(1, 3)
            h_round(0)
            mlp(0)

            act.wait_ge(up_mm, 32)
            norm(2, mlp_added, 24)
            adaln_begin(1)
            for i in range(3):
                adaln_round(1, i)
            modulate(2, 0)
            act.wait_ge(gl_mm, 1)
            act.activation(glT[0:RANK, 0:SEQ], ps[0:RANK, 0, :], ACT.Copy)
            act.activation(glT[0:RANK, SEQ:T], ps[0:RANK, 4, 0:TS], ACT.Copy).then_inc(gl_kept, 1)
            act.wait_ge(gz_abs, 2 * HC)
            act.activation(gtmp[:, :, :], gtmp[:, :, :], ACT.Abs).then_inc(act_chain, 1)
            act.wait_ge(act_chain, 5)
            act.activation(gtmp[:, :, :], gtmp[:, :, :], ACT.Exp, scale=-1.0).then_inc(act_chain, 1)
            act.wait_ge(act_chain, 6)
            act.activation(gtmp[:, :, :], gtmp[:, :, :], ACT.Ln, bias=ones[:, 0:1]).then_inc(gz_ln, 1)
            def g_exps(h):
                b = gbt[:, h, :]
                bp = b[:, 0:SEQ].rearrange("p (c t) -> p c t", c=NCH)
                if h == 0:
                    act.wait_ge(b_ready, HC)
                    act.wait_ge(r_ready, KC)
                else:
                    act.wait_ge(prep_ready, h)
                    act.wait_ge(att_mm, h)
                act.activation(geb, b, ACT.Exp, scale=1.0 / TAU).then_inc(eb_ready, 1)
                act.activation(gkp[0], bp[:, :, 0:SUB], ACT.Exp, scale=-1.0 / TAU)
                act.activation(gkp_s, b[:, SEQ:T], ACT.Exp, scale=-1.0 / TAU).then_inc(eb_ready, 1)
                act.wait_ge(gsub_ready, h + 1)
                act.activation(gqd, gqd, ACT.Exp, scale=1.0 / TAU)
                later = gscr[:, kp_at[1]:kp_at[4]]
                act.activation(later, later, ACT.Exp, scale=1.0 / TAU)
                act.activation(gkd, gkd, ACT.Exp, scale=1.0 / TAU).then_inc(ex_ready, 1)

            for u, (kind, c, t) in enumerate(gin):
                if u == gin_upto[3]:
                    g_exps(0)
                act.wait_ge(gin_mm, u + 1)
                M = rows_of(t)
                if kind == "v":
                    ins = act.activation(gv[0:M, t, c * 512:(c + 1) * 512], ps[0:M, u % 4, :], ACT.Copy)
                else:
                    dst = {"q": gq, "k": gk, "r": gr}[kind][:, c, :]
                    scale = DKC ** -0.5 if kind == "q" else 1.0
                    act.activation(dst[:, 0:SEQ], ps[:, u % 4, :], ACT.Copy, scale=scale)
                    ins = act.activation(dst[:, SEQ:T], ps[:, 4 + u % 4, 0:TS], ACT.Copy, scale=scale)
                ins.then_inc(gin_kept, 1)
                if kind == "r":
                    act.wait_ge(gin_kept, u + 1)
                    if c >= 2:
                        act.wait_ge(r_ready, c - 1)
                    act.activation(er[:, c % 2, :], dst, ACT.Exp, scale=-1.0).then_inc(r_exp, 1)

            def g_keep_turn(h):
                act.wait_ge(kd_turned, h + 1)
                if h >= 2:
                    act.wait_ge(st_mm, 8 * (h - 1))
                act.activation(gkdT[:, h % 2, 0:NT, :], ps[:, 1, :].rearrange("p (t d) -> p t d", t=NT), ACT.Copy).then_inc(kd_kept, 1)

            def g_keep_prompt(h):
                act.wait_ge(go_mm, NCH * (h + 1))
                for e in range(2):
                    act.activation(hT[:, 2 * h + e, 0:SEQ], ps[:, 3 + e, :], ACT.Copy)

            def g_keep_samples(h):
                act.wait_ge(os_mm, h + 1)
                act.activation(hT[:, 2 * h:2 * h + 2, SEQ:T], ps[:, 2, 0:2 * TS].rearrange("p (e t) -> p e t", e=2), ACT.Copy).then_inc(go_kept, 1)

            g_keep_turn(0)
            g_exps(1)
            for h in range(HC):
                g_keep_prompt(h)
                if h + 1 < HC:
                    g_keep_turn(h + 1)
                g_keep_samples(h)
                if h + 2 < HC:
                    g_exps(h + 2)
            act.wait_ge(go_kept, HC)
            for k in range(KC):
                act.activation(gsq[:, k, :], hT[:, k, :], ACT.Square).then_inc(gn_sq, 1)
            act.wait_ge(gn_sum, 1)
            act.activation(gstd[:, :, 0:SEQ], ps[:, 0:HC, :], ACT.Sqrt, scale=1.0 / DVC, bias=eps[:, 0:1])
            act.activation(gstd[:, :, SEQ:T], ps[:, 4:4 + HC, 0:TS], ACT.Sqrt, scale=1.0 / DVC, bias=eps[:, 0:1]).then_inc(gn_std, 1)
            w_round(1, 0)
            w_round(1, 1)
            norm(3, resid_kept, KC)
            modulate(3, 3)
            h_round(1)
            mlp(1)
            act.wait_ge(up_mm, 64)
            norm(4, mlp_added, 56)
            for c in range(2 * (NT + 1)):
                t, half = c // 2, c % 2
                M = rows_of(t)
                act.wait_ge(fin_mm, c + 1)
                act.activation(fin[0:M, t, half * 512:(half + 1) * 512], ps[0:M, 2 + c % 4, :], ACT.Copy).then_inc(fin_kept, 1)

        @block.vector
        def _(dve):
            chain = [0]

            def step(ins):
                chain[0] += 1
                ins.then_inc(dve_chain, 1)
                dve.wait_ge(dve_chain, chain[0])

            dve.wait_ge(small_turned, 1)
            dve.tensor_copy(v1T[:, :], ps[:, 0, 0:P]).then_inc(small_kept, 1)
            dve.tensor_copy(v2T[:, :], ps[:, 0, P:P + V2_ROWS]).then_inc(small_kept, 1)
            dve.tensor_copy(peT[:, :], ps[:, 0, 256:256 + 2 * CL]).then_inc(small_kept, 1)
            dve.wait_ge(small_kept, 3)
            dve.wait_ge(cexp_ready, 1)
            step(dve.tensor_scalar(cexp, cexp, 1.0, None, ALU.add))
            step(dve.reciprocal(cexp, cexp))
            dve.tensor_tensor(scT[:, :, :], v2T[:, V2_C:V2_ROWS].rearrange("p (b k) -> p k b", k=KC),
                              cexp.rearrange("p (b k) -> p k b", k=KC), ALU.mult).then_inc(silu_ready, 1)
            lwp = lw[:, :, :].rearrange("p (a b) d -> p a b d", b=2)
            step(dve.tensor_tensor(lprod[:, :, :], lwp[:, :, 0, :], lwp[:, :, 1, :], ALU.mult))
            dve.tensor_reduce(lam[:, 0:2], lprod[:, :, :], AX.X, ALU.add).then_inc(lam_sums, 1)
            dve.wait_ge(lam_exp, 1)
            step(dve.tensor_tensor(lam[:, 4:5], lam[:, 3:4], lam[:, 2:3], ALU.subtract))
            dve.tensor_scalar(lam[:, 5:6], lam[:, 4:5], -LAM_INIT, None, ALU.add).then_inc(lam_ready, 1)
            for k in range(KC + 1):
                dve.wait_ge(x_turned, k + 1)
                bank = ps[:, 1 + k % 3, :]
                if k < KC:
                    ins = dve.tensor_copy(xT[:, k, 0:SEQ], bank)
                else:
                    ins = dve.tensor_copy(xT[:, :, SEQ:T], bank.rearrange("p (k c) -> p k c", k=KC))
                ins.then_inc(x_evac, 1)
            dve.wait_ge(x_evac, KC + 1)
            def adaln_begin():
                step(dve.memset(ada_row, 0.0))
                dve.sem_inc(ada_kept, WSLOTS)

            def adaln_round(layer, i):
                bias = v1T[:, V1_ADAB + 48 * layer:V1_ADAB + 48 * layer + 48]
                for n in range(WSLOTS * i, WSLOTS * (i + 1)):
                    dve.wait_ge(ada_turned, 12 * layer + n + 1)
                    dve.tensor_tensor(mod[:, 4 * n:4 * n + 4, :],
                                      ps[:, WSLOTS + n % WSLOTS, 0:64].rearrange("p (c b) -> p c b", c=4)[:, :, 0:9],
                                      bias[:, 4 * n:4 * n + 4].unsqueeze(2).to_broadcast([P, 4, 9]), ALU.add).then_inc(ada_kept, 1)
                dve.wait_ge(ada_kept, 16 * layer + WSLOTS * (i + 2))

            def compress_samples(v):
                dve.wait_ge(cmp_mm, v + 1)
                step(dve.tensor_copy(lam[:, 6 + v:7 + v], ps[:, 2 * v + 1, 0:1]))
                dve.tensor_scalar(hids[:, v, :], ps[:, 2 * v, 0:16 * NB_S], lam[:, 6 + v:7 + v], None, ALU.add).then_inc(cmp_exp, 1)
                dve.wait_ge(act_chain, v + 1)
                step(dve.tensor_scalar(hids[:, v, :], hids[:, v, :], 1.0, None, ALU.add))
                step(dve.reciprocal(hids[:, v, :], hids[:, v, :]))
                dve.scalar_tensor_tensor(out=hids[:, v, :], in0=ps[:, 2 * v, 0:16 * NB_S], scalar=lam[:, 6 + v:7 + v],
                                         in1=hids[:, v, :], op0=ALU.add, op1=ALU.mult).then_inc(cmp_hid, 1)

            def mod_scale(term, w):
                step(dve.scalar_tensor_tensor(out=modA[:, :, :], in0=mod[:, (term + 1) * KC:(term + 2) * KC, :], scalar=1.0,
                                              in1=w.unsqueeze(2).to_broadcast([P, KC, 9]), op0=ALU.add, op1=ALU.mult))
                dve.sem_inc(norm_x, 1)

            def norm(idx):
                dve.wait_ge(norm_std, idx + 1)
                step(dve.reciprocal(rstd[:, :], rstd[:, :]))
                for k in range(KC):
                    dve.tensor_tensor(hT[:, k, :], xT[:, k, :], rstd[:, :], ALU.mult).then_inc(norm_x, 1)
                dve.wait_ge(norm_x, norm_steps(idx, KC - 1))

            def modulate(term):
                for n in range(NS):
                    cols = hT[:, :, SEQ + DS * n:SEQ + DS * (n + 1)]
                    ins = dve.tensor_tensor(cols, cols, modA[:, :, 1 + n:2 + n].to_broadcast([P, KC, DS]), ALU.mult)
                step(ins)
                for n in range(NS):
                    cols = hT[:, :, SEQ + DS * n:SEQ + DS * (n + 1)]
                    ins = dve.tensor_tensor(cols, cols, mod[:, term * KC:(term + 1) * KC, 1 + n:2 + n].to_broadcast([P, KC, DS]), ALU.add)
                ins.then_inc(h_sample, 1)

            dve.wait_ge(x_evac, KC + 1)
            norm(0)
            adaln_begin()
            for i in range(3):
                adaln_round(0, i)
                if i < 2:
                    compress_samples(i)
            mod_scale(0, v1T[:, V1_N1:V1_N1 + KC])
            modulate(0)
            dve.wait_ge(cmp2_mm, 1)
            step(dve.tensor_copy(kccs[:, :, :], ps[:, 4, 0:GB * NS * NB_S].rearrange("p (g c) -> p g c", g=GB)))
            dve.tensor_copy(vccs[0:NS * NB_S, :, :], ps[0:NS * NB_S, 5, 0:GB * P].rearrange("p (g c) -> p g c", g=GB)
                            ).then_inc(cmp2_kept, 1)

            def rope(src, t, M, kind, blocks):
                cos, sin = rope_tab[kind]
                w = 32 if kind == "a" else 64
                n = blocks * 2 * w
                x = src[:, 0:n].rearrange("p (b h w) -> p b h w", b=blocks, h=2)
                t1 = rt1[0:M, 0:n].rearrange("p (b h w) -> p b h w", b=blocks, h=2)
                t2 = rt2[0:M, 0:n].rearrange("p (b h w) -> p b h w", b=blocks, h=2)
                c = cos[0:M, t, :].unsqueeze(1).to_broadcast([M, blocks, w])
                s = sin[0:M, t, :].unsqueeze(1).to_broadcast([M, blocks, w])
                dve.tensor_tensor(t1[:, :, 0, :], x[:, :, 0, :], c, ALU.mult)
                dve.tensor_tensor(t1[:, :, 1, :], x[:, :, 1, :], c, ALU.mult)
                dve.tensor_tensor(t2[:, :, 0, :], x[:, :, 1, :], s, ALU.mult)
                dve.tensor_tensor(t2[:, :, 1, :], x[:, :, 0, :], s, ALU.mult).then_inc(pj_dve, 1)
                return t1, t2

            for u, (j, t) in enumerate(pj_units):
                if not has_dve[u]:
                    continue
                M, r = rows_of(t), use_of[u]
                dve.wait_ge(pj_mm, u + 1)
                kind, blocks = ("a", 8) if j in (QA, KA) else ("b", 4 if j == QB else 2)
                t1, t2 = rope(ps[0:M, u % 4, :], t, M, kind, blocks)
                tok_slot_free(dve, r)
                dve.wait_ge(pj_dve, r + 1)
                w = t1.shape[3]
                o = tok[0:M, r % 3, 0:blocks * 2 * w].rearrange("p (b h w) -> p b h w", b=blocks, h=2)
                step(dve.tensor_tensor(o[:, :, 0, :], t1[:, :, 0, :], t2[:, :, 0, :], ALU.subtract))
                dve.tensor_tensor(o[:, :, 1, :], t1[:, :, 1, :], t2[:, :, 1, :], ALU.add).then_inc(tok_ready, 1)
                dve.wait_ge(tok_ready, r + 1)
            for v in range(2):
                ins = dve.tensor_copy(cxp[:, v, 2 * SEQ:2 * SEQ + CL], peT[:, v * CL:(v + 1) * CL])
            ins.then_inc(pe_col, 1)
            dve.wait_ge(gate_exp, 2)
            dve.tensor_scalar(gates[:, 0:NT, :], gates[:, 0:NT, :], 1.0, None, ALU.add)
            step(dve.tensor_scalar(gates[0:TS, NT, :], gates[0:TS, NT, :], 1.0, None, ALU.add))
            dve.reciprocal(gates[:, 0:NT, :], gates[:, 0:NT, :])
            step(dve.reciprocal(gates[0:TS, NT, :], gates[0:TS, NT, :]))
            dve.wait_ge(turn_kept, len(turns))
            dve.tensor_tensor(gdiag[0:TS, :, :], gates[0:TS, NT, :].unsqueeze(2).to_broadcast([TS, 12, TS]),
                              ident[0:TS, 0:TS].unsqueeze(1).to_broadcast([TS, 12, TS]), ALU.mult).then_inc(gate_diag, 1)
            for v in range(2):
                dve.wait_ge(cmpp_mm, v + 1)
                step(dve.tensor_copy(lam[:, 6 + v:7 + v], ps[:, 1 + v, 64:65]))
                z = ps[:, 1 + v, 0:64].rearrange("p (g i) -> p g i", g=GB)[:, :, 0:NB_P]
                dve.tensor_scalar(hidp[:, v, 0:2 * NB_P].rearrange("p (g i) -> p g i", g=GB), z, lam[:, 6 + v:7 + v], None, ALU.add).then_inc(cmpp_exp, 1)
            for v in range(2):
                z = ps[:, 1 + v, 0:64].rearrange("p (g i) -> p g i", g=GB)[:, :, 0:NB_P]
                hv = hidp[:, v, 0:2 * NB_P]
                dve.wait_ge(act_chain, 3 + v)
                step(dve.tensor_scalar(hv, hv, 1.0, None, ALU.add))
                step(dve.reciprocal(hv, hv))
                hg = hv.rearrange("p (g i) -> p g i", g=GB)
                dve.scalar_tensor_tensor(out=hg, in0=z, scalar=lam[:, 6 + v:7 + v], in1=hg, op0=ALU.add, op1=ALU.mult).then_inc(cmpp_hid, 1)
            dve.wait_ge(cmpp2_mm, 1)
            dve.tensor_copy(kccp[:, :, :], ps[:, 3, 0:2 * NB_P].rearrange("p (g i) -> p g i", g=GB)).then_inc(cmpp2_kept, 1)
            dve.tensor_copy(vccp[0:NB_P, :, :], ps[0:NB_P, 3, P:3 * P].rearrange("p (g i) -> p g i", g=GB)).then_inc(cmpp2_kept, 1)
            dve.wait_ge(cs_mm, 1)
            step(dve.tensor_tensor(s1[:, :, :].rearrange("p (h t) i -> p h (t i)", h=HB),
                                   ps[:, 6, 0:16 * NB_P].rearrange("p (h c) -> p h c", h=HB),
                                   const("cmask").unsqueeze(1).to_broadcast([P, HB, NT * NB_P]), ALU.add))
            step(dve.tensor_reduce(r16[:, 0, :], s1[:, :, :], AX.X, ALU.max))
            dve.tensor_tensor(s1[:, :, :], s1[:, :, :], r16[:, 0, :].unsqueeze(2).to_broadcast([P, 16, NB_P]), ALU.subtract).then_inc(cs_sub, 1)
            dve.wait_ge(cs_exp, 1)
            step(dve.tensor_reduce(r16[:, 1, :], s1[:, :, :], AX.X, ALU.add))
            step(dve.reciprocal(r16[:, 1, :], r16[:, 1, :]))
            rr = r16[:, 1, :].rearrange("p (h t) -> p h t", h=HB)
            step(dve.tensor_tensor(rr, rr, gates[:, 0:NT, 0:12:3].rearrange("p t h -> p h t"), ALU.mult))
            step(dve.tensor_tensor(rr, rr, const("cvalid").unsqueeze(1).to_broadcast([P, HB, NT]), ALU.mult))
            dve.tensor_tensor(s1[:, :, :], s1[:, :, :], r16[:, 1, :].unsqueeze(2).to_broadcast([P, 16, NB_P]), ALU.mult).then_inc(cs_p, 1)

            def p_max(v):
                h, t, b = units[v]
                dve.wait_ge(s_mm, v + 1)
                if v >= 4:
                    dve.wait_ge(p_ready, v - 3)
                dve.tensor_reduce(nm[:, v % 4:v % 4 + 1], ps[:, v % 3, 0:(t + 1) * P], AX.X, ALU.max, negate=True).then_inc(nm_ready, 1)

            def p_factor(v):
                h, t, b = units[v]
                dve.wait_ge(p_ready, v + 1)
                step(dve.reciprocal(rsum[:, v % 4:v % 4 + 1], sums[:, v % 4:v % 4 + 1]))
                if v >= 3:
                    dve.wait_ge(pt_mm, group_of[v - 3] + 1)
                if h < HA:
                    f = lam[:, 5:6] if b else ones[:, 0:1]
                else:
                    c = 3 * (h - HA) + 1 + b
                    f = gates[:, t, c:c + 1]
                dve.tensor_scalar(diag[:, v % 3, :], ident[:, :], rsum[:, v % 4:v % 4 + 1], f, ALU.mult, ALU.mult).then_inc(diag_ready, 1)

            def o_keep(h):
                dve.wait_ge(pv_mm, head_groups[h])
                dve.tensor_copy(hT[:, h, 0:SEQ], ps[:, 5 + h % 2, :]).then_inc(o_kept, 1)

            due = {last_unit[h] + 6: h for h in range(HA + HB)}
            for v in range(len(units) + 8):
                if v < len(units):
                    p_max(v)
                if 1 <= v <= len(units):
                    p_factor(v - 1)
                if v in due:
                    o_keep(due[v])

            dve.tensor_copy(qbc[:, :, :].rearrange("p g (n c) -> p g n c", n=NS), qBs[:, :, :, 0:16]).then_inc(qbc_ready, 1)
            dve.wait_ge(ss_mm, 1)
            step(dve.tensor_tensor(sc[:, :, :], ps[:, 7, 0:GB * P].rearrange("p (g c) -> p g c", g=GB)[:, :, 0:NS * NB_S],
                                   const("smask").unsqueeze(1).to_broadcast([P, GB, NS * NB_S]), ALU.add))
            step(dve.tensor_reduce(r16[:, 0, 0:GB], sc[:, :, :], AX.X, ALU.max))
            dve.tensor_tensor(sc[:, :, :], sc[:, :, :], r16[:, 0, 0:GB].unsqueeze(2).to_broadcast([P, GB, NS * NB_S]), ALU.subtract).then_inc(ss_sub, 1)
            dve.wait_ge(ss_exp, 1)
            step(dve.tensor_reduce(r16[:, 1, 0:GB], sc[:, :, :], AX.X, ALU.add))
            step(dve.reciprocal(r16[:, 1, 0:GB], r16[:, 1, 0:GB]))
            dve.tensor_tensor(sc[:, :, :], sc[:, :, :], r16[:, 1, 0:GB].unsqueeze(2).to_broadcast([P, GB, NS * NB_S]), ALU.mult).then_inc(ss_p, 1)
            dve.wait_ge(ss_pv, 1)
            dve.tensor_copy(oc[:, :, :], ps[:, 7, 0:GB * P].rearrange("p (g c) -> p g c", g=GB)).then_inc(oc_kept, 1)

            def s_max(v):
                dve.wait_ge(ss2_mm, v + 1)
                if v >= 4:
                    dve.wait_ge(sp_ready, v - 3)
                dve.tensor_reduce(nm[:, v % 4:v % 4 + 1], ps[:, 3 + v % 2, 0:PAST + TS], AX.X, ALU.max, negate=True).then_inc(snm_ready, 1)

            def s_factor(v):
                dve.wait_ge(sp_ready, v + 1)
                step(dve.reciprocal(rsum[:, v % 4:v % 4 + 1], sums[:, v % 4:v % 4 + 1]))
                if v >= 3:
                    dve.wait_ge(spt_mm, v - 2)
                dve.tensor_scalar(diag[:, v % 3, :], ident[:, :], rsum[:, v % 4:v % 4 + 1], None, ALU.mult).then_inc(sdiag_ready, 1)

            def so_keep(v):
                dve.wait_ge(spv_mm, v + 1)
                dve.tensor_copy((osb if v % 2 else osa)[:, v // 2, :, :],
                                ps[:, 6 + v % 2, 0:P].rearrange("p (s c) -> p s c", s=4)[:, :, 0:16]).then_inc(so_kept, 1)

            for v in range(2 * NS + 3):
                if v < 2 * NS:
                    s_max(v)
                    s_factor(v)
                if v >= 3:
                    so_keep(v - 3)
            dve.wait_ge(so_kept, 2 * NS)
            dve.wait_ge(gb_kept, 1)
            for h in range(HA):
                dve.scalar_tensor_tensor(out=hT[:, h, SEQ:T].rearrange("p (n s) -> p n s", n=NS), in0=osa[:, :, h, DS:2 * DS],
                                         scalar=lam[:, 5:6], in1=osa[:, :, h, 0:DS], op0=ALU.mult, op1=ALU.add)
            for h in range(HB):
                g, r = h // 2, h % 2
                parts = [oc[:, g, :].rearrange("p (n r s) -> p n r s", n=NS, r=2)[:, :, r, :],
                         osb[:, :, g, DS * r:DS * r + DS], osb[:, :, 2 + g, DS * r:DS * r + DS]]
                for b, part in enumerate(parts):
                    ins = dve.tensor_tensor(part, part, gb[:, 3 * h + b, :].rearrange("p (n s) -> p n s", n=NS), ALU.mult)
            step(ins)
            for h in range(HB):
                g, r = h // 2, h % 2
                ins = dve.tensor_tensor(osb[:, :, g, DS * r:DS * r + DS], osb[:, :, g, DS * r:DS * r + DS],
                                        osb[:, :, 2 + g, DS * r:DS * r + DS], ALU.add)
            step(ins)
            for h in range(HB):
                g, r = h // 2, h % 2
                ins = dve.tensor_tensor(hT[:, HA + h, SEQ:T].rearrange("p (n s) -> p n s", n=NS),
                                        oc[:, g, :].rearrange("p (n r s) -> p n r s", n=NS, r=2)[:, :, r, :],
                                        osb[:, :, g, DS * r:DS * r + DS], ALU.add)
            ins.then_inc(comb_ready, 1)
            step(dve.tensor_scalar(lam[:, 4:5], v2T[:, V2_SUB:V2_SUB + 1], 1.0 - LAM_INIT, None, ALU.mult))
            dve.wait_ge(sub_std, 1)
            for h in range(HA):
                step(dve.reciprocal(sq[:, h, :], sq[:, h, :]))
                dve.scalar_tensor_tensor(out=hT[:, h, :], in0=hT[:, h, :], scalar=lam[:, 4:5], in1=sq[:, h, :],
                                         op0=ALU.mult, op1=ALU.mult).then_inc(mix_ready, 1)

            def residual(m, main, side, term):
                g = mod[:, term * KC + m, :]
                dve.scalar_tensor_tensor(out=xT[:, m, 0:SEQ], in0=main, scalar=g[:, 0:1], in1=xT[:, m, 0:SEQ], op0=ALU.mult, op1=ALU.add)
                t8 = xs_tmp[:, :].rearrange("p (n s) -> p n s", n=NS)
                step(dve.tensor_tensor(t8, side.rearrange("p (n s) -> p n s", n=NS), g[:, 1:9].unsqueeze(2).to_broadcast([P, NS, DS]), ALU.mult))
                return dve.tensor_tensor(xT[:, m, SEQ:T], xT[:, m, SEQ:T], xs_tmp[:, :], ALU.add)

            def out_projection(layer):
                for m in range(KC):
                    dve.wait_ge(out_mm, layer * KC + m + 1)
                    if m in (4, 5):
                        w_rest(layer, m - 4)
                    residual(m, ps[:, m % 4, :], ps[:, 4 + m % 4, 0:TS], 2).then_inc(resid_kept, 1)
                    dve.wait_ge(resid_kept, layer * KC + m + 1)

            def w_rest(layer, at, more=0):
                raw, high, low = unit(at)
                dve.wait_ge(w_high, more + (at + 1 + MLP_UNITS * layer))
                dve.tensor_tensor(low, raw, high.bitcast(F32), ALU.subtract).then_inc(w_split, 1)

            def h_rest(layer):
                for k in range(KC):
                    dve.wait_ge(h_high, layer * KC + k + 1)
                    dve.tensor_tensor(hT_r[:, k, :], hT[:, k, :], h_hi[:, k, :].bitcast(F32), ALU.subtract).then_inc(h_split, 1)

            def mlp(layer):
                dve.sem_inc(down_free, 4)

                def quarter(q, ahead):
                    for j in range(8):
                        if j < ahead:
                            w_rest(layer, j + 2, q * 8)
                        for g in (2 * j, 2 * j + 1):
                            pair = 2 * (g % 4)
                            if g < 8:
                                new = hid_new[:, g % 2, :]
                                dve.wait_ge(up_mm, q * QUARTER + (g + 1 + 32 * layer))
                                dve.tensor_scalar(new.rearrange("p (i c) -> p i c", i=2), ps[:, pair:pair + 2, 0:HALF], 0.0, None,
                                                  ALU.max).then_inc(up_free, 1)
                                dve.wait_ge(up_free, q * QUARTER + (g + 1 + 32 * layer))
                                dve.tensor_tensor(new, new, new, ALU.mult).then_inc(hid_high, 1)
                                dve.wait_ge(hid_high, q * 2 * QUARTER + (2 * g + 1 + 64 * layer))
                                dve.tensor_copy(hid_hi[:, g, :], new).then_inc(hid_high, 1)
                                dve.wait_ge(hid_high, q * 2 * QUARTER + (2 * g + 2 + 64 * layer))
                                dve.tensor_tensor(hid_lo[:, g, :], new, hid_hi[:, g, :].bitcast(F32), ALU.subtract).then_inc(hid_ready, 1)
                            else:
                                m = g - 8
                                gate = mod[:, 5 * KC + m, :]
                                cut = SEQ - HALF
                                dve.wait_ge(down_mm, q * QUARTER + (m + 1 + 32 * layer))
                                for bank, cols in ((ps[:, pair, 0:HALF], slice(0, HALF)), (ps[:, pair + 1, 0:cut], slice(HALF, SEQ))):
                                    dve.scalar_tensor_tensor(out=xT[:, m, cols], in0=bank, scalar=gate[:, 0:1], in1=xT[:, m, cols],
                                                             op0=ALU.mult, op1=ALU.add)
                                dve.tensor_tensor(xs_new[:, m % 2, :].rearrange("p (n s) -> p n s", n=NS),
                                                  ps[:, pair + 1, cut:HALF].rearrange("p (n s) -> p n s", n=NS),
                                                  gate[:, 1:9].unsqueeze(2).to_broadcast([P, NS, DS]), ALU.mult).then_inc(down_free, 1)
                                dve.wait_ge(down_free, q * QUARTER + (m + 5 + 36 * layer))
                                dve.tensor_tensor(xT[:, m, SEQ:T], xT[:, m, SEQ:T], xs_new[:, m % 2, :], ALU.add).then_inc(mlp_added, 1)

                with dve.Fori(0, 3) as q:
                    quarter(q, 8)
                quarter(3, 6)
                dve.wait_ge(mlp_added, 32 * (layer + 1))

            out_projection(0)
            mod_scale(3, v1T[:, V1_N2:V1_N2 + KC])
            norm(1)
            modulate(3)
            h_rest(0)
            mlp(0)

            norm(2)
            adaln_begin()
            for i in range(3):
                adaln_round(1, i)
            mod_scale(0, v1T[:, V1_N1 + KC:V1_N1 + 2 * KC])
            modulate(0)
            for h in range(HC):
                dve.wait_ge(gz_mm, h + 1)
                bg = v2T[:, V2_BG + h:V2_BG + h + 1]
                for src, lo, hi in ((ps[:, h, :], 0, SEQ), (ps[:, 4 + h, 0:TS], SEQ, T)):
                    dve.tensor_scalar(gtmp[:, h, lo:hi], src, bg, None, ALU.add)
                    dve.tensor_scalar(gbt[:, h, lo:hi], src, bg, 0.0, ALU.add, ALU.min).then_inc(gz_abs, 1)
            dve.wait_ge(gz_abs, 2 * HC)
            dve.wait_ge(gz_ln, 1)
            step(dve.tensor_tensor(gtmp[:, :, :], gbt[:, :, :], gtmp[:, :, :], ALU.subtract))
            for h in range(HC):
                dve.tensor_tensor_scan(gbt[:, h, :], const("keep"), gtmp[:, h, :], 0.0, ALU.mult, ALU.add).then_inc(b_ready, 1)
            dve.wait_ge(b_ready, HC)
            for c in range(KC):
                dve.wait_ge(r_exp, c + 1)
                step(dve.tensor_scalar(er[:, c % 2, :], er[:, c % 2, :], 1.0, None, ALU.add))
                step(dve.reciprocal(er[:, c % 2, :], er[:, c % 2, :]))
                dve.scalar_tensor_tensor(out=gr[:, c, :], in0=gr[:, c, :], scalar=v2T[:, V2_GLAN + c % 2:V2_GLAN + c % 2 + 1],
                                         in1=er[:, c % 2, :], op0=ALU.mult, op1=ALU.mult).then_inc(r_ready, 1)
            dve.wait_ge(r_ready, KC)
            step(dve.memset(gatt[:, :, :, :], 0.0))

            def g_prepare(h):
                b, q, k = gbt[:, h, :], gq[:, h, :], gk[:, h, :]
                bp = b[:, 0:SEQ].rearrange("p (c t) -> p c t", c=NCH)
                qp = q[:, 0:SEQ].rearrange("p (c t) -> p c t", c=NCH)
                kk = k[:, 0:SEQ].rearrange("p (c t) -> p c t", c=NCH)
                bs = b[:, SEQ:T].rearrange("p (n t) -> p n t", n=NS)
                if h == 0:
                    dve.wait_ge(gin_kept, gin_upto[3])
                else:
                    dve.wait_ge(att_mm, h)
                    dve.wait_ge(kd_turned, h)
                for i in range(1, 4):
                    start = bp[:, :, i * SUB - 1:i * SUB]
                    n = (i + 1) * SUB
                    dve.tensor_tensor(gqd[:, :, (i - 1) * SUB:i * SUB], bp[:, :, i * SUB:n], start.to_broadcast([P, NCH, SUB]), ALU.subtract)
                    dve.tensor_tensor(gkp[i], start.to_broadcast([P, NCH, n]), bp[:, :, 0:n], ALU.subtract)
                dve.tensor_tensor(gkd[:, 0:SEQ].rearrange("p (c t) -> p c t", c=NCH), bp[:, :, GCH - 1:GCH].to_broadcast([P, NCH, GCH]), bp, ALU.subtract)
                dve.tensor_tensor(gkd[:, SEQ:T].rearrange("p (n t) -> p n t", n=NS), bs[:, :, DS - 1:DS].to_broadcast([P, NS, DS]), bs, ALU.subtract
                                  ).then_inc(gsub_ready, 1)
                dve.wait_ge(eb_ready, 2 * h + 2)
                if h >= 2:
                    dve.wait_ge(os_mm, h - 1)
                    dve.wait_ge(st_kept, 8 * (h - 1))
                dve.tensor_tensor(gqe[:, h % 2, :], q, geb, ALU.mult)
                dve.tensor_copy(gebl[:, h % 2, 0:NCH], geb[:, GCH - 1:SEQ:GCH])
                dve.tensor_copy(gebl[:, h % 2, NCH:NCH + NS], geb[:, SEQ + DS - 1:T:DS])
                dve.tensor_tensor(gkp[0], gkp[0], kk[:, :, 0:SUB], ALU.mult)
                dve.tensor_tensor(gkp_s, gkp_s, k[:, SEQ:T], ALU.mult)
                dve.wait_ge(ex_ready, h + 1)
                dve.tensor_tensor(gqd, gqd, qp[:, :, SUB:GCH], ALU.mult)
                for i in range(1, 4):
                    dve.tensor_tensor(gkp[i], gkp[i], kk[:, :, 0:(i + 1) * SUB], ALU.mult)
                dve.tensor_tensor(gkd, gkd, k, ALU.mult).then_inc(prep_ready, 1)
                dve.wait_ge(prep_ready, h + 1)

            def g_scores(h):
                dve.wait_ge(att_mm, h + 1)
                if h >= 2:
                    dve.wait_ge(os_mm, h - 1)
                step(dve.tensor_copy(gkdT[0:TS, h % 2, NT, :], ps[0:TS, 0, 384:512]))
                tri = const("tri")
                for i in range(4):
                    m = (i + 1) * SUB
                    cols = slice(i * SUB, m)
                    for lo in ((0, 64) if i < 3 else (0,)):
                        r = slice(lo, lo + m) if i < 3 else slice(0, P)
                        n = m if i < 3 else P
                        dve.tensor_tensor(gatt[r, h % 2, 0:4, cols], ps[r, 0, 0:4 * GCH].rearrange("p (t c) -> p t c", t=4)[:, :, cols],
                                          tri[r, cols].unsqueeze(1).to_broadcast([n, 4, SUB]), ALU.mult)
                dve.tensor_tensor(gatt[0:TS, h % 2, 4, :], ps[0:TS, 0, 4 * GCH:5 * GCH], const("stri")[0:TS, :], ALU.mult
                                  ).then_inc(att_kept, 1)

            def g_sample_keys(h):
                if h:
                    dve.wait_ge(st_mm, 8 * h)
                dve.tensor_tensor(gkdm[0:TS, :, :], gkdT[0:TS, h % 2, NT, :].unsqueeze(1).to_broadcast([TS, NS, P]),
                                  const("rowof")[0:TS, :].unsqueeze(2).to_broadcast([TS, NS, P]), ALU.mult).then_inc(gkdm_ready, 1)

            def g_chain(h):
                for p in range(4):
                    dve.wait_ge(st_mm, 8 * h + p + 1)
                    for w in range(2):
                        c = 2 * p + w
                        kv = ps[:, 5 + (8 * h + p) % 3, w * DVC:(w + 1) * DVC]
                        if NCH * h + c + 1 >= 4:
                            last = NCH * h + c + 1 - 4
                            dve.wait_ge(go_mm, last + 1)
                        if c + 1 == 4 and h:
                            dve.wait_ge(gs_stored, 16 * h)
                        if c == 0:
                            ins = dve.tensor_copy(sp_[:, 1, :], kv)
                        else:
                            ins = dve.scalar_tensor_tensor(out=sp_[:, (c + 1) % 4, :], in0=sp_[:, c % 4, :], scalar=gebl[:, h % 2, c:c + 1],
                                                           in1=kv, op0=ALU.mult, op1=ALU.add)
                        ins.then_inc(s_ready, 1)
                        dve.wait_ge(s_ready, NCH * h + c + 1)
                    dve.sem_inc(st_kept, 1)

            def g_sample_states(h):
                dve.wait_ge(os_mm, h + 1)
                for p in range(4, 8):
                    dve.wait_ge(st_mm, 8 * h + p + 1)
                    for w in range(2):
                        n = 2 * (p - 4) + w
                        ins = dve.scalar_tensor_tensor(out=s0[:, h % 2, n, :], in0=s0[:, h % 2, n, :], scalar=gebl[:, h % 2, NCH + n:NCH + n + 1],
                                                       in1=ps[:, 5 + (8 * h + p) % 3, w * DVC:(w + 1) * DVC], op0=ALU.mult, op1=ALU.add)
                    ins.then_inc(st_kept, 1)

            g_prepare(0)
            g_scores(0)
            g_sample_keys(0)
            g_prepare(1)
            for h in range(HC):
                g_chain(h)
                if h + 1 < HC:
                    g_scores(h + 1)
                g_sample_states(h)
                if h + 1 < HC:
                    g_sample_keys(h + 1)
                if h + 2 < HC:
                    g_prepare(h + 2)
            for k in range(KC):
                dve.wait_ge(gn_sq, k + 1)
                dve.tensor_tensor(hT[:, k, :], hT[:, k, :], gr[:, k, :], ALU.mult)
            dve.wait_ge(gn_std, 1)
            for h in range(HC):
                step(dve.reciprocal(gstd[:, h, :], gstd[:, h, :]))
                for k in (2 * h, 2 * h + 1):
                    dve.tensor_tensor(hT[:, k, :], hT[:, k, :], gstd[:, h, :], ALU.mult).then_inc(gmix_ready, 1)
            out_projection(1)
            mod_scale(3, v1T[:, V1_N2 + KC:V1_N2 + 2 * KC])
            norm(3)
            modulate(3)
            h_rest(1)
            mlp(1)
            dve.wait_ge(norm_std, 5)
            step(dve.reciprocal(rstd[:, :], rstd[:, :]))
            for k in range(KC):
                dve.scalar_tensor_tensor(out=hT[:, k, :], in0=xT[:, k, :], scalar=v2T[:, V2_FIN + k:V2_FIN + k + 1], in1=rstd[:, :],
                                         op0=ALU.mult, op1=ALU.mult).then_inc(norm_x, 1)


_INS = ["x_prompt", "x_sample", "c_prompt", "c_sample", "cache_diff_k", "cache_diff_v", "cache_cmp_kv", "cache_sel_kv",
        "state_win_kv", "state_gla", "page_table", "norm1_w", "norm2_w", "ada_w", "ada_b", "even_w_in", "even_w_out",
        "diff_lambda_w", "diff_subln_w", "cmp_pe", "cmp_w1", "cmp_w2", "gla_w_in", "gla_w_gate", "gla_b_gate",
        "gla_norm_w", "gla_w_out", "mlp_w1", "mlp_w2", "final_norm_w"]
_OUTS = [(1, SEQ, D), (NS, DS, D), (1, 1, SEQ, HA, 2, DKA), (1, 1, SEQ, HA, 2 * DKA), (1, 1, SEQ, 2, GB, DHB),
         (1, 1, SEQ, 2, GB, DHB), (1, 1, SEQ, 2, GB, DHB), (1, 1, HC, DKC, DVC), (1, NS, DS, HA, 2, DKA),
         (1, NS, DS, HA, 2 * DKA), (1, NS, DS, 2, GB, DHB), (1, NS, DS, 2, GB, DHB), (1, NS, PAST, 2, GB, DHB),
         (1, NS, HC, DKC, DVC)]


def kernel(**inputs):
    import concourse.bacc as _bacc
    from concourse.bass_utils import run_bass_kernel_spmd as _run

    nc = _bacc.Bacc("TRN2", target_bir_lowering=False, num_devices=1)
    arrays, aps = {}, {}
    const_f32, const_bf16, const_cols = shape_constants()
    given = {name: np.ascontiguousarray(inputs[name]) for name in _INS}
    given["const_f32"], given["const_bf16"] = const_f32, const_bf16
    for name, v in given.items():
        arrays[f"in_{name}"] = v
        aps[name] = nc.dram_tensor(f"in_{name}", v.shape, mybir.dt.from_np(v.dtype), kind="ExternalInput").ap()
    outs = [nc.dram_tensor(f"out_{i}", s, F32, kind="ExternalOutput").ap() for i, s in enumerate(_OUTS)]
    decoder_program(nc, aps, outs, const_cols)
    r = _run(nc, [arrays], core_ids=[0])
    return tuple(r.results[0][f"out_{i}"] for i in range(len(_OUTS)))
```
